# Optimizing a Trainium2 kernel written in Bass

```python
import jax, jax.numpy as jnp
from jax import lax
import numpy as np

D_MODEL = 1024
BATCH = 1
SEQ = 128
DEPTH = 2
DEC_BATCH = 1
DEC_SEQ = 128
PAST_LEN = 128

GRID_W = 64
EPS = 1e-6
ROPE_BASE = 10000.0
BLOCK = 128
NEG_INF = -1e30

MLA_HEADS = 4
MLA_NOPE = 64
MLA_ROPE = 32
MLA_V = 64
MLA_Q_LORA = 256
MLA_KV_LORA = 128
HG_HEADS = 4
HG_DK = 64
HG_DV = 64
HG_CHUNK = 32
FN_GROUPS = 4
FN_WIDTH = 256
SWA_HEADS = 4
SWA_KV_HEADS = 2
SWA_HD = 64
WINDOW = 128
N_EXPERTS = 64
TOP_K = 6
D_EXPERT = 256
D_SHARED = 256
ROUTE_SCALE = 2.5

MLA_IN = MLA_Q_LORA + MLA_KV_LORA + MLA_ROPE
HG_IN = 3 * HG_HEADS * HG_DK + 2 * HG_HEADS * HG_DV
FN_IN = FN_WIDTH
SWA_IN = (SWA_HEADS + 2 * SWA_KV_HEADS) * SWA_HD
IN_COLS = MLA_IN + HG_IN + FN_IN + SWA_IN
IN_SPLITS = (MLA_IN, MLA_IN + HG_IN, MLA_IN + HG_IN + FN_IN)
MIX_W = MLA_HEADS * MLA_V + HG_HEADS * HG_DV + FN_WIDTH + SWA_HEADS * SWA_HD

kernel_name = 'hybrid_prefix_diffusion_step'

def rmsnorm(x, g):
    xf = x.astype(jnp.float32)
    y = xf * lax.rsqrt(jnp.mean(xf * xf, axis=-1, keepdims=True) + EPS)
    return (y * g.astype(jnp.float32)).astype(x.dtype)

def rope_tables(pos, dim):
    nf = dim // 4
    inv = ROPE_BASE ** (-jnp.arange(nf, dtype=jnp.float32) / nf)
    ang = pos.astype(jnp.float32)[:, :, None] * inv
    return jnp.cos(ang), jnp.sin(ang)

def apply_rope(x, tables):
    cos, sin = tables
    B, T, H, dim = x.shape
    xr = x.astype(jnp.float32).reshape(B, T, H, 2, dim // 4, 2)
    a, b = xr[..., 0], xr[..., 1]
    c, s = cos[None, :, None], sin[None, :, None]
    out = jnp.stack([a * c - b * s, a * s + b * c], axis=-1)
    return out.reshape(B, T, H, dim).astype(x.dtype)

def sink_softmax(s, sink):
    sk = jnp.broadcast_to(sink.astype(jnp.float32)[..., None, None], s.shape[:-1] + (1,))
    return jax.nn.softmax(jnp.concatenate([s, sk], axis=-1), axis=-1)[..., :-1]

def dense_attention(q, k, v, scale, sink=None):
    B, Tq, KVH, G, dq = q.shape
    nb = Tq // BLOCK
    qb = jnp.moveaxis(q.reshape(B, nb, BLOCK, KVH, G, dq), 1, 0)

    def one_block(qi):
        s = jnp.einsum('bqhgd,bkhd->bhgqk', qi, k).astype(jnp.float32) * scale
        p = jax.nn.softmax(s, axis=-1) if sink is None else sink_softmax(s, sink)
        return jnp.einsum('bhgqk,bkhe->bqhge', p.astype(v.dtype), v)

    o = lax.map(one_block, qb)
    return jnp.moveaxis(o, 0, 1).reshape(B, Tq, KVH, G, -1)

def window_ctx_attention(q, k, v, kc, vc, sink, scale):
    B, T, KVH, G, d = q.shape
    nb = T // BLOCK
    qb = q.reshape(B, nb, BLOCK, KVH, G, d)
    padw = ((0, 0), (BLOCK, BLOCK), (0, 0), (0, 0))
    kp, vp = jnp.pad(k, padw), jnp.pad(v, padw)
    idx = jnp.arange(nb)[:, None] * BLOCK + jnp.arange(3 * BLOCK)[None, :]
    kb, vb = kp[:, idx], vp[:, idx]
    qpos = jnp.arange(nb)[:, None] * BLOCK + jnp.arange(BLOCK)[None, :]
    kpos = idx - BLOCK
    valid = ((jnp.abs(qpos[:, :, None] - kpos[:, None, :]) <= WINDOW)
             & (kpos[:, None, :] >= 0) & (kpos[:, None, :] < T))
    s_loc = jnp.einsum('bnqhgd,bnkhd->bnhgqk', qb, kb).astype(jnp.float32) * scale
    s_loc = jnp.where(valid[None, :, None, None], s_loc, NEG_INF)
    s_ctx = jnp.einsum('bnqhgd,bchd->bnhgqc', qb, kc).astype(jnp.float32) * scale
    p = sink_softmax(jnp.concatenate([s_loc, s_ctx], axis=-1), sink)
    p_loc, p_ctx = p[..., :3 * BLOCK].astype(v.dtype), p[..., 3 * BLOCK:].astype(v.dtype)
    o = (jnp.einsum('bnhgqk,bnkhe->bnqhge', p_loc, vb)
         + jnp.einsum('bnhgqc,bche->bnqhge', p_ctx, vc))
    return o.reshape(B, T, KVH, G, d)

def hgrn2_chunk_scan(q, k, v, logf, s0):
    B, T, H, DK = q.shape
    C = HG_CHUNK
    n = T // C
    r = lambda a: a.reshape(B, n, C, H, a.shape[-1]).transpose(1, 0, 3, 2, 4)
    qc, kc, vc = r(q), r(k), r(v)
    G = jnp.cumsum(r(logf).astype(jnp.float32), axis=-2)
    mask = jnp.tril(jnp.ones((C, C), dtype=bool))
    diff = G[..., :, None, :] - G[..., None, :, :]
    decay = jnp.exp(jnp.where(mask[:, :, None], diff, -jnp.inf))
    A = jnp.einsum('nbhtsd,nbhsd->nbhts', qc[..., :, None, :] * decay, kc)
    o_intra = jnp.einsum('nbhts,nbhse->nbhte', A, vc)
    q_dec = qc * jnp.exp(G)
    k_dec = kc * jnp.exp(G[..., -1:, :] - G)
    chunk_decay = jnp.exp(G[..., -1, :])

    def step(S, inp):
        qd, kd, vv, cd = inp
        o_inter = jnp.einsum('bhtd,bhde->bhte', qd, S)
        S_new = cd[..., None] * S + jnp.einsum('bhsd,bhse->bhde', kd, vv)
        return S_new, o_inter

    S_fin, o_inter = lax.scan(step, s0.astype(jnp.float32), (q_dec, k_dec, vc, chunk_decay))
    o = o_intra + o_inter
    return o.transpose(1, 0, 3, 2, 4).reshape(B, T, H, -1), S_fin

def mla_mixer(u, q_norm_g, w_q_up, kv_norm_g, w_kv_up, rope, cache):
    B, T, _ = u.shape
    c_q, c_kv, k_rope = jnp.split(u, [MLA_Q_LORA, MLA_Q_LORA + MLA_KV_LORA], axis=-1)
    q = jnp.einsum('btr,rk->btk', rmsnorm(c_q, q_norm_g), w_q_up).reshape(B, T, MLA_HEADS, MLA_NOPE + MLA_ROPE)
    q_nope, q_rope = q[..., :MLA_NOPE], q[..., MLA_NOPE:]
    c_kv = rmsnorm(c_kv, kv_norm_g)
    k_rope = k_rope[:, :, None, :]
    if cache is None:
        ckv_all, kr_all = c_kv, k_rope
        new = (c_kv, k_rope[:, :, 0])
    else:
        q_rope, k_rope = apply_rope(q_rope, rope), apply_rope(k_rope, rope)
        ckv_ctx, kr_ctx = cache
        ckv_all = jnp.concatenate([ckv_ctx.astype(c_kv.dtype), c_kv], axis=1)
        kr_all = jnp.concatenate([kr_ctx[:, :, None].astype(k_rope.dtype), k_rope], axis=1)
        new = ()
    Tk = ckv_all.shape[1]
    kv = jnp.einsum('btr,rk->btk', ckv_all, w_kv_up).reshape(B, Tk, MLA_HEADS, MLA_NOPE + MLA_V)
    k_nope, v = kv[..., :MLA_NOPE], kv[..., MLA_NOPE:]
    k = jnp.concatenate([k_nope, jnp.broadcast_to(kr_all, (B, Tk, MLA_HEADS, MLA_ROPE))], axis=-1)
    qf = jnp.concatenate([q_nope, q_rope], axis=-1)[:, :, :, None, :]
    o = dense_attention(qf, k, v, (MLA_NOPE + MLA_ROPE) ** -0.5)
    return o.reshape(B, T, MLA_HEADS * MLA_V), new

def hgrn_mixer(u, lb_f, lb_b, norm_g, state):
    B, T, _ = u.shape
    HK, HV = HG_HEADS * HG_DK, HG_HEADS * HG_DV
    q, zf, zb, i, g = jnp.split(u, [HK, 2 * HK, 3 * HK, 3 * HK + HV], axis=-1)
    q = jax.nn.silu(q).reshape(B, T, HG_HEADS, HG_DK)
    i = i.reshape(B, T, HG_HEADS, HG_DV)

    def gates(z, lb):
        f = lb + (1.0 - lb) * jax.nn.sigmoid(z.astype(jnp.float32))
        return (1.0 - f).reshape(B, T, HG_HEADS, HG_DK), jnp.log(f).reshape(B, T, HG_HEADS, HG_DK)

    kf, gf = gates(zf, lb_f)
    kb, gb = gates(zb, lb_b)
    if state is None:
        s0 = jnp.zeros((B, 2, HG_HEADS, HG_DK, HG_DV), jnp.float32)
    else:
        s0 = state.astype(jnp.float32)
    flip = lambda a: jnp.flip(a, axis=1)
    o_f, s_f = hgrn2_chunk_scan(q, kf, i, gf, s0[:, 0])
    o_b, s_b = hgrn2_chunk_scan(flip(q), flip(kb), flip(i), flip(gb), s0[:, 1])
    o = rmsnorm(o_f + flip(o_b), norm_g).reshape(B, T, HV) * jax.nn.silu(g)
    new = (jnp.stack([s_f, s_b], axis=1).astype(u.dtype),) if state is None else ()
    return o.astype(u.dtype), new

def fourier_mixer(u, w):
    B, T, _ = u.shape
    ug = u.astype(jnp.float32).reshape(B, T, FN_GROUPS, FN_WIDTH // FN_GROUPS)
    y = jnp.fft.fft2(ug, axes=(1, 3), norm='ortho').real
    return jnp.einsum('btk,kj->btj', y.reshape(B, T, FN_WIDTH).astype(u.dtype), w)

def swa_mixer(u, sink, rope, cache):
    B, T, _ = u.shape
    G = SWA_HEADS // SWA_KV_HEADS
    q, k, v = jnp.split(u, [SWA_HEADS * SWA_HD, (SWA_HEADS + SWA_KV_HEADS) * SWA_HD], axis=-1)
    q = q.reshape(B, T, SWA_HEADS, SWA_HD)
    k = k.reshape(B, T, SWA_KV_HEADS, SWA_HD)
    v = v.reshape(B, T, SWA_KV_HEADS, SWA_HD)
    sink = sink.reshape(SWA_KV_HEADS, G)
    scale = SWA_HD ** -0.5
    if cache is None:
        o = dense_attention(q.reshape(B, T, SWA_KV_HEADS, G, SWA_HD), k, v, scale, sink)
        new = (k, v)
    else:
        q, k = apply_rope(q, rope), apply_rope(k, rope)
        kc, vc = cache
        o = window_ctx_attention(q.reshape(B, T, SWA_KV_HEADS, G, SWA_HD), k, v,
                                 kc.astype(k.dtype), vc.astype(v.dtype), sink, scale)
        new = ()
    return o.reshape(B, T, SWA_HEADS * SWA_HD), new

def moe_ffn(h, w_router, b_router, w_gate, w_up, w_down, ws_gate, ws_up, ws_down):
    scores = jax.nn.sigmoid(jnp.einsum('btd,de->bte', h, w_router).astype(jnp.float32))
    _, idx = lax.top_k(scores + b_router.astype(jnp.float32), TOP_K)
    sel = jnp.take_along_axis(scores, idx, axis=-1)
    wts = ROUTE_SCALE * sel / jnp.sum(sel, axis=-1, keepdims=True)
    gate = jnp.sum(jax.nn.one_hot(idx, N_EXPERTS, dtype=jnp.float32) * wts[..., None], axis=-2).astype(h.dtype)
    hid = (jax.nn.silu(jnp.einsum('btd,edf->btef', h, w_gate))
           * jnp.einsum('btd,edf->btef', h, w_up) * gate[..., None])
    routed = jnp.einsum('btef,efd->btd', hid, w_down)
    shared = jnp.einsum('btf,fd->btd', jax.nn.silu(h @ ws_gate) * (h @ ws_up), ws_down)
    return routed + shared

def trunk_layer(x, cvec, P, l, lb, ropes, cache):
    m = (jnp.einsum('bd,dk->bk', jax.nn.silu(cvec), P['w_ada'][l]) + P['b_ada'][l])[:, None, :]
    sh1, sc1, g1, sh2, sc2, g2 = jnp.split(m, 6, axis=-1)
    h = rmsnorm(x, P['norm1_g'][l]) * (1 + sc1) + sh1
    u = jnp.einsum('btd,dk->btk', h, P['w_in'][l])
    u_mla, u_hg, u_fn, u_swa = jnp.split(u, IN_SPLITS, axis=-1)
    o_mla, n_mla = mla_mixer(u_mla, P['mla_q_norm_g'][l], P['mla_w_q_up'][l], P['mla_kv_norm_g'][l],
                             P['mla_w_kv_up'][l], ropes[0], None if cache is None else cache[0:2])
    o_hg, n_hg = hgrn_mixer(u_hg, lb[0, l], lb[1, l], P['hg_norm_g'][l], None if cache is None else cache[4])
    o_fn = fourier_mixer(u_fn, P['fn_w'][l])
    o_swa, n_swa = swa_mixer(u_swa, P['swa_sink'][l], ropes[1], None if cache is None else cache[2:4])
    mix = jnp.einsum('btk,kd->btd', jnp.concatenate([o_mla, o_hg, o_fn, o_swa], axis=-1), P['w_out'][l])
    x = x + g1 * mix
    h = rmsnorm(x, P['norm2_g'][l]) * (1 + sc2) + sh2
    x = x + g2 * moe_ffn(h, P['moe_w_router'][l], P['moe_b_router'][l], P['moe_w_gate'][l], P['moe_w_up'][l],
                         P['moe_w_down'][l], P['sh_w_gate'][l], P['sh_w_up'][l], P['sh_w_down'][l])
    return x, n_mla + n_swa + n_hg

def setup_inputs(seed: int = 0) -> dict:
    key = jax.random.key(seed)
    ks = list(jax.random.split(key, 40))
    cnt = [0]

    def nk():
        cnt[0] += 1
        return ks[cnt[0] - 1]

    def nrm(shape, scale=1.0):
        return scale * jax.random.normal(nk(), shape, jnp.float32)

    def gain(shape):
        return 1.0 + 0.05 * jax.random.normal(nk(), shape, jnp.float32)

    D = D_MODEL
    return {
        'x_prompt': nrm((BATCH, SEQ, D)),
        'x_sample': nrm((DEC_BATCH, DEC_SEQ, D)),
        'c': nrm((DEC_BATCH, D)),
        'cache_mla_ckv': nrm((DEC_BATCH, DEPTH, PAST_LEN, MLA_KV_LORA)),
        'cache_mla_krope': nrm((DEC_BATCH, DEPTH, PAST_LEN, MLA_ROPE)),
        'cache_swa_k': nrm((DEC_BATCH, DEPTH, PAST_LEN, SWA_KV_HEADS, SWA_HD)),
        'cache_swa_v': nrm((DEC_BATCH, DEPTH, PAST_LEN, SWA_KV_HEADS, SWA_HD)),
        'state_hgrn': nrm((DEC_BATCH, DEPTH, 2, HG_HEADS, HG_DK, HG_DV), 0.5),
        'c_ctx': nrm((D,)),
        'w_ada': nrm((DEPTH, D, 6 * D), 0.5 * D ** -0.5),
        'b_ada': nrm((DEPTH, 6 * D), 0.02),
        'norm1_g': gain((DEPTH, D)),
        'norm2_g': gain((DEPTH, D)),
        'w_in': nrm((DEPTH, D, IN_COLS), D ** -0.5),
        'mla_q_norm_g': gain((DEPTH, MLA_Q_LORA)),
        'mla_w_q_up': nrm((DEPTH, MLA_Q_LORA, MLA_HEADS * (MLA_NOPE + MLA_ROPE)), MLA_Q_LORA ** -0.5),
        'mla_kv_norm_g': gain((DEPTH, MLA_KV_LORA)),
        'mla_w_kv_up': nrm((DEPTH, MLA_KV_LORA, MLA_HEADS * (MLA_NOPE + MLA_V)), MLA_KV_LORA ** -0.5),
        'hg_lb_logits': nrm((2, DEPTH, HG_HEADS * HG_DK), 0.5),
        'hg_norm_g': gain((DEPTH, HG_DV)),
        'fn_w': nrm((DEPTH, FN_WIDTH, FN_WIDTH), FN_WIDTH ** -0.5),
        'swa_sink': nrm((DEPTH, SWA_HEADS), 0.5),
        'w_out': nrm((DEPTH, MIX_W, D), MIX_W ** -0.5),
        'moe_w_router': nrm((DEPTH, D, N_EXPERTS), D ** -0.5),
        'moe_b_router': nrm((DEPTH, N_EXPERTS), 0.01),
        'moe_w_gate': nrm((DEPTH, N_EXPERTS, D, D_EXPERT), D ** -0.5),
        'moe_w_up': nrm((DEPTH, N_EXPERTS, D, D_EXPERT), D ** -0.5),
        'moe_w_down': nrm((DEPTH, N_EXPERTS, D_EXPERT, D), D_EXPERT ** -0.5),
        'sh_w_gate': nrm((DEPTH, D, D_SHARED), D ** -0.5),
        'sh_w_up': nrm((DEPTH, D, D_SHARED), D ** -0.5),
        'sh_w_down': nrm((DEPTH, D_SHARED, D), D_SHARED ** -0.5),
        'final_norm_g': gain((D,)),
    }

def reference(x_prompt, x_sample, c, cache_mla_ckv, cache_mla_krope, cache_swa_k, cache_swa_v, state_hgrn,
              c_ctx, w_ada, b_ada, norm1_g, norm2_g, w_in, mla_q_norm_g, mla_w_q_up, mla_kv_norm_g, mla_w_kv_up,
              hg_lb_logits, hg_norm_g, fn_w, swa_sink, w_out, moe_w_router, moe_b_router, moe_w_gate, moe_w_up,
              moe_w_down, sh_w_gate, sh_w_up, sh_w_down, final_norm_g):
    P = {'w_ada': w_ada, 'b_ada': b_ada, 'norm1_g': norm1_g, 'norm2_g': norm2_g, 'w_in': w_in,
         'mla_q_norm_g': mla_q_norm_g, 'mla_w_q_up': mla_w_q_up, 'mla_kv_norm_g': mla_kv_norm_g,
         'mla_w_kv_up': mla_w_kv_up, 'hg_norm_g': hg_norm_g, 'fn_w': fn_w, 'swa_sink': swa_sink, 'w_out': w_out,
         'moe_w_router': moe_w_router, 'moe_b_router': moe_b_router, 'moe_w_gate': moe_w_gate,
         'moe_w_up': moe_w_up, 'moe_w_down': moe_w_down, 'sh_w_gate': sh_w_gate, 'sh_w_up': sh_w_up,
         'sh_w_down': sh_w_down}
    lb = jnp.cumsum(jax.nn.softmax(hg_lb_logits.astype(jnp.float32), axis=1), axis=1)
    lb = lb - lb[:, :1]

    xp = x_prompt
    cc = c_ctx[None, :]
    per_layer = []
    for l in range(DEPTH):
        xp, new = trunk_layer(xp, cc, P, l, lb, (None, None), None)
        per_layer.append(new)
    y_prompt = rmsnorm(xp, final_norm_g)

    rows = x_sample.shape[1] // GRID_W
    r_idx, c_idx = jnp.meshgrid(jnp.arange(rows), jnp.arange(GRID_W), indexing='ij')
    lat_pos = jnp.stack([r_idx.reshape(-1), c_idx.reshape(-1)], axis=-1)
    ropes = (rope_tables(lat_pos, MLA_ROPE), rope_tables(lat_pos, SWA_HD))
    xs = x_sample
    for l in range(DEPTH):
        cache_l = (cache_mla_ckv[:, l], cache_mla_krope[:, l], cache_swa_k[:, l], cache_swa_v[:, l], state_hgrn[:, l])
        xs, _ = trunk_layer(xs, c, P, l, lb, ropes, cache_l)
    y_sample = rmsnorm(xs, final_norm_g)

    new_mla_ckv = jnp.stack([n[0] for n in per_layer], axis=1)
    new_mla_krope = jnp.stack([n[1] for n in per_layer], axis=1)
    new_swa_k = jnp.stack([n[2] for n in per_layer], axis=1)
    new_swa_v = jnp.stack([n[3] for n in per_layer], axis=1)
    new_state_hgrn = jnp.stack([n[4] for n in per_layer], axis=1)
    return (y_prompt, y_sample, new_mla_ckv, new_mla_krope, new_swa_k, new_swa_v, new_state_hgrn)


_drawn_inputs = setup_inputs


def setup_inputs(seed=0):
    import zlib

    import numpy as np

    out = dict(_drawn_inputs(seed))
    spreads = {}
    factors = {'state_hgrn': 4.766, 'mla_q_norm_g': 3.909, 'swa_sink': 64.0}
    for name, (base, spread) in spreads.items():
        noise = np.random.default_rng([zlib.crc32(name.encode()), seed]).standard_normal(out[name].shape)
        drawn = base * np.exp(spread * noise) if base else spread * noise
        out[name] = __import__('jax').numpy.asarray(drawn.astype(out[name].dtype))
    for name, factor in factors.items():
        out[name] = (out[name] * factor).astype(out[name].dtype)
    return out
```

```python
from contextlib import ExitStack

import numpy as np
import concourse.bass as bass
from concourse import mybir

F32 = mybir.dt.float32
I32 = mybir.dt.int32
ALU = mybir.AluOpType
ACT = mybir.ActivationFunctionType
AX_X = mybir.AxisListType.X

P = 128
D = 1024
KB = D // P
DEPTH = 2
T = 128
NG = 2
TT = NG * T
EPS = 1e-6
GRID_W = 64
ROPE_BASE = 10000.0

MH, NOPE, ROPE, MV, QL, KVL = 4, 64, 32, 64, 256, 128
HH, HD = 4, 64
HP = HH // 2
SH, SKV, SD = 4, 2, 64
FNW, FNG = 256, 4
NE, TOPK, DE = 64, 6, 256
ROUTE_SCALE = 2.5
CK = 32
NCK = T // CK
MLA_SCALE = float(NOPE + ROPE) ** -0.5
SWA_SCALE = float(SD) ** -0.5

C_Q, C_KV = 0, QL
C_HQ = QL + KVL + ROPE
C_ZF, C_ZB, C_I, C_G = (C_HQ + n * 256 for n in range(1, 5))
C_FN = C_G + 256
C_SQ = C_FN + FNW
C_SK = C_SQ + SH * SD
IN_COLS = C_SK + 2 * SKV * SD
IN_UNITS = [(C_Q, 256), (C_KV, KVL + ROPE), (C_HQ, 256), (C_ZF, 256), (C_ZB, 256), (C_I, 256),
            (C_G, 256), (C_FN, 256), (C_SQ, 256), (C_SK, 256)]

UNIT = 2048
RING = 6
CLASSES = 3
N_ADA = 6 * D // 256
N_IN = len(IN_UNITS)
N_OUT = D // 256
N_SHARED = 3
N_PRE = N_ADA + N_IN + N_OUT + N_SHARED
EB = RING // 3
E_ITERS = NE // EB
N_USED = N_PRE + 3 * NE
N_LAYER = -(-N_USED // RING) * RING
U_IN, U_OUT, U_SH, U_EX = N_ADA, N_ADA + N_IN, N_ADA + N_IN + N_OUT, N_PRE

R_BADA, R_N1, R_N2, R_QN, R_KVN, R_HGN = 0, 48, 56, 64, 66, 67
VROWS = 68
R_COND, R_LB, R_FG = 0, 16, 24
GROWS = 32

LOADS = 21
STORES = 8
ACT_LINKS = 4
DVE_LINKS = 50

CONSTS = {}


def constant_array():
    parts = []
    at = 0

    def add(name, a):
        nonlocal at
        full = np.zeros((P, a.shape[1]), np.float32)
        full[:a.shape[0]] = a
        CONSTS[name] = (at, a.shape[1])
        at += a.shape[1]
        parts.append(full)

    n = np.arange(P)
    add("ident", np.eye(P))
    add("flip", np.eye(P)[::-1])
    ang = 2 * np.pi * np.outer(n, n) / T
    add("dft", np.concatenate([np.cos(ang), np.sin(ang)], axis=1))
    w = FNW // FNG
    ang = 2 * np.pi * np.outer(np.arange(w), np.arange(w)) / w
    s = 1.0 / np.sqrt(T * w)
    add("fcos", np.kron(np.eye(2), np.cos(ang)) * s)
    add("fsin", np.kron(np.eye(2), np.sin(ang)) * -s)

    def pair_swap(size, lo):
        m = np.zeros((size, size))
        for i in range(lo, size, 2):
            m[i + 1, i] = -1.0
            m[i, i + 1] = 1.0
        return m

    def tables(dim):
        nf = dim // 4
        inv = ROPE_BASE ** (-np.arange(nf, dtype=np.float32) / np.float32(nf))
        pos = np.stack([n // GRID_W, n % GRID_W]).astype(np.float32)
        a = pos[:, None, :] * inv[None, :, None]
        a = np.repeat(a.reshape(2 * nf, T), 2, axis=0)
        return np.cos(a), np.sin(a)

    add("swap_s", pair_swap(P, 0))
    add("swap_m", pair_swap(NOPE + ROPE, NOPE))
    cs, sn = tables(SD)
    add("cos_s", np.tile(cs, (2, 1)))
    add("sin_s", np.tile(sn, (2, 1)))
    cs, sn = tables(ROPE)
    add("cos_m", np.concatenate([np.ones((NOPE, T)), cs]))
    add("sin_m", np.concatenate([np.zeros((NOPE, T)), sn]))
    add("causal", (n[:, None] <= n[None, :]).astype(np.float32))
    add("mean_d", np.full((P, P), 1.0 / D))
    add("mean_q", np.full((P, P), 1.0 / QL))
    add("mean_kv", np.full((P, P), 1.0 / KVL))
    add("mean_h", np.kron(np.eye(2), np.full((HD, HD), 1.0 / HD)))
    add("ones", np.ones((P, P)))
    return np.ascontiguousarray(np.concatenate(parts, axis=1))


constant_array()
CONST_W = sum(w for _, w in CONSTS.values())


def build(nc, a, out):
    ctx = ExitStack()
    with ctx:
        def sb(name, shape, dt=F32):
            return ctx.enter_context(nc.sbuf_tensor(name, shape, dt))

        def sem(name):
            return ctx.enter_context(nc.semaphore(name))

        ring = sb("ring", [P, RING, UNIT])
        cst = sb("cst", [P, CONST_W])
        C = {k: cst[:, at:at + w] for k, (at, w) in CONSTS.items()}
        ident = C["ident"]
        xT = sb("xT", [P, KB, TT])
        HX = sb("HX", [P, 2 * KB * TT])
        hx = HX[:].rearrange("p (i b t) -> p i b t", i=2, b=KB)
        hT = hx[:, 0]
        xn = hx[:, 1]
        xrow = HX[:, KB * TT:]
        Kt = HX[:].rearrange("p (j n t) -> p j n t", j=NCK, n=8)
        rstd = sb("rstd", [P, TT])
        lnv = sb("lnv", [P, TT])
        gvec_rows = sb("gvec_rows", [GROWS, P])
        gvec = sb("gvec", [P, GROWS])
        lvec_rows = sb("lvec_rows", [VROWS, P])
        lvec = sb("lvec", [P, VROWS])
        scond = sb("scond", [P, KB, NG])
        stmp = sb("stmp", [P, 64])
        lb = sb("lb", [P, DEPTH, 2, HP])
        oml = sb("oml", [P, DEPTH, 2, HP])
        mod = sb("mod", [P, 6, KB, NG])
        gain = sb("gain", [P, 2, KB, NG])
        epsc = sb("epsc", [P, 1])
        wq = sb("wq", [P, 2, MH * (NOPE + ROPE)])
        wkv = sb("wkv", [P, MH, NOPE + MV])
        fnw = sb("fnw", [P, 2, FNW])
        wr = sb("wr", [P, KB, NE])
        brt = sb("brt", [P, NE])
        sink = sb("sink", [P, SH])
        kcache = sb("kcache", [P, 3, P])
        vcache = sb("vcache", [P, P])
        s0 = sb("s0", [P, 2, HP, HD])
        U = sb("U", [P, 11, 512])
        u2 = lambda i: U[:, i, :].rearrange("p (b t) -> p b t", b=2)
        U_Q, U_KV, U_HQ, U_ZF, U_ZB, U_I, U_HG, U_FN, U_SQ, U_SK, U_SKV = range(11)
        OT = sb("OT", [P, 8, TT])
        cqn = OT[:, 0:2, :]
        ckvT = sb("ckvT", [P, 3, T])
        krT = sb("krT", [NOPE + ROPE, 3, T])
        qT = sb("qT", [NOPE + ROPE, MH, TT])
        kT = sb("kT", [NOPE + ROPE, MH, 3, T])
        vM = sb("vM", [P, 3, MH * MV])
        rsq = sb("rsq", [P, 512])
        kcT = sb("kcT", [P, T])
        prS = sb("prS", [P, 4, 2 * T])
        prP = sb("prP", [P, 4, T])
        pT = sb("pT", [P, 12, T])
        mx = sb("mx", [P, 8])
        negm = sb("negm", [P, 8])
        den = sb("den", [P, 8])
        esk = sb("esk", [P, 8])
        qs = sb("qs", [P, 8, T])
        kk = sb("kk", [P, 8, T])
        lf = U[:, U_ZF:U_ZB + 1, :].rearrange("p i (n t) -> p (i n) t", t=T)
        Gc = sb("Gc", [P, 8, T])
        Qt = sb("Qt", [P, 8, T])
        QD = sb("QD", [P, 4, T])
        KD = sb("KD", [P, 4, T])
        KDt = prP
        Vh = sb("Vh", [P, 2, NG, 256])
        AT = U[:, U_HQ:U_I + 1, :].rearrange("p i (n t) -> p (i n) t", t=T)
        gs = sb("gs", [P, 512])
        F1 = pT[:, 0:8, :].rearrange("p (c h g) t -> p c h g t", c=2, h=2)
        F2 = pT[:, 8:12, :].rearrange("p (b g) t -> p b (g t)", b=2)
        sg = sb("sg", [P, NG, NE])
        sbs = sb("sbs", [P, NG, NE])
        top8 = sb("top8", [P, NG, 8])
        sel = sb("sel", [P, NG, NE])
        eqm = sb("eqm", [P, NG, NE])
        cum = sb("cum", [P, NG, NE])
        cnt = sb("cnt", [P, NG, 2])
        eg, tmp_h, tmp_c = U[:, 2, :], U[:, 3, :], U[:, 4, :]
        hid = U[:, 5:7, :]
        gsel = U[0:NE, 7, :].rearrange("p (i t) -> p i t", i=2)
        gateT = U[0:NE, 8, 0:TT]
        o_ckv = sb("o_ckv", [P, KVL])
        o_kr = sb("o_kr", [P, ROPE])
        o_st = sb("o_st", [P, 2 * HP * HD])

        ps = ctx.enter_context(nc.psum_tensor("ps", [P, 8, 512], F32))
        B = lambda i: ps[:, i, :]

        slot_full = [sem(f"slot_full{i}") for i in range(RING)]
        unit_used = [sem(f"unit_used{i}") for i in range(CLASSES)]
        S = {}

        def declare(**per_layer):
            for name, n in per_layer.items():
                S[name] = (sem(name), n)

        def wait(eng, name, l, k):
            s, n = S[name]
            assert 0 <= k <= n, name
            if l * n + k > 0:
                eng.wait_ge(s, l * n + k)

        class Chain:

            def __init__(self, name, per_layer):
                self.s, self.n, self.k, self.l = sem(name), per_layer, 0, 0

            def layer(self, l):
                assert self.k in (0, self.n), (self.k, self.n)
                self.l, self.k = l, 0

            def link(self, eng, ins):
                self.k += 1
                ins.then_inc(self.s, 1)
                eng.wait_ge(self.s, self.l * self.n + self.k)

        glob_in, layer_in = sem("glob_in"), sem("layer_in")
        out_sem, y_out = sem("out_sem"), sem("y_out")
        x_turned, x_stored, cond_turned, cond_ready, g_turned, g_stored = (
            sem(n) for n in ("x_turned", "x_stored", "cond_turned", "cond_ready", "g_turned", "g_stored"))
        setup_dve, setup_act, consts_set = sem("setup_dve"), sem("setup_act"), sem("consts_set")
        fin_sq, fin_mean, fin_rstd, fin_y, fin_turned, fin_copied = (
            sem(n) for n in ("fin_sq", "fin_mean", "fin_rstd", "fin_y", "fin_turned", "fin_copied"))
        declare(vec_turned=1, vec_stored=1, mod_done=1,
                squares=2, mean_done=2, rstd_done=2, h_ready=2 * KB,
                u_copied=11, cache_turned=1, cache_copied=1,
                lat_sq=1, lat_mean=1, lat_rstd=1, cqn_ready=1, kvn_ready=1,
                hg_exp=1, hg_f=1, hg_ln=1,
                flip_done=1, flip_copied=1, srot_done=1, srot_used=1,
                fn1_done=1, fn1_copied=1, fn2_done=1, fn2_copied=1, fn3_done=1, fn3_copied=1,
                mq_done=1, mq_copied=1, mv_done=1, mv_copied=1, krot_done=1, krot_used=1,
                kv_turned=1, kvout_copied=1,
                mk_done=1, mk_copied=1, qrot_done=1, qrot_used=1, kr_ready=1,
                scores=2, negmax=2, exps=2, probs=2, p_turned=2, p_copied=2, pv_done=2, pv_copied=2,
                keys_zeroed=1, attn_zeroed=1, diffs=1, decays=1, recur_ready=1, kd_turned=1, kd_copied=1, st_done=1, st_copied=1,
                at_done=1, at_masked=1, of_done=2, of_copied=1, o_sq=1, o_mean=1, o_rstd=1, o_ready=1,
                mix_added=N_OUT,
                route_done=1, route_exp=1, gates_ready=1, gates_turned=1, gates_stored=1,
                e_done=NE + 1, b_sel=NE, b_done=NE, hid_done=NE + 1, moe_added=1)
        moe_dve = sem("moe_dve")

        def unit_full(eng, l, n, more=0):
            per_layer = len(range(n % RING, N_USED, RING))
            eng.wait_ge(slot_full[n % RING], (l * per_layer + n // RING + 1) * 16 + more)

        def slot(n):
            return ring[:, n % RING, :]

        def used_count(l, n):
            return l * (N_LAYER // CLASSES) + n // CLASSES + 1 + RING // CLASSES

        def unit_done(eng, l, n, more=0):
            eng.wait_ge(unit_used[n % CLASSES], used_count(l, n) + more)

        block = ctx.enter_context(nc.Block())

        @block.sync
        def _(sp):
            w_in_v = a["w_in"].rearrange("l (b p) n -> l p b n", p=P)
            w_ada_v = a["w_ada"].rearrange("l (b p) n -> l p b n", p=P)
            w_out_v = a["w_out"].rearrange("l (b p) n -> l p b n", p=P)

            def load(l, n, src, shape, it=0):
                at = l * (N_LAYER // CLASSES) + n // CLASSES + 1
                sp.wait_ge(unit_used[n % CLASSES], at + it * (RING // CLASSES))
                dst = slot(n)[:, 0:shape[0] * shape[1]].rearrange("p (b n) -> p b n", b=shape[0])
                sp.dma_start(dst, src).then_inc(slot_full[n % RING], 16)

            for l in range(DEPTH):
                for j in range(N_ADA):
                    load(l, j, w_ada_v[l, :, :, j * 256:(j + 1) * 256], (KB, 256))
                for j, (c0, w) in enumerate(IN_UNITS):
                    load(l, U_IN + j, w_in_v[l, :, :, c0:c0 + w], (KB, w))
                for j in range(N_OUT):
                    load(l, U_OUT + j, w_out_v[l, :, :, j * 256:(j + 1) * 256], (KB, 256))
                for j, name in enumerate(("sh_w_gate", "sh_w_up")):
                    load(l, U_SH + j, a[name].rearrange("l (b p) n -> l p b n", p=P)[l], (KB, DE))
                load(l, U_SH + 2, a["sh_w_down"].rearrange("l (b p) n -> l p b n", p=P)[l], (2, D))
                with sp.Fori(0, E_ITERS, 1) as it:
                    for e in range(EB):
                        for j, (name, sh) in enumerate((("moe_w_gate", (KB, DE)), ("moe_w_up", (KB, DE)),
                                                        ("moe_w_down", (2, D)))):
                            src = a[name].rearrange("l e (b p) n -> l e p b n", p=P)
                            load(l, U_EX + 3 * e + j, src[l, it * EB + e], sh, it)

        @block.gpsimd
        def _(pool):
            pool.memset(epsc[:], EPS).then_inc(consts_set, 1)
            pool.memset(krT[:], 0.0).then_inc(consts_set, 1)
            pool.memset(kcache[:], 0.0).then_inc(consts_set, 1)
            pool.dma_start(cst[:], a["consts"]).then_inc(glob_in, 16)
            pool.dma_start(gvec_rows[R_COND:R_COND + 8], a["c_ctx"].rearrange("(b p) -> b p", p=P)).then_inc(glob_in, 16)
            pool.dma_start(gvec_rows[R_COND + 8:R_COND + 16], a["c"].rearrange("o (b p) -> (o b) p", p=P)).then_inc(glob_in, 16)
            pool.dma_start(gvec_rows[R_LB:R_LB + 8], a["hg_lb_logits"].rearrange("r l (b p) -> (r l b) p", p=P)).then_inc(glob_in, 16)
            pool.dma_start(gvec_rows[R_FG:R_FG + 8], a["final_norm_g"].rearrange("(b p) -> b p", p=P)).then_inc(glob_in, 16)
            for g, name in enumerate(("x_prompt", "x_sample")):
                pool.dma_start(xrow[:, g * D:(g + 1) * D], a[name][0]).then_inc(glob_in, 16)
            pool.wait_ge(consts_set, 3)
            for l in range(DEPTH):
                wait(pool, "gates_stored", l, 0)
                rows = (("b_ada", R_BADA, 48), ("norm1_g", R_N1, 8), ("norm2_g", R_N2, 8),
                        ("mla_q_norm_g", R_QN, 2), ("mla_kv_norm_g", R_KVN, 1))
                loads = [(lvec_rows[r:r + n], a[name].rearrange("l (b p) -> l b p", p=P)[l]) for name, r, n in rows]
                hgn = a["hg_norm_g"].rearrange("l (o p) -> l o p", o=1)
                loads += [(lvec_rows[R_HGN:R_HGN + 1, r * HD:(r + 1) * HD], hgn[l]) for r in range(2)]
                loads += [
                    (wq[:], a["mla_w_q_up"].rearrange("l (b p) n -> l p b n", p=P)[l]),
                    (wkv[:].rearrange("p h n -> p (h n)"), a["mla_w_kv_up"][l]),
                    (fnw[:], a["fn_w"].rearrange("l (b p) n -> l p b n", p=P)[l]),
                    (wr[:], a["moe_w_router"].rearrange("l (b p) n -> l p b n", p=P)[l]),
                    (brt[:], a["moe_b_router"].rearrange("l (o n) -> l o n", o=1)[l].broadcast_to([P, NE])),
                    (sink[:], a["swa_sink"].rearrange("l (o n) -> l o n", o=1)[l].broadcast_to([P, SH])),
                    (kcache[:, 0, :], a["cache_swa_k"][0].rearrange("l t k d -> l t (k d)")[l]),
                    (kcache[:, 1, :], a["cache_mla_ckv"][0][l]),
                    (kcache[:, 2, NOPE:NOPE + ROPE], a["cache_mla_krope"][0][l]),
                    (vcache[:], a["cache_swa_v"][0].rearrange("l t k d -> l t (k d)")[l]),
                ]
                st = a["state_hgrn"][0].rearrange("l r (q s) d e -> l r q (s d) e", s=2)
                loads += [(s0[:, r, q, :], st[l, r, q]) for r in range(2) for q in range(HP)]
                assert len(loads) == LOADS
                for dst, src in loads:
                    pool.dma_start(dst, src).then_inc(layer_in, 16)
                wait(pool, "u_copied", l, 11)
                for j in range(NCK - 1):
                    z = pool.memset(Kt[:, j, :, (j + 1) * CK:], 0.0)
                z.then_inc(S["keys_zeroed"][0], 1)
                kv = u2(U_SKV)[:, 0, :]
                for dst, src in ((out["k"], kv[:, 0:128]), (out["v"], kv[:, 128:256])):
                    pool.dma_start(dst[0].rearrange("l t k d -> l t (k d)")[l], src).then_inc(out_sem, 16)
                wait(pool, "kvout_copied", l, 1)
                pool.dma_start(out["ckv"][0][l], o_ckv[:]).then_inc(out_sem, 16)
                pool.dma_start(out["kr"][0][l], o_kr[:]).then_inc(out_sem, 16)
                wait(pool, "recur_ready", l, 1)
                pool.memset(AT, 0.0).then_inc(S["attn_zeroed"][0], 1)
                wait(pool, "st_copied", l, 1)
                sto = out["st"][0].rearrange("l r (q s) d e -> l r q (s d) e", s=2)
                for r in range(2):
                    for q in range(HP):
                        at = (r * HP + q) * HD
                        pool.dma_start(sto[l, r, q], o_st[:, at:at + HD]).then_inc(out_sem, 16)
            for g, name in enumerate(("y_p", "y_s")):
                pool.wait_ge(fin_copied, 4 * (g + 1))
                pool.dma_start(out[name][0], xrow[:, g * D:(g + 1) * D]).then_inc(y_out, 16)
            pool.wait_ge(y_out, 32)
            pool.wait_ge(out_sem, 16 * STORES * DEPTH)

        @block.tensor
        def _(pe):
            mm = nc.tensor.matmul

            def tr(o, i, n=P):
                return nc.tensor.transpose(o, i, ident[0:n, 0:n])

            def used(ins, n):
                ins.then_inc(unit_used[n % CLASSES], 1)

            for s in unit_used:
                pe.sem_inc(s, RING // CLASSES)

            pe.wait_ge(glob_in, 16 * 7)
            tr(ps[:, 0, 0:GROWS], gvec_rows[:], GROWS).then_inc(g_turned, 1)
            for b in range(KB):
                for g in range(NG):
                    t = tr(ps[:, 1 + b // 2, (b % 2) * TT + g * T:(b % 2) * TT + (g + 1) * T],
                           xrow[:, g * D + b * P:g * D + (b + 1) * P])
                if b % 2:
                    t.then_inc(x_turned, 1)
            pe.wait_ge(cond_ready, 1)

            for l in range(DEPTH):
                pe.wait_ge(layer_in, (l + 1) * 16 * LOADS)
                pe.wait_ge(x_stored, 4)
                pe.wait_ge(g_stored, 1)
                wait(pe, "moe_added", l, 0)
                tr(ps[:, 0, 0:VROWS], lvec_rows[:], VROWS).then_inc(S["vec_turned"][0], 1)
                for j in range(3):
                    c = tr(ps[0:(P if j < 2 else NOPE + ROPE), 1, j * P:(j + 1) * P],
                           kcache[:, j, 0:(P if j < 2 else NOPE + ROPE)])
                c.then_inc(S["cache_turned"][0], 1)
                for j in range(N_ADA):
                    unit_full(pe, l, j)
                    w = slot(j).rearrange("p (b n) -> p b n", b=KB)
                    for h in range(2):
                        o = ps[:, 7, (2 * j + h) * NG:(2 * j + h + 1) * NG]
                        for b in range(KB):
                            m = mm(o, w[:, b, h * P:(h + 1) * P], scond[:, b, :], start=(b == 0), stop=(b == KB - 1))
                    used(m, j)

                def mean_square(k):
                    wait(pe, "squares", l, k + 1)
                    bank = 0 if k == 0 else 4
                    if k == 0:
                        wait(pe, "vec_stored", l, 1)
                    for b in range(KB):
                        m = mm(ps[:, bank, 0:TT], C["mean_d"], xn[:, b, :], start=(b == 0), stop=(b == KB - 1))
                    m.then_inc(S["mean_done"][0], 1)

                mean_square(0)

                def in_unit(j):
                    unit_full(pe, l, U_IN + j)
                    w_ = IN_UNITS[j][1]
                    return slot(U_IN + j)[:, 0:KB * w_].rearrange("p (b n) -> p b n", b=KB)

                def into(i):
                    if i == 0:
                        wait(pe, "cache_copied", l, 1)
                    if i == 6:
                        wait(pe, "mod_done", l, 1)
                    if i == 7:
                        wait(pe, "rstd_done", l, 1)
                    if i >= 8:
                        wait(pe, "u_copied", l, i - 7)
                    return (i + 1) % 8

                def feature_major(i, lhs):
                    bank = into(i)
                    for h in range(2):
                        for b in range(KB):
                            if i == 0 and h == 0:
                                wait(pe, "h_ready", l, b + 1)
                            m = mm(ps[:, bank, h * TT:(h + 1) * TT], lhs(h, b), hT[:, b, :], start=(b == 0), stop=(b == KB - 1))
                    return m

                def token_major(i, w):
                    bank = into(i)
                    for g in range(NG):
                        for b in range(KB):
                            m = mm(ps[:, bank, g * 256:(g + 1) * 256], hT[:, b, g * T:(g + 1) * T], w[:, b, :],
                                   start=(b == 0), stop=(b == KB - 1))
                    return m

                for j in range(N_IN):
                    w = in_unit(j)
                    if j == 1:
                        bank = into(1)
                        for b in range(KB):
                            mm(ps[:, bank, 0:TT], w[:, b, 0:KVL], hT[:, b, :], start=(b == 0), stop=(b == KB - 1))
                        for b in range(KB):
                            m = mm(ps[NOPE:NOPE + ROPE, bank, TT:2 * TT], w[:, b, KVL:KVL + ROPE], hT[:, b, :],
                                   start=(b == 0), stop=(b == KB - 1))
                    elif j in (5, 7):
                        m = token_major(j, w)
                    elif j == 8:
                        bank = into(8)
                        for h in range(SH):
                            r, c = h // 2, h % 2
                            for b in range(KB):
                                m = mm(ps[64 * r:64 * r + 64, bank, c * TT:(c + 1) * TT], w[:, b, h * SD:(h + 1) * SD],
                                       hT[:, b, :], start=(b == 0), stop=(b == KB - 1))
                    elif j == 9:
                        bank = into(9)
                        for b in range(KB):
                            mm(ps[:, bank, 0:TT], w[:, b, 0:128], hT[:, b, :], start=(b == 0), stop=(b == KB - 1))
                        m = token_major(10, w)
                    else:
                        m = feature_major(j, lambda h, b, w=w: w[:, b, h * P:(h + 1) * P])
                    used(m, U_IN + j)

                wait(pe, "lat_sq", l, 1)
                wait(pe, "u_copied", l, 11)
                for b in range(2):
                    mm(ps[:, 3, 0:TT], C["mean_q"], cqn[:, b, :], start=(b == 0), stop=(b == 1))
                mm(ps[:, 3, TT:2 * TT], C["mean_kv"], rsq[:, 0:TT], start=True, stop=True).then_inc(S["lat_mean"][0], 1)
                mm(B(4), C["flip"], U[:, U_I, :], start=True, stop=True).then_inc(S["flip_done"][0], 1)
                srt = U[:, U_SQ:U_SK + 1, :].rearrange("p i t -> p (i t)").rearrange("p (b t) -> p b t", t=TT)[:, 0:3, T:TT]
                mm(ps[:, 5, 0:3 * T], C["swap_s"], srt, start=True, stop=True).then_inc(S["srot_done"][0], 1)
                for g in range(NG):
                    for cb in range(2):
                        m = mm(ps[:, 6 + g, cb * 256:(cb + 1) * 256], u2(U_FN)[:, g, cb * P:(cb + 1) * P], C["dft"],
                               start=True, stop=True)
                m.then_inc(S["fn1_done"][0], 1)
                wait(pe, "cqn_ready", l, 1)
                HQ = NOPE + ROPE
                for h in range(MH):
                    for b in range(2):
                        m = mm(ps[0:HQ, h // 2, (h % 2) * TT:(h % 2 + 1) * TT], wq[:, b, h * HQ:(h + 1) * HQ], cqn[:, b, :],
                               start=(b == 0), stop=(b == 1))
                m.then_inc(S["mq_done"][0], 1)
                wait(pe, "kvn_ready", l, 1)
                for n in range(3):
                    m = mm(ps[:, 2 + n // 2, (n % 2) * 256:(n % 2 + 1) * 256], ckvT[:, n, :], wkv[:, :, NOPE:],
                           start=True, stop=True)
                m.then_inc(S["mv_done"][0], 1)
                mm(ps[0:HQ, 3, 256:384], C["swap_m"][0:HQ, 0:HQ], krT[:, 1, :], start=True, stop=True)\
                    .then_inc(S["krot_done"][0], 1)
                wait(pe, "fn1_copied", l, 1)
                for cb in range(2):
                    for h, m_ in enumerate(("fcos", "fsin")):
                        m = mm(ps[:, 6, cb * TT:(cb + 1) * TT], C[m_], F1[:, cb, h].rearrange("p g t -> p (g t)"),
                               start=(h == 0), stop=(h == 1))
                m.then_inc(S["fn2_done"][0], 1)
                wait(pe, "flip_copied", l, 1)
                wait(pe, "srot_used", l, 1)
                wait(pe, "mq_copied", l, 1)
                for h, bank in enumerate((4, 5, 0, 1)):
                    m = mm(ps[0:NOPE, bank, 0:3 * T], wkv[:, h, 0:NOPE], ckvT[:].rearrange("p n t -> p (n t)"),
                           start=True, stop=True)
                m.then_inc(S["mk_done"][0], 1)
                wait(pe, "fn2_copied", l, 1)
                for ob in range(2):
                    for cb in range(2):
                        m = mm(ps[:, 7, ob * TT:(ob + 1) * TT], fnw[:, cb, ob * P:(ob + 1) * P], F2[:, cb, :],
                               start=(cb == 0), stop=(cb == 1))
                m.then_inc(S["fn3_done"][0], 1)
                mm(ps[0:HQ, 6, :].rearrange("p (h t) -> p h t", h=MH), C["swap_m"][0:HQ, 0:HQ], qT[:, :, T:TT], start=True, stop=True)\
                    .then_inc(S["qrot_done"][0], 1)
                wait(pe, "mk_copied", l, 1)
                tr(ps[:, 0, 0:P], ckvT[:, 0, :])
                tr(ps[:, 0, P:P + HQ], krT[:, 0, :], HQ).then_inc(S["kv_turned"][0], 1)

                def score(o, q, k):
                    return mm(o, q, k, start=True, stop=True)

                def transpose_probs(n):
                    wait(pe, "probs", l, n + 1)
                    if n == 0:
                        wait(pe, "qrot_used", l, 1)
                        wait(pe, "fn3_copied", l, 1)
                        wait(pe, "kvout_copied", l, 1)
                    wait(pe, "p_copied", l, n)
                    for h in range(4):
                        for c in range(3):
                            i = 3 * h + c
                            src = prS[:, h, c * T:(c + 1) * T] if c < 2 else prP[:, h, :]
                            m = tr(ps[:, (6 + i // 4) % 8, (i % 4) * T:(i % 4 + 1) * T], src)
                    m.then_inc(S["p_turned"][0], 1)

                def values(n, v):
                    wait(pe, "p_copied", l, n + 1)
                    if n == 0:
                        wait(pe, "mk_copied", l, 1)
                    wait(pe, "pv_copied", l, n)
                    for h in range(4):
                        r = (h % 2) * 64
                        o = ps[r:r + 64, 1, (h // 2) * TT:(h // 2 + 1) * TT]
                        mm(o[:, 0:T], v(h, 2), pT[:, 3 * h + 2, :], start=True, stop=True)
                        mm(o[:, T:TT], v(h, 0), pT[:, 3 * h, :], start=True, stop=False)
                        m = mm(o[:, T:TT], v(h, 1), pT[:, 3 * h + 1, :], start=False, stop=True)
                    m.then_inc(S["pv_done"][0], 1)

                wait(pe, "srot_used", l, 1)
                wait(pe, "mv_copied", l, 1)
                wait(pe, "krot_used", l, 1)
                for h in range(SH):
                    r, c = h // 2, h % 2
                    q = u2(U_SQ)[64 * r:64 * r + 64, c, :]
                    k = u2(U_SK)[64 * r:64 * r + 64, 0, :]
                    score(ps[:, 4 + r, c * T:(c + 1) * T], q[:, 0:T], k[:, 0:T])
                    score(ps[:, 2 + r, c * TT:c * TT + T], q[:, T:TT], k[:, T:TT])
                    m = score(ps[:, 2 + r, c * TT + T:(c + 1) * TT], q[:, T:TT], kcT[64 * r:64 * r + 64, :])
                m.then_inc(S["scores"][0], 1)
                transpose_probs(0)

                def swa_v(h, c):
                    k = h // 2
                    if c == 1:
                        return vcache[:, k * SD:(k + 1) * SD]
                    return u2(U_SKV)[:, 0 if c == 2 else 1, 128 + k * SD:128 + (k + 1) * SD]

                values(0, swa_v)
                wait(pe, "exps", l, 1)
                wait(pe, "kr_ready", l, 1)
                wait(pe, "qrot_used", l, 1)
                for h in range(MH):
                    r, c = h // 2, h % 2
                    score(ps[:, 4 + r, c * T:(c + 1) * T], qT[:, h, 0:T], kT[:, h, 0, :])
                    m = score(ps[:, 2 + r, c * TT:(c + 1) * TT], qT[:, h, T:TT], kT[:, h, 1:3, :].rearrange("p n t -> p (n t)"))
                m.then_inc(S["scores"][0], 1)
                transpose_probs(1)
                values(1, lambda h, c: vM[:, (1, 2, 0)[c], h * MV:(h + 1) * MV])

                wait(pe, "recur_ready", l, 1)
                wait(pe, "exps", l, 2)
                for n in range(4):
                    m = tr(ps[:, 2, n * P:(n + 1) * P], KD[:, n, :])
                m.then_inc(S["kd_turned"][0], 1)
                wait(pe, "p_copied", l, 2)
                wait(pe, "keys_zeroed", l, 1)
                for r in range(2):
                    for n in range(8):
                        for j in range(NCK):
                            m = mm(ps[:, 4 + 2 * r + n // 4, (n % 4) * T + j * CK:(n % 4) * T + (j + 1) * CK],
                                   Kt[64 * r:64 * r + 64, j, n, :], Qt[64 * r:64 * r + 64, n, j * CK:(j + 1) * CK],
                                   start=True, stop=True)
                m.then_inc(S["at_done"][0], 1)
                wait(pe, "kd_copied", l, 1)
                for n in range(4):
                    for r in range(2):
                        h = 2 * (n % 2) + r
                        m = mm(ps[64 * r:64 * r + 64, 3, n * HD:(n + 1) * HD], KDt[:, n, 64 * r:64 * r + 64],
                               Vh[:, n // 2, 0, h * HD:(h + 1) * HD], start=True, stop=True)
                m.then_inc(S["st_done"][0], 1)
                wait(pe, "at_masked", l, 1)
                wait(pe, "pv_copied", l, 2)
                wait(pe, "st_copied", l, 1)
                for d in range(2):
                    for q in range(HP):
                        for g in range(NG):
                            n = (d * HP + q) * NG + g
                            for r in range(2):
                                h = 2 * q + r
                                o = ps[64 * r:64 * r + 64, 2 * d + r, (q * NG + g) * T:(q * NG + g + 1) * T]
                                if g == 1:
                                    mm(o, s0[64 * r:64 * r + 64, d, q, :], QD[64 * r:64 * r + 64, d * HP + q, :],
                                       start=True, stop=False)
                                m = mm(o, Vh[:, d, g, h * HD:(h + 1) * HD], AT[:, r * 8 + n, :],
                                       start=(g == 0), stop=True)
                    m.then_inc(S["of_done"][0], 1)
                wait(pe, "o_sq", l, 1)
                mm(B(4), C["mean_h"], Qt[:, 0:4, :].rearrange("p n t -> p (n t)"), start=True, stop=True)\
                    .then_inc(S["o_mean"][0], 1)

                wait(pe, "o_ready", l, 1)
                for j in range(N_OUT):
                    unit_full(pe, l, U_OUT + j)
                    w = slot(U_OUT + j).rearrange("p (b n) -> p b n", b=KB)
                    for h in range(2):
                        for b in range(KB):
                            m = mm(ps[:, j, h * TT:(h + 1) * TT], w[:, b, h * P:(h + 1) * P], OT[:, b, :],
                                   start=(b == 0), stop=(b == KB - 1))
                    used(m, U_OUT + j)

                mean_square(1)
                wait(pe, "h_ready", l, 2 * KB)
                for g in range(NG):
                    for b in range(KB):
                        m = mm(ps[:, 5, g * NE:(g + 1) * NE], hT[:, b, g * T:(g + 1) * T], wr[:, b, :],
                               start=(b == 0), stop=(b == KB - 1))
                m.then_inc(S["route_done"][0], 1)
                wait(pe, "gates_ready", l, 1)
                for g in range(NG):
                    m = tr(ps[0:NE, 5, 256 + g * T:256 + (g + 1) * T], sel[:, g, :])
                m.then_inc(S["gates_turned"][0], 1)

                def expert_in(n, k, it, step, first=False):
                    for i, bank in enumerate((4, 5)):
                        unit_full(pe, l, n + i, it * 16)
                        w = slot(n + i).rearrange("p (b n) -> p b n", b=KB)
                        if first:
                            if i == 0:
                                wait(pe, "rstd_done", l, 2)
                            else:
                                wait(pe, "gates_stored", l, 1)
                        elif i == 0:
                            pe.wait_ge(S["hid_done"][0], l * (NE + 1) + k + it * step)
                        for h in range(2):
                            for b in range(KB):
                                m = mm(ps[:, bank, h * TT:(h + 1) * TT], w[:, b, h * P:(h + 1) * P], hT[:, b, :],
                                       start=(b == 0), stop=(b == KB - 1))
                        used(m, n + i)

                def expert_out(n, k, it, step, start, stop):
                    pe.wait_ge(S["hid_done"][0], l * (NE + 1) + k + 1 + it * step)
                    unit_full(pe, l, n, it * 16)
                    w = slot(n).rearrange("p (b n) -> p b n", b=2)
                    for db in range(KB):
                        for f in range(2):
                            m = mm(ps[:, db // 2, (db % 2) * TT:(db % 2 + 1) * TT], w[:, f, db * P:(db + 1) * P],
                                   hid[:, k % 2, f * TT:(f + 1) * TT],
                                   start=(start and f == 0 and db % 2 == 0), stop=(stop and f == 1), skip_group_check=True)
                    used(m, n)

                expert_in(U_SH, 0, 0, 0, first=True)
                wait(pe, "mix_added", l, N_OUT)
                wait(pe, "gates_stored", l, 1)
                expert_out(U_SH + 2, 0, 0, 0, True, False)
                with pe.Fori(0, E_ITERS, 1) as it:
                    for e in range(EB):
                        expert_in(U_EX + 3 * e, e + 1, it, EB)
                        pe.wait_ge(S["b_sel"][0], l * NE + e + 1 + it * EB)
                        mm(ps[:, 6, 0:TT], C["ones"][0:NE, :], gsel[:, e % 2, :], start=True, stop=True)\
                            .then_inc(S["b_done"][0], 1)
                        expert_out(U_EX + 3 * e + 2, e + 1, it, EB, False, False)
                for n in range(N_USED, N_LAYER):
                    pe.sem_inc(unit_used[n % CLASSES], 1)

            pe.wait_ge(fin_sq, 1)
            for b in range(KB):
                m = mm(ps[:, 4, 0:TT], C["mean_d"], xn[:, b, :], start=(b == 0), stop=(b == KB - 1))
            m.then_inc(fin_mean, 1)
            pe.wait_ge(fin_y, 1)
            for g in range(NG):
                for b in range(KB):
                    m = tr(ps[:, g * 2 + b // 4, (b % 4) * P:(b % 4 + 1) * P], hT[:, b, g * T:(g + 1) * T])
                    if b % 4 == 3:
                        m.then_inc(fin_turned, 1)

        @block.scalar
        def _(act):
            fn = nc.scalar.activation
            chain = Chain("act_order", ACT_LINKS)

            def rsqrt(out_ap, tmp, src, name, l, s=None):
                chain.link(act, fn(tmp, src, ACT.Ln, bias=epsc[:, 0:1]))
                r = fn(out_ap, tmp, ACT.Exp, scale=-0.5)
                r.then_inc(s if s is not None else S[name][0], 1)

            act.wait_ge(consts_set, 3)
            act.wait_ge(g_stored, 1)
            fn(stmp[:, 0:16], gvec[:, R_COND:R_COND + 16], ACT.Exp, scale=-1.0).then_inc(setup_act, 1)
            act.wait_ge(setup_dve, 1)
            fn(stmp[:, 16:24], stmp[:, 24:32], ACT.Exp).then_inc(setup_act, 1)
            for j in range(4):
                act.wait_ge(x_turned, j + 1)
                fn(xT[:, 2 * j:2 * j + 2, :].rearrange("p b t -> p (b t)"), B(1 + j), ACT.Copy).then_inc(x_stored, 1)

            for l in range(DEPTH):
                chain.layer(l)

                def copy(dst, src, name=None):
                    c = fn(dst, src, ACT.Copy)
                    if name:
                        c.then_inc(S[name][0], 1)
                    return c

                wait(act, "vec_turned", l, 1)
                copy(lvec[:], ps[:, 0, 0:VROWS], "vec_stored")
                wait(act, "cache_turned", l, 1)
                copy(kcT[:], ps[:, 1, 0:P])
                copy(ckvT[:, 2, :], ps[:, 1, P:2 * P])
                copy(krT[NOPE:, 2, :], ps[NOPE:NOPE + ROPE, 1, 2 * P:3 * P], "cache_copied")
                wait(act, "mean_done", l, 1)
                rsqrt(rstd[:], lnv[:], ps[:, 0, 0:TT], "rstd_done", l)
                for i in range(11):
                    unit_done(act, l, U_IN + min(i, N_IN - 1))
                    if i == 0:
                        if l > 0:
                            act.wait_ge(out_sem, l * 16 * STORES)
                    bank = (i + 1) % 8
                    if i == 1:
                        copy(U[:, i, 0:TT], ps[:, bank, 0:TT])
                        copy(krT[NOPE:, 0:2, :].rearrange("p n t -> p (n t)"), ps[NOPE:NOPE + ROPE, bank, TT:2 * TT], "u_copied")
                    elif i == 9:
                        copy(U[:, i, 0:TT], ps[:, bank, 0:TT], "u_copied")
                    else:
                        copy(U[:, i, :], ps[:, bank, :], "u_copied")
                wait(act, "u_copied", l, 11)
                fn(lf.rearrange("p n t -> p (n t)"), U[:, U_ZF:U_ZB + 1, :].rearrange("p i t -> p (i t)"), ACT.Exp, scale=-1.0)
                fn(Gc[:, 0:4, :].rearrange("p n t -> p (n t)"), U[:, U_HQ, :], ACT.Exp, scale=-1.0)
                fn(Gc[:, 4:8, :].rearrange("p n t -> p (n t)"), U[:, U_HG, :], ACT.Exp, scale=-1.0).then_inc(S["hg_exp"][0], 1)
                wait(act, "lat_mean", l, 1)
                wait(act, "lat_sq", l, 1)
                rsqrt(rsq[:], gs[:], B(3), "lat_rstd", l)
                wait(act, "flip_done", l, 1)
                copy(Vh[:, 1, :, :].rearrange("p g n -> p (g n)"), B(4))
                copy(Vh[:, 0, :, :].rearrange("p g n -> p (g n)"), U[:, U_I, :], "flip_copied")
                wait(act, "fn1_done", l, 1)
                for g in range(NG):
                    c = copy(F1[:, :, :, g, :], ps[:, 6 + g, :].rearrange("p (c h t) -> p c h t", c=2, h=2))
                c.then_inc(S["fn1_copied"][0], 1)
                wait(act, "hg_f", l, 1)
                fn(lf[:, 0:4, :], Qt[:, 0:4, :], ACT.Ln)
                fn(lf[:, 4:8, ::-1], Qt[:, 4:8, :], ACT.Ln).then_inc(S["hg_ln"][0], 1)
                wait(act, "mq_done", l, 1)
                copy(qT[:].rearrange("p h t -> p (h t)"), ps[0:NOPE + ROPE, 0:2, :].rearrange("p b t -> p (b t)"), "mq_copied")
                wait(act, "mv_done", l, 1)
                wait(act, "krot_done", l, 1)
                copy(vM[:].rearrange("p n t -> p (n t)"), ps[:, 2:4, :].rearrange("p b t -> p (b t)")[:, 0:768], "mv_copied")
                wait(act, "fn2_done", l, 1)
                copy(F2.rearrange("p b t -> p (b t)"), B(6), "fn2_copied")
                wait(act, "mk_done", l, 1)
                for h, bank in enumerate((4, 5, 0, 1)):
                    c = copy(kT[0:NOPE, h].rearrange("p n t -> p (n t)"), ps[0:NOPE, bank, 0:3 * T])
                c.then_inc(S["mk_copied"][0], 1)
                wait(act, "fn3_done", l, 1)
                copy(OT[:, 4:6, :].rearrange("p b t -> p (b t)"), B(7), "fn3_copied")
                wait(act, "kv_turned", l, 1)
                copy(o_ckv[:], ps[:, 0, 0:P])
                copy(o_kr[:], ps[:, 0, P + NOPE:P + NOPE + ROPE], "kvout_copied")

                def softmax_exp(n, scale):
                    wait(act, "negmax", l, n + 1)
                    for h in range(4):
                        r, c = h // 2, h % 2
                        fn(prS[:, h, :], ps[:, 2 + r, c * TT:(c + 1) * TT], ACT.Exp, bias=negm[:, h:h + 1], scale=scale,
                           accum_out=den[:, h:h + 1])
                        e = fn(prP[:, h, :], ps[:, 4 + r, c * T:(c + 1) * T], ACT.Exp, bias=negm[:, 4 + h:5 + h], scale=scale,
                               accum_out=den[:, 4 + h:5 + h])
                        if h == 3 and n == 1:
                            e.then_inc(S["exps"][0], 1)
                    if n == 0:
                        fn(esk[:], mx[:], ACT.Exp).then_inc(S["exps"][0], 1)

                def softmax_out(n, blk):
                    wait(act, "p_turned", l, n + 1)
                    for i, bank in enumerate((6, 7, 0)):
                        c = copy(pT[:, 4 * i:4 * i + 4, :].rearrange("p n t -> p (n t)"), B(bank))
                    c.then_inc(S["p_copied"][0], 1)
                    wait(act, "pv_done", l, n + 1)
                    copy(OT[:, blk:blk + 2, :].rearrange("p b t -> p (b t)"), B(1), "pv_copied")

                softmax_exp(0, SWA_SCALE)
                softmax_out(0, 6)
                softmax_exp(1, MLA_SCALE)
                wait(act, "diffs", l, 1)
                fn(Qt[:], Qt[:], ACT.Exp)
                for j in range(NCK):
                    kj = Kt[:, j, :, 0:(j + 1) * CK]
                    fn(kj, kj, ACT.Exp)
                fn(KD[:], KD[:], ACT.Exp)
                fn(QD[:], QD[:], ACT.Exp).then_inc(S["decays"][0], 1)
                softmax_out(1, 0)
                wait(act, "kd_turned", l, 1)
                copy(KDt[:].rearrange("p n t -> p (n t)"), B(2), "kd_copied")
                wait(act, "st_done", l, 1)
                copy(o_st[:], ps[:, 3, 0:256], "st_copied")
                wait(act, "of_done", l, 1)
                ofw = prS[:, 0:2, :].rearrange("p n t -> p (n t)")
                for r in range(2):
                    c = copy(ofw[64 * r:64 * r + 64], ps[64 * r:64 * r + 64, r, :])
                c.then_inc(S["of_copied"][0], 1)
                wait(act, "o_mean", l, 1)
                rsqrt(rsq[:], prP[:].rearrange("p n t -> p (n t)"), B(4), "o_rstd", l)
                wait(act, "mean_done", l, 2)
                rsqrt(rstd[:], lnv[:], ps[:, 4, 0:TT], "rstd_done", l)
                wait(act, "route_done", l, 1)
                fn(sg[:].rearrange("p g e -> p (g e)"), ps[:, 5, 0:NG * NE], ACT.Exp, scale=-1.0).then_inc(S["route_exp"][0], 1)
                wait(act, "gates_turned", l, 1)
                copy(gateT, ps[0:NE, 5, 256:512], "gates_stored")

                def gate_exp(k, it, step):
                    unit_done(act, l, U_SH + 3 * k, it * step)
                    fn(eg, B(4), ACT.Exp, scale=-1.0).then_inc(S["e_done"][0], 1)

                gate_exp(0, 0, 0)
                with act.Fori(0, E_ITERS, 1) as it:
                    for e in range(EB):
                        gate_exp(e + 1, it, EB)

            act.wait_ge(fin_mean, 1)
            chain2 = sem("fin_act")
            fn(lnv[:], ps[:, 4, 0:TT], ACT.Ln, bias=epsc[:, 0:1]).then_inc(chain2, 1)
            act.wait_ge(chain2, 1)
            fn(rstd[:], lnv[:], ACT.Exp, scale=-0.5).then_inc(fin_rstd, 1)
            for i in range(4):
                act.wait_ge(fin_turned, i + 1)
                for q in range(2):
                    fn(xrow[:, i * 512 + q * 256:i * 512 + (q + 1) * 256], ps[:, i, q * 256:(q + 1) * 256], ACT.Copy)\
                        .then_inc(fin_copied, 1)

        @block.vector
        def _(dve):
            v = nc.vector
            chain = Chain("dve_order", DVE_LINKS)
            sc_ = sem("dve_setup")
            cnt_ = [0]

            def link0(ins):
                cnt_[0] += 1
                ins.then_inc(sc_, 1)
                dve.wait_ge(sc_, cnt_[0])

            dve.wait_ge(consts_set, 3)
            dve.wait_ge(g_turned, 1)
            v.tensor_copy(gvec[:], ps[:, 0, 0:GROWS]).then_inc(g_stored, 1)
            dve.wait_ge(g_stored, 1)
            lg = gvec[:, R_LB:R_LB + 8].rearrange("p (r l q) -> p l r q", r=2, l=DEPTH)
            m_ = stmp[:, 32:36].rearrange("p (r q) -> p r q", r=2)
            d_ = stmp[:, 24:32].rearrange("p (l r q) -> p l r q", l=DEPTH, r=2)
            e_ = stmp[:, 16:24].rearrange("p (l r q) -> p l r q", l=DEPTH, r=2)
            link0(v.tensor_tensor(m_, lg[:, 0], lg[:, 1], ALU.max))
            link0(v.tensor_tensor(d_[:, 0], lg[:, 0], m_, ALU.subtract))
            v.tensor_tensor(d_[:, 1], lg[:, 1], m_, ALU.subtract).then_inc(setup_dve, 1)
            dve.wait_ge(setup_act, 1)
            link0(v.tensor_scalar(stmp[:, 40:56], stmp[:, 0:16], 1.0, None, ALU.add))
            link0(v.reciprocal(stmp[:, 40:56], stmp[:, 40:56]))
            link0(v.tensor_tensor(scond[:].rearrange("p b g -> p g b"), gvec[:, 0:16].rearrange("p (g b) -> p g b", g=2),
                                  stmp[:, 40:56].rearrange("p (g b) -> p g b", g=2), ALU.mult))
            dve.wait_ge(setup_act, 2)
            link0(v.tensor_tensor(m_, e_[:, 0], e_[:, 1], ALU.add))
            link0(v.reciprocal(stmp[:, 36:40], stmp[:, 32:36]))
            r_ = stmp[:, 36:40].rearrange("p (r q) -> p r q", r=2)
            for i in range(DEPTH):
                link0(v.tensor_tensor(e_[:, i], e_[:, i], r_, ALU.mult))
            link0(v.tensor_tensor(d_[:, 1], e_[:, 0], e_[:, 1], ALU.add))
            link0(v.tensor_tensor(lb[:, 0], e_[:, 0], e_[:, 0], ALU.subtract))
            link0(v.tensor_tensor(lb[:, 1], d_[:, 1], e_[:, 0], ALU.subtract))
            link0(v.tensor_scalar(oml[:], lb[:], -1.0, 1.0, ALU.mult, ALU.add))
            dve.wait_ge(x_stored, 4)
            v.memset(stmp[:, 56:57], 0.0).then_inc(cond_ready, 1)

            for l in range(DEPTH):
                chain.layer(l)
                link = lambda ins: chain.link(dve, ins)
                sig = lambda ins, name: ins.then_inc(S[name][0], 1)

                def norm_mod(k):
                    sig(v.tensor_tensor(xn, xT[:], xT[:], ALU.mult), "squares")
                    if k == 0:
                        unit_done(dve, l, N_ADA - 1)
                        wait(dve, "vec_stored", l, 1)
                        link(v.tensor_tensor(mod[:].rearrange("p s b g -> p (s b) g"),
                                             ps[:, 7, 0:96].rearrange("p (s g) -> p s g", g=NG),
                                             lvec[:, 0:48].unsqueeze(2).broadcast_to([P, 48, NG]), ALU.add))
                        for i, (s_, r_) in enumerate(((1, R_N1), (4, R_N2))):
                            ins = v.scalar_tensor_tensor(gain[:, i], mod[:, s_], 1.0,
                                                         lvec[:, r_:r_ + 8].unsqueeze(2).broadcast_to([P, KB, NG]), ALU.add, ALU.mult)
                            if i == 0:
                                link(ins)
                            else:
                                sig(ins, "mod_done")
                                wait(dve, "mod_done", l, 1)
                    wait(dve, "rstd_done", l, k + 1)
                    link(v.tensor_tensor(xn, xT[:], rstd[:].unsqueeze(1).broadcast_to([P, KB, TT]), ALU.mult))
                    for b in range(KB):
                        for g in range(NG):
                            t = slice(g * T, (g + 1) * T)
                            ins = v.tensor_scalar(hT[:, b, t], xn[:, b, t], gain[:, k, b, g:g + 1],
                                                  mod[:, 3 * k, b, g:g + 1], ALU.mult, ALU.add)
                        sig(ins, "h_ready")

                norm_mod(0)

                wait(dve, "u_copied", l, 2)
                v.tensor_tensor(cqn, u2(U_Q), u2(U_Q), ALU.mult)
                sig(v.tensor_tensor(rsq[:, 0:TT], U[:, U_KV, 0:TT], U[:, U_KV, 0:TT], ALU.mult), "lat_sq")
                wait(dve, "hg_exp", l, 1)
                flat = lambda x: x.rearrange("p n t -> p (n t)")
                link(v.tensor_scalar(lf, lf, 1.0, None, ALU.add))
                link(v.reciprocal(lf, lf))
                for d in range(2):
                    for q in range(HP):
                        n = 2 * (d * HP + q)
                        link(v.tensor_scalar(Qt[:, n:n + 2, :], lf[:, n:n + 2, :], oml[:, l, d, q:q + 1], lb[:, l, d, q:q + 1],
                                             ALU.mult, ALU.add))
                v.tensor_scalar(kk[:, 0:4, :], Qt[:, 0:4, :], -1.0, 1.0, ALU.mult, ALU.add)
                sig(v.tensor_scalar(kk[:, 4:8, ::-1], Qt[:, 4:8, :], -1.0, 1.0, ALU.mult, ALU.add), "hg_f")
                link(v.tensor_scalar(Gc[:], Gc[:], 1.0, None, ALU.add))
                link(v.reciprocal(Gc[:], Gc[:]))
                wait(dve, "lat_rstd", l, 1)
                q4 = U[:, U_HQ, :].rearrange("p (n t) -> p n t", t=T)
                v.tensor_tensor(qs[:, 0:4, :], q4, Gc[:, 0:4, :], ALU.mult)
                v.tensor_tensor(qs[:, 4:8, ::-1], q4, Gc[:, 0:4, :], ALU.mult)
                v.tensor_tensor(gs[:], U[:, U_HG, :], flat(Gc[:, 4:8, :]), ALU.mult)
                rq = rsq[:, 0:TT]
                link(v.tensor_tensor(cqn, u2(U_Q), rq.unsqueeze(1).broadcast_to([P, 2, TT]), ALU.mult))
                for b in range(2):
                    ins = v.tensor_scalar(cqn[:, b, :], cqn[:, b, :], lvec[:, R_QN + b:R_QN + b + 1], None, ALU.mult)
                sig(ins, "cqn_ready")
                sig(v.scalar_tensor_tensor(ckvT[:, 0:2, :].rearrange("p n t -> p (n t)"), U[:, U_KV, 0:TT],
                                           lvec[:, R_KVN:R_KVN + 1], rsq[:, TT:2 * TT], ALU.mult, ALU.mult), "kvn_ready")
                wait(dve, "srot_done", l, 1)
                raw = U[:, U_SQ:U_SK + 1, :].rearrange("p i t -> p (i t)").rearrange("p (b t) -> p b t", t=TT)[:, 0:3, T:TT]
                rot = prP[:, 0:3, :]
                bc3 = lambda x: x.unsqueeze(1).broadcast_to([x.shape[0], 3, T])
                v.tensor_tensor(rot, ps[:, 5, 0:3 * T].rearrange("p (b t) -> p b t", b=3), bc3(C["sin_s"]), ALU.mult)
                link(v.tensor_tensor(raw, raw, bc3(C["cos_s"]), ALU.mult))
                sig(v.tensor_tensor(raw, raw, rot, ALU.add), "srot_used")
                wait(dve, "hg_ln", l, 1)
                for n in range(8):
                    ins = v.tensor_tensor_scan(Gc[:, n, :], C["ones"], lf[:, n, :], 0.0, ALU.mult, ALU.add)
                link(ins)
                NR = NOPE + ROPE
                wait(dve, "krot_done", l, 1)
                wait(dve, "mv_copied", l, 1)
                link(v.tensor_tensor(prS[0:NR, 0, 0:T], ps[0:NR, 3, 256:384], C["sin_m"][0:NR], ALU.mult))
                link(v.tensor_tensor(krT[:, 1, :], krT[:, 1, :], C["cos_m"][0:NR], ALU.mult))
                sig(v.tensor_tensor(krT[:, 1, :], krT[:, 1, :], prS[0:NR, 0, 0:T], ALU.add), "krot_used")
                wait(dve, "krot_used", l, 1)
                sig(v.tensor_copy(kT[NOPE:].rearrange("p h n t -> p h (n t)"),
                                  krT[NOPE:].rearrange("p n t -> p (n t)").unsqueeze(1).broadcast_to([ROPE, MH, 3 * T])), "kr_ready")
                wait(dve, "qrot_done", l, 1)
                qv = qT[:, :, T:TT]
                bc4 = lambda x: x.unsqueeze(1).broadcast_to([NR, MH, T])
                rt = prS[0:NR, :, 0:T]
                v.tensor_tensor(rt, ps[0:NR, 6, :].rearrange("p (h t) -> p h t", h=MH), bc4(C["sin_m"][0:NR]), ALU.mult)
                link(v.tensor_tensor(qv, qv, bc4(C["cos_m"][0:NR]), ALU.mult))
                sig(v.tensor_tensor(qv, qv, rt, ALU.add), "qrot_used")

                def softmax_max(n, scale):
                    wait(dve, "scores", l, n + 1)
                    if n == 1:
                        wait(dve, "exps", l, 1)
                    v.tensor_reduce(mx[:, 0:4], ps[:, 2:4, :].rearrange("p b (c t) -> p (b c) t", c=2), AX_X, ALU.max)
                    link(v.tensor_reduce(mx[:, 4:8].rearrange("p (b c) -> p b c", b=2),
                                         ps[:, 4:6, 0:TT].rearrange("p b (c t) -> p b c t", c=2), AX_X, ALU.max))
                    if n == 0:
                        link(v.tensor_scalar(mx[:], mx[:], scale, None, ALU.mult))
                        m2 = mx[:].rearrange("p (g h) -> p g h", g=2)
                        sk = sink[:].unsqueeze(1).broadcast_to([P, 2, SH])
                        link(v.tensor_tensor(m2, m2, sk, ALU.max))
                        link(v.tensor_scalar(negm[:], mx[:], -1.0, None, ALU.mult))
                        sig(v.tensor_tensor(m2, sk, m2, ALU.subtract), "negmax")
                    else:
                        sig(v.tensor_scalar(negm[:], mx[:], -scale, None, ALU.mult), "negmax")

                def softmax_div(n):
                    wait(dve, "exps", l, n + 1)
                    if n == 0:
                        link(v.tensor_tensor(den[:], den[:], esk[:], ALU.add))
                    link(v.reciprocal(den[:], den[:]))
                    v.tensor_tensor(prS[:], prS[:], den[:, 0:4].unsqueeze(2).broadcast_to([P, 4, 2 * T]), ALU.mult)
                    sig(v.tensor_tensor(prP[:], prP[:], den[:, 4:8].unsqueeze(2).broadcast_to([P, 4, T]), ALU.mult), "probs")

                softmax_max(0, SWA_SCALE)
                Gb = Gc[:].rearrange("p n (j t) -> p n j t", t=CK)
                mid = CK // 2 - 1
                Qf = Qt[:].rearrange("p n (j t) -> p (n j) t", t=CK)
                ref = Gc[:].rearrange("p n (j t) -> p (n j) t", t=CK)[:, :, mid:mid + 1]
                v.tensor_tensor(Qf, Gc[:].rearrange("p n (j t) -> p (n j) t", t=CK), ref.broadcast_to([P, 8 * NCK, CK]), ALU.subtract)
                for j in range(NCK):
                    w = (j + 1) * CK
                    v.tensor_tensor(Kt[:, j, :, 0:w], Gb[:, :, j, mid:mid + 1].broadcast_to([P, 8, w]), Gc[:, :, 0:w], ALU.subtract)
                gP = Gc[:].rearrange("p (n g) t -> p n g t", g=NG)
                v.tensor_tensor(KD[:], gP[:, :, 0, T - 1:T].broadcast_to([P, 4, T]), gP[:, :, 0, :], ALU.subtract)
                sig(v.tensor_copy(QD[:], gP[:, :, 1, :]), "diffs")
                softmax_div(0)
                softmax_max(1, MLA_SCALE)
                softmax_div(1)
                wait(dve, "decays", l, 1)
                for j in range(NCK):
                    w = (j + 1) * CK
                    v.tensor_tensor(Kt[:, j, :, 0:w], Kt[:, j, :, 0:w], kk[:, :, 0:w], ALU.mult)
                v.tensor_tensor(Qt[:], Qt[:], qs[:], ALU.mult)
                kP = kk[:].rearrange("p (n g) t -> p n g t", g=NG)
                qP = qs[:].rearrange("p (n g) t -> p n g t", g=NG)
                v.tensor_tensor(KD[:], KD[:], kP[:, :, 0, :], ALU.mult)
                sig(v.tensor_tensor(QD[:], QD[:], qP[:, :, 1, :], ALU.mult), "recur_ready")
                wait(dve, "at_done", l, 1)
                wait(dve, "attn_zeroed", l, 1)
                msk = C["causal"].bitcast(I32).unsqueeze(1).broadcast_to([P, 4, T])
                for i in range(4):
                    ins = v.copy_predicated(AT[:, 4 * i:4 * i + 4, :], msk, B(4 + i).rearrange("p (n t) -> p n t", n=4))
                sig(ins, "at_masked")
                wait(dve, "of_done", l, 2)
                wait(dve, "of_copied", l, 1)
                for r in range(2):
                    h = slice(64 * r, 64 * r + 64)
                    link(v.tensor_tensor(KD[h], ps[h, 2 + r, :].rearrange("p (n t) -> p n t", t=T)[:, :, ::-1],
                                         prS[h, 0:2, :].rearrange("p b (c t) -> p (b c) t", c=2), ALU.add))
                sig(v.tensor_tensor(Qt[:, 0:4, :], KD[:], KD[:], ALU.mult), "o_sq")
                link(v.tensor_tensor(gs[:], gs[:], flat(KD[:]), ALU.mult))
                wait(dve, "o_rstd", l, 1)
                sig(v.scalar_tensor_tensor(OT[:, 2:4, :].rearrange("p b t -> p (b t)"), gs[:], lvec[:, R_HGN:R_HGN + 1], rsq[:],
                                           ALU.mult, ALU.mult), "o_ready")

                for j in range(N_OUT):
                    unit_done(dve, l, U_OUT + j)
                    for h in range(2):
                        b = 2 * j + h
                        for g in range(NG):
                            t = slice(g * T, (g + 1) * T)
                            ins = v.scalar_tensor_tensor(xT[:, b, t], ps[:, j, h * TT + g * T:h * TT + (g + 1) * T],
                                                         mod[:, 2, b, g:g + 1], xT[:, b, t], ALU.mult, ALU.add)
                    sig(ins, "mix_added")
                wait(dve, "mix_added", l, N_OUT)
                norm_mod(1)

                wait(dve, "route_exp", l, 1)
                link(v.tensor_scalar(sg[:], sg[:], 1.0, None, ALU.add))
                link(v.reciprocal(sg[:], sg[:]))
                link(v.tensor_tensor(sbs[:], sg[:], brt[:].unsqueeze(1).broadcast_to([P, NG, NE]), ALU.add))
                for g in range(NG):
                    link(v.max(top8[:, g, :], sbs[:, g, :]))
                for g in range(NG):
                    th = top8[:, g, TOPK - 1:TOPK]
                    link(v.tensor_scalar(sel[:, g, :], sbs[:, g, :], th, None, ALU.is_gt))
                    link(v.tensor_reduce(cnt[:, g, 0:1], sel[:, g, :], AX_X, ALU.add))
                    link(v.tensor_scalar(cnt[:, g, 1:2], cnt[:, g, 0:1], -1.0, float(TOPK), ALU.mult, ALU.add))
                    link(v.tensor_scalar(eqm[:, g, :], sbs[:, g, :], th, None, ALU.is_equal))
                    link(v.tensor_tensor_scan(cum[:, g, :], C["ones"][:, 0:NE], eqm[:, g, :], 0.0, ALU.mult, ALU.add))
                    link(v.scalar_tensor_tensor(eqm[:, g, :], cum[:, g, :], cnt[:, g, 1:2], eqm[:, g, :], ALU.is_le, ALU.mult))
                link(v.tensor_tensor(sel[:], sel[:], eqm[:], ALU.add))
                link(v.tensor_tensor(sel[:], sel[:], sg[:], ALU.mult))
                link(v.tensor_reduce(cnt[:, :, 0], sel[:], AX_X, ALU.add))
                link(v.reciprocal(cnt[:, :, 1], cnt[:, :, 0]))
                for g in range(NG):
                    ins = v.tensor_scalar(sel[:, g, :], sel[:, g, :], ROUTE_SCALE, cnt[:, g, 1:2], ALU.mult, ALU.mult)
                sig(ins, "gates_ready")

                def act_mul(k, it, step, routed):
                    dve.wait_ge(S["e_done"][0], l * (NE + 1) + k + 1 + it * step)
                    lk = lambda ins, i: (ins.then_inc(moe_dve, 1),
                                         dve.wait_ge(moe_dve, l * (4 * (NE + 1)) + 4 * k + i + it * step * 4))
                    lk(v.tensor_scalar(tmp_h, eg, 1.0, None, ALU.add), 1)
                    lk(v.reciprocal(tmp_h, tmp_h), 2)
                    lk(v.tensor_tensor(tmp_h, B(4), tmp_h, ALU.mult), 3)
                    unit_done(dve, l, U_SH + 3 * k + 1, it * step)
                    if routed:
                        lk(v.tensor_tensor(tmp_h, B(5), tmp_h, ALU.mult), 4)
                        dve.wait_ge(S["b_done"][0], l * NE + k + it * step)
                        unit_done(dve, l, U_SH + 3 * (k - 2) + 2, it * step)
                        v.tensor_tensor(hid[:, k % 2, :].rearrange("p (f t) -> p f t", f=2),
                                        tmp_h.rearrange("p (f t) -> p f t", f=2),
                                        ps[:, 6, 0:TT].unsqueeze(1).broadcast_to([P, 2, TT]), ALU.mult)\
                            .then_inc(S["hid_done"][0], 1)
                    else:
                        lk(v.tensor_copy(tmp_c, B(5)), 4)
                        v.tensor_tensor(hid[:, 0, :], tmp_c, tmp_h, ALU.mult).then_inc(S["hid_done"][0], 1)

                act_mul(0, 0, 0, False)
                wait(dve, "gates_stored", l, 1)
                with dve.Fori(0, E_ITERS, 1) as it:
                    for e in range(EB):
                        v.tensor_scalar(gsel[:, e % 2, :], gateT, ident[0:NE, bass.ds(it * EB + e, 1)], None, ALU.mult)\
                            .then_inc(S["b_sel"][0], 1)
                        act_mul(e + 1, it, EB, True)
                unit_done(dve, l, N_USED - 1)
                for b in range(KB):
                    for g in range(NG):
                        t = slice(g * T, (g + 1) * T)
                        ins = v.scalar_tensor_tensor(xT[:, b, t], ps[:, b // 2, (b % 2) * TT + g * T:(b % 2) * TT + (g + 1) * T],
                                                     mod[:, 5, b, g:g + 1], xT[:, b, t], ALU.mult, ALU.add)
                sig(ins, "moe_added")
                wait(dve, "moe_added", l, 1)
            assert chain.k == chain.n, ("DVE_LINKS", chain.k)

            v.tensor_tensor(xn, xT[:], xT[:], ALU.mult).then_inc(fin_sq, 1)
            dve.wait_ge(fin_rstd, 1)
            link0(v.tensor_tensor(xn, xT[:], rstd[:].unsqueeze(1).broadcast_to([P, KB, TT]), ALU.mult))
            for b in range(KB):
                ins = v.tensor_scalar(hT[:, b, :], xn[:, b, :], gvec[:, R_FG + b:R_FG + b + 1], None, ALU.mult)
            ins.then_inc(fin_y, 1)


_INS = ["x_prompt", "x_sample", "c", "cache_mla_ckv", "cache_mla_krope", "cache_swa_k", "cache_swa_v", "state_hgrn",
        "c_ctx", "w_ada", "b_ada", "norm1_g", "norm2_g", "w_in", "mla_q_norm_g", "mla_w_q_up", "mla_kv_norm_g",
        "mla_w_kv_up", "hg_lb_logits", "hg_norm_g", "fn_w", "swa_sink", "w_out", "moe_w_router", "moe_b_router",
        "moe_w_gate", "moe_w_up", "moe_w_down", "sh_w_gate", "sh_w_up", "sh_w_down", "final_norm_g"]
_OUTS = [("y_p", (1, T, D)), ("y_s", (1, T, D)), ("ckv", (1, DEPTH, T, KVL)), ("kr", (1, DEPTH, T, ROPE)),
         ("k", (1, DEPTH, T, SKV, SD)), ("v", (1, DEPTH, T, SKV, SD)), ("st", (1, DEPTH, 2, HH, HD, HD))]


def kernel(**inputs):
    import concourse.bacc as _bacc
    from concourse.bass_utils import run_bass_kernel_spmd as _run

    nc = _bacc.Bacc("TRN2", target_bir_lowering=False, num_devices=1)
    arrays, a, out = {}, {}, {}
    for name in _INS:
        x = np.ascontiguousarray(inputs[name])
        arrays[f"in_{name}"] = x
        a[name] = nc.dram_tensor(f"in_{name}", x.shape, F32, kind="ExternalInput").ap()
    arrays["in_consts"] = constant_array()
    a["consts"] = nc.dram_tensor("in_consts", arrays["in_consts"].shape, F32, kind="ExternalInput").ap()
    for name, shape in _OUTS:
        out[name] = nc.dram_tensor(f"out_{name}", shape, F32, kind="ExternalOutput").ap()
    build(nc, a, out)
    r = _run(nc, [arrays], core_ids=[0])
    return tuple(r.results[0][f"out_{name}"] for name, _ in _OUTS)
```

```python
from contextlib import ExitStack

import numpy as np
import concourse.bass as bass
from concourse import mybir

F32 = mybir.dt.float32
I32 = mybir.dt.int32
ALU = mybir.AluOpType
ACT = mybir.ActivationFunctionType
AX_X = mybir.AxisListType.X

P = 128
D = 1024
KB = D // P
DEPTH = 2
T = 128
NG = 2
TT = NG * T
EPS = 1e-6
GRID_W = 64
ROPE_BASE = 10000.0

MH, NOPE, ROPE, MV, QL, KVL = 4, 64, 32, 64, 256, 128
HH, HD = 4, 64
HP = HH // 2
SH, SKV, SD = 4, 2, 64
FNW, FNG = 256, 4
NE, TOPK, DE = 64, 6, 256
ROUTE_SCALE = 2.5
CK = 32
NCK = T // CK
MLA_SCALE = float(NOPE + ROPE) ** -0.5
SWA_SCALE = float(SD) ** -0.5

C_Q, C_KV = 0, QL
C_HQ = QL + KVL + ROPE
C_ZF, C_ZB, C_I, C_G = (C_HQ + n * 256 for n in range(1, 5))
C_FN = C_G + 256
C_SQ = C_FN + FNW
C_SK = C_SQ + SH * SD
IN_COLS = C_SK + 2 * SKV * SD
IN_UNITS = [(C_Q, 256), (C_KV, KVL + ROPE), (C_HQ, 256), (C_ZF, 256), (C_ZB, 256), (C_I, 256),
            (C_G, 256), (C_FN, 256), (C_SQ, 256), (C_SK, 256)]

UNIT = 2048
RING = 8
SECT = 4
SLOTS = 64
NPAIR = NE // 2
PB = 4
GE = 4
OVER = TT * TOPK // (SLOTS + 1)
NGRP = NE // GE
N_IN = len(IN_UNITS)
U_ADA1 = 0
U_IN = U_ADA1 + 2 * SECT
U_ADA2 = U_IN + N_IN
N_OUT = D // 256
U_OUT = U_ADA2 + 4 * SECT
U_SH = U_OUT + N_OUT
U_EX = U_SH + 3
N_LAYER = U_EX + 6 * NPAIR

R_BADA, R_N1, R_N2, R_QN, R_KVN, R_HGN = 0, 48, 56, 64, 66, 67
VROWS = 68
R_COND, R_LB, R_FG = 0, 16, 24
GROWS = 32

LOADS = 21
STORES = 8
ACT_LINKS = 6
DVE_LINKS = 52

CONSTS = {}


def constant_array():
    parts = []
    at = 0

    def add(name, a):
        nonlocal at
        full = np.zeros((P, a.shape[1]), np.float32)
        full[:a.shape[0]] = a
        CONSTS[name] = (at, a.shape[1])
        at += a.shape[1]
        parts.append(full)

    n = np.arange(P)
    add("ident", np.eye(P))
    add("flip", np.eye(P)[::-1])
    ang = 2 * np.pi * np.outer(n, n) / T
    add("dft", np.concatenate([np.cos(ang), np.sin(ang)], axis=1))
    w = FNW // FNG
    ang = 2 * np.pi * np.outer(np.arange(w), np.arange(w)) / w
    s = 1.0 / np.sqrt(T * w)
    add("fcos", np.kron(np.eye(2), np.cos(ang)) * s)
    add("fsin", np.kron(np.eye(2), np.sin(ang)) * -s)

    def pair_swap(size, lo):
        m = np.zeros((size, size))
        for i in range(lo, size, 2):
            m[i + 1, i] = -1.0
            m[i, i + 1] = 1.0
        return m

    def tables(dim):
        nf = dim // 4
        inv = ROPE_BASE ** (-np.arange(nf, dtype=np.float32) / np.float32(nf))
        pos = np.stack([n // GRID_W, n % GRID_W]).astype(np.float32)
        a = pos[:, None, :] * inv[None, :, None]
        a = np.repeat(a.reshape(2 * nf, T), 2, axis=0)
        return np.cos(a), np.sin(a)

    add("swap_s", pair_swap(P, 0))
    add("swap_m", pair_swap(NOPE + ROPE, NOPE))
    cs, sn = tables(SD)
    add("cos_s", np.tile(cs, (2, 1)))
    add("sin_s", np.tile(sn, (2, 1)))
    cs, sn = tables(ROPE)
    add("cos_m", np.concatenate([np.ones((NOPE, T)), cs]))
    add("sin_m", np.concatenate([np.zeros((NOPE, T)), sn]))
    add("causal", (n[:, None] <= n[None, :]).astype(np.float32))
    add("mean_d", np.full((P, P), 1.0 / D))
    add("mean_q", np.full((P, P), 1.0 / QL))
    add("mean_kv", np.full((P, P), 1.0 / KVL))
    add("mean_h", np.kron(np.eye(2), np.full((HD, HD), 1.0 / HD)))
    add("ones", np.ones((P, P)))
    add("before", (n[:, None] < n[None, :]).astype(np.float32))
    add("slots", np.tile(np.arange(SLOTS), (P, 1)))
    add("experts", np.tile(np.arange(NE), (P, 1)))
    add("place", np.arange(1, P + 1)[:, None])
    return np.ascontiguousarray(np.concatenate(parts, axis=1))


constant_array()
CONST_W = sum(w for _, w in CONSTS.values())


def build(nc, a, out):
    ctx = ExitStack()
    with ctx:
        def sb(name, shape, dt=F32):
            return ctx.enter_context(nc.sbuf_tensor(name, shape, dt))

        def sem(name):
            return ctx.enter_context(nc.semaphore(name))

        ring = sb("ring", [P, RING, UNIT])
        F32R = mybir.dt.float32r
        cst = sb("cst", [P, CONST_W])
        C = {k: cst[:, at:at + w] for k, (at, w) in CONSTS.items()}
        ident = C["ident"]
        xT = sb("xT", [P, KB, TT])
        HX = sb("HX", [P, 2 * KB * TT])
        hx = HX[:].rearrange("p (i b t) -> p i b t", i=2, b=KB)
        hT = hx[:, 0]
        xn = hx[:, 1]
        xrow = HX[:, KB * TT:]
        Kt = HX[:].rearrange("p (j n t) -> p j n t", j=NCK, n=8)
        rstd = sb("rstd", [P, TT])
        lnv = sb("lnv", [P, TT])
        gvec_rows = sb("gvec_rows", [GROWS, P])
        gvec = sb("gvec", [P, GROWS])
        lvec_rows = sb("lvec_rows", [VROWS, P])
        lvec = sb("lvec", [P, VROWS])
        scond = sb("scond", [P, KB, 32])
        stmp = sb("stmp", [P, 64])
        lb = sb("lb", [P, DEPTH, 2, HP])
        oml = sb("oml", [P, DEPTH, 2, HP])
        mod = sb("mod", [P, 6, KB, NG])
        gain = sb("gain", [P, 2, KB, NG])
        epsc = sb("epsc", [P, 1])
        wq = sb("wq", [P, 2, MH * (NOPE + ROPE)])
        wkv = sb("wkv", [P, MH, NOPE + MV])
        fnw = sb("fnw", [P, 2, FNW])
        wr = sb("wr", [P, KB, NE])
        brt = sb("brt", [P, NE])
        sink = sb("sink", [P, SH])
        kcache = sb("kcache", [P, 3, P])
        vcache = sb("vcache", [P, P])
        s0 = sb("s0", [P, 2, HP, HD])
        sg = sb("sg", [P, NG, NE])
        sbs = sb("sbs", [P, NG, NE])
        top8 = sb("top8", [P, NG, 8])
        sel = sb("sel", [P, NG, NE])
        eqm = sb("eqm", [P, NG, NE])
        cum = sb("cum", [P, NG, NE])
        cnt = sb("cnt", [P, NG, 2])
        counts = sb("counts", [P, 2])
        rank = sb("rank", [P, NG, NE + 2 * GE])
        gatew = sb("gatew", [P, NG, NE + 2 * GE])
        gslot = sb("gslot", [P, 1])
        o_ckv = sb("o_ckv", [P, KVL])
        o_kr = sb("o_kr", [P, ROPE])
        o_st = sb("o_st", [P, 2 * HP * HD])

        mixers = ctx.enter_context(ExitStack())

        def sb_all(name, shape, dt=F32):
            return ctx.enter_context(nc.sbuf_tensor(name, shape, dt))

        def sb(name, shape, dt=F32):
            return mixers.enter_context(nc.sbuf_tensor(name, shape, dt))

        U = sb("U", [P, 11, 512])
        u2 = lambda i: U[:, i, :].rearrange("p (b t) -> p b t", b=2)
        U_Q, U_KV, U_HQ, U_ZF, U_ZB, U_I, U_HG, U_FN, U_SQ, U_SK, U_SKV = range(11)
        OT = sb("OT", [P, 8, TT])
        cqn = OT[:, 0:2, :]
        ckvT = sb("ckvT", [P, 3, T])
        krT = sb("krT", [NOPE + ROPE, 3, T])
        qT = sb("qT", [NOPE + ROPE, MH, TT])
        kT = sb("kT", [NOPE + ROPE, MH, 3, T])
        vM = sb("vM", [P, 3, MH * MV])
        rsq = sb("rsq", [P, 512])
        kcT = sb("kcT", [P, T])
        prS = sb("prS", [P, 4, 2 * T])
        prP = sb("prP", [P, 4, T])
        pT = sb("pT", [P, 12, T])
        mx = sb("mx", [P, 8])
        negm = sb("negm", [P, 8])
        den = sb("den", [P, 8])
        esk = sb("esk", [P, 8])
        qs = sb("qs", [P, 8, T])
        kk = sb("kk", [P, 8, T])
        lf = U[:, U_ZF:U_ZB + 1, :].rearrange("p i (n t) -> p (i n) t", t=T)
        Gc = sb("Gc", [P, 8, T])
        Qt = sb("Qt", [P, 8, T])
        QD = sb("QD", [P, 4, T])
        KD = sb("KD", [P, 4, T])
        KDt = prP
        Vh = sb("Vh", [P, 2, NG, 256])
        AT = U[:, U_HQ:U_I + 1, :].rearrange("p i (n t) -> p (i n) t", t=T)
        gs = sb("gs", [P, 512])
        F1 = pT[:, 0:8, :].rearrange("p (c h g) t -> p c h g t", c=2, h=2)
        F2 = pT[:, 8:12, :].rearrange("p (b g) t -> p b (g t)", b=2)
        modrows = pT[:].rearrange("p (k c) t -> p k (c t)", k=3)
        mixers.close()
        moe = ctx.enter_context(ExitStack())

        def sb(name, shape, dt=F32):
            return moe.enter_context(nc.sbuf_tensor(name, shape, dt))

        h_hi = sb("h_hi", [P, NG, D], F32R)
        h_lo = sb("h_lo", [P, NG, D], F32R)
        sel01 = sb("sel01", [P, 2, NG, GE * SLOTS], F32R)
        selw = sb("selw", [P, 2, NG, GE * SLOTS])
        hslots = sb("hslots", [P, 2, KB, GE * SLOTS])
        slotT = sb("slotT", [P, TT], F32R)
        silu_g = sb("silu_g", [P, 512])
        hid = sb("hid", [P, 512])
        hidT = sb("hidT", [P, 2, P])
        y_hi = sb("y_hi", [P, D], F32R)
        y_lo = sb("y_lo", [P, D], F32R)
        over_w = sb("over_w", [P, 6, 1024])
        over_hT = sb("over_hT", [P, 2, TT])
        over_gate = sb("over_gate", [P, NG, NE])
        over_s = sb("over_s", [P, 3, NE])
        over_diag = sb("over_diag", [P, P])
        over_at = sb("over_at", [P, 1])
        over_list = sb("over_list", [P, OVER + 1], I32)

        ps = ctx.enter_context(nc.psum_tensor("ps", [P, 8, 512], F32))
        B = lambda i: ps[:, i, :]

        slot_full = [sem(f"slot_full{i}") for i in range(RING)]
        unit_used = sem("unit_used")
        S = {}
        sel_built = sem("sel_built")
        S = {}

        def declare(**per_layer):
            for name, n in per_layer.items():
                S[name] = (sem(name), n)

        def wait(eng, name, l, k):
            s, n = S[name]
            assert 0 <= k <= n, name
            if l * n + k > 0:
                eng.wait_ge(s, l * n + k)

        class Chain:

            def __init__(self, name, per_layer):
                self.s, self.n, self.k, self.l = sem(name), per_layer, 0, 0

            def layer(self, l):
                assert self.k in (0, self.n), (self.k, self.n)
                self.l, self.k = l, 0

            def link(self, eng, ins):
                self.k += 1
                ins.then_inc(self.s, 1)
                eng.wait_ge(self.s, self.l * self.n + self.k)

        glob_in, layer_in = sem("glob_in"), sem("layer_in")
        out_sem, y_out = sem("out_sem"), sem("y_out")
        x_turned, x_stored, cond_turned, cond_ready, g_turned, g_stored = (
            sem(n) for n in ("x_turned", "x_stored", "cond_turned", "cond_ready", "g_turned", "g_stored"))
        setup_dve, setup_act, consts_set = sem("setup_dve"), sem("setup_act"), sem("consts_set")
        fin_sq, fin_mean, fin_rstd, fin_y, fin_turned, fin_copied = (
            sem(n) for n in ("fin_sq", "fin_mean", "fin_rstd", "fin_y", "fin_turned", "fin_copied"))
        declare(vec_turned=1, vec_stored=1, mod_done=1,
                squares=2, mean_done=2, rstd_done=2, h_ready=2 * KB,
                u_copied=11, cache_turned=1, cache_copied=1,
                lat_sq=1, lat_mean=1, lat_rstd=1, cqn_ready=1, kvn_ready=1,
                hg_exp=1, hg_f=1, hg_ln=1,
                flip_done=1, flip_copied=1, srot_done=1, srot_used=1,
                fn1_done=1, fn1_copied=1, fn2_done=1, fn2_copied=1, fn3_done=1, fn3_copied=1,
                mq_done=1, mq_copied=1, mv_done=1, mv_copied=1, krot_done=1, krot_used=1,
                kv_turned=1, kvout_copied=1,
                mk_done=1, mk_copied=1, qrot_done=1, qrot_used=1, kr_ready=1,
                scores=2, negmax=2, exps=2, probs=2, p_turned=2, p_copied=2, pv_done=2, pv_copied=2,
                kr_zeroed=1, keys_zeroed=1, attn_zeroed=1, diffs=1, decays=1, recur_ready=1, kd_turned=1, kd_copied=1, st_done=1, st_copied=1,
                at_done=1, at_masked=1, of_done=2, of_copied=1, o_sq=1, o_mean=1, o_rstd=1, o_ready=1,
                mix_added=N_OUT,
                rows_copied=3, rows_turned=3, mod_rest=1,
                route_done=1, route_exp=1, mask_ready=1, ranks_done=1, gates_ready=1,
                h_turned=1, hhi_done=1, h_split=1, ssilu=1, shid=1,
                sel_ready=NGRP + 2, gathered=4 + 2 * NPAIR, gather_copied=4 + 2 * NPAIR,
                silu_done=NPAIR, hid_ready=NPAIR, turned=NPAIR, hidT_copied=NPAIR, slotT_ready=NPAIR + 1,
                yhi_done=NPAIR, y_ready=NPAIR + 1, scattered=NPAIR + 1, moe_added=1,
                over_marked=1, sums_done=1, over_counted=2, over_listed=1)
        V = [{name: sem(f"{name}{l}") for name in ("over_full", "over_up", "over_silu", "over_hid", "over_turned",
                                                   "over_copied", "over_down")} for l in range(DEPTH)]

        def over_visits(eng, l, visit):
            wait(eng, "over_listed", l, 1)
            n = eng.value_load(over_list[0:1, OVER:OVER + 1], min_val=0, max_val=OVER)
            with eng.If(n > 0):
                with eng.Fori(0, OVER, 1) as k:
                    with eng.If(n > k):
                        visit(k)

        def unit_full(eng, l, n, more=0):
            n += l * N_LAYER
            eng.wait_ge(slot_full[n % RING], (n // RING + 1) * 32 + more)

        def slot(l, n):
            return ring[:, (l * N_LAYER + n) % RING, :]

        def unit_done(eng, l, n, more=0):
            eng.wait_ge(unit_used, l * N_LAYER + n + 1 + more)

        block = ctx.enter_context(nc.Block())

        @block.sync
        def _(sp):
            w_in_v = a["w_in"].rearrange("l (b p) n -> l p b n", p=P)
            w_ada_v = a["w_ada"].rearrange("l (b p) n -> l p b n", p=P)
            w_out_v = a["w_out"].rearrange("l (b p) n -> l p b n", p=P)

            def load(l, n, parts, it=0):
                if l * N_LAYER + n >= RING:
                    sp.wait_ge(unit_used, l * N_LAYER + n - RING + 1 + it * 6 * PB)
                s = slot_full[(l * N_LAYER + n) % RING]
                for at, src in parts:
                    b, w = src.shape[1:]
                    dst = slot(l, n)[:, at:at + b * w].rearrange("p (b n) -> p b n", b=b)
                    sp.dma_start(dst, src).then_inc(s, 16)

            def halves(v, w):
                h = v.shape[1] // 2
                return [(0, v[:, 0:h]), (h * w, v[:, h:])]

            gate_v, up_v, down_v = (a[n].rearrange("l e (b p) n -> l e p b n", p=P)
                                    for n in ("moe_w_gate", "moe_w_up", "moe_w_down"))
            for l in range(DEPTH):
                def ada(n, j):
                    load(l, n, halves(w_ada_v[l, :, :, j * 256:(j + 1) * 256], 256))

                for j in range(2 * SECT):
                    ada(U_ADA1 + j, j)
                for j, (c0, w) in enumerate(IN_UNITS):
                    load(l, U_IN + j, halves(w_in_v[l, :, :, c0:c0 + w], w))
                for j in range(4 * SECT):
                    ada(U_ADA2 + j, 2 * SECT + j)
                for j in range(N_OUT):
                    load(l, U_OUT + j, halves(w_out_v[l, :, :, j * 256:(j + 1) * 256], 256))
                for j, name in enumerate(("sh_w_gate", "sh_w_up", "sh_w_down")):
                    v = a[name].rearrange("l (b p) n -> l p b n", p=P)[l]
                    load(l, U_SH + j, halves(v, v.shape[2]))
                with sp.Fori(0, NPAIR // PB, 1) as it:
                    for p in range(PB):
                        for h in range(2):
                            for e in range(2):
                                x = it * (2 * PB) + 2 * p + e
                                b = slice(4 * h, 4 * h + 4)
                                load(l, U_EX + 6 * p + 2 * h + e,
                                     [(0, gate_v[l, x, :, b]), (1024, up_v[l, x, :, b])], it)
                        for e in range(2):
                            load(l, U_EX + 6 * p + 4 + e, halves(down_v[l, it * (2 * PB) + 2 * p + e], D), it)

                def visit(k):
                    x = sp.value_load(over_list[0:1, bass.ds(k, 1)], min_val=0, max_val=NE - 1)
                    sp.wait_ge(V[l]["over_down"], k + 1)
                    for i, v_ in enumerate((gate_v, up_v)):
                        sp.dma_start(over_w[:, 2 * i:2 * i + 2].rearrange("p i (b n) -> p (i b) n", n=DE), v_[l, x])\
                            .then_inc(V[l]["over_full"], 16)
                    sp.dma_start(over_w[:, 4:6], down_v[l, x]).then_inc(V[l]["over_full"], 16)

                over_visits(sp, l, visit)

        @block.gpsimd
        def _(pool):
            pool.memset(epsc[:], EPS).then_inc(consts_set, 1)
            pool.memset(scond[:], 0.0).then_inc(consts_set, 1)
            pool.memset(rank[:], -1.0).then_inc(consts_set, 1)
            pool.memset(gatew[:], 0.0).then_inc(consts_set, 1)
            pool.memset(kcache[:], 0.0).then_inc(consts_set, 1)
            pool.dma_start(cst[:], a["consts"]).then_inc(glob_in, 16)
            pool.dma_start(gvec_rows[R_COND:R_COND + 8], a["c_ctx"].rearrange("(b p) -> b p", p=P)).then_inc(glob_in, 16)
            pool.dma_start(gvec_rows[R_COND + 8:R_COND + 16], a["c"].rearrange("o (b p) -> (o b) p", p=P)).then_inc(glob_in, 16)
            pool.dma_start(gvec_rows[R_LB:R_LB + 8], a["hg_lb_logits"].rearrange("r l (b p) -> (r l b) p", p=P)).then_inc(glob_in, 16)
            pool.dma_start(gvec_rows[R_FG:R_FG + 8], a["final_norm_g"].rearrange("(b p) -> b p", p=P)).then_inc(glob_in, 16)
            for g, name in enumerate(("x_prompt", "x_sample")):
                pool.dma_start(xrow[:, g * D:(g + 1) * D], a[name][0]).then_inc(glob_in, 16)
            pool.wait_ge(consts_set, 5)
            for l in range(DEPTH):
                wait(pool, "gates_ready", l, 0)
                rows = (("b_ada", R_BADA, 48), ("norm1_g", R_N1, 8), ("norm2_g", R_N2, 8),
                        ("mla_q_norm_g", R_QN, 2), ("mla_kv_norm_g", R_KVN, 1))
                loads = [(lvec_rows[r:r + n], a[name].rearrange("l (b p) -> l b p", p=P)[l]) for name, r, n in rows]
                hgn = a["hg_norm_g"].rearrange("l (o p) -> l o p", o=1)
                loads += [(lvec_rows[R_HGN:R_HGN + 1, r * HD:(r + 1) * HD], hgn[l]) for r in range(2)]
                loads += [
                    (wq[:], a["mla_w_q_up"].rearrange("l (b p) n -> l p b n", p=P)[l]),
                    (wkv[:].rearrange("p h n -> p (h n)"), a["mla_w_kv_up"][l]),
                    (fnw[:], a["fn_w"].rearrange("l (b p) n -> l p b n", p=P)[l]),
                    (wr[:], a["moe_w_router"].rearrange("l (b p) n -> l p b n", p=P)[l]),
                    (brt[:], a["moe_b_router"].rearrange("l (o n) -> l o n", o=1)[l].broadcast_to([P, NE])),
                    (sink[:], a["swa_sink"].rearrange("l (o n) -> l o n", o=1)[l].broadcast_to([P, SH])),
                    (kcache[:, 0, :], a["cache_swa_k"][0].rearrange("l t k d -> l t (k d)")[l]),
                    (kcache[:, 1, :], a["cache_mla_ckv"][0][l]),
                    (kcache[:, 2, NOPE:NOPE + ROPE], a["cache_mla_krope"][0][l]),
                    (vcache[:], a["cache_swa_v"][0].rearrange("l t k d -> l t (k d)")[l]),
                ]
                st = a["state_hgrn"][0].rearrange("l r (q s) d e -> l r q (s d) e", s=2)
                loads += [(s0[:, r, q, :], st[l, r, q]) for r in range(2) for q in range(HP)]
                assert len(loads) == LOADS
                for dst, src in loads:
                    pool.dma_start(dst, src).then_inc(layer_in, 16)
                wait(pool, "moe_added", l, 0)
                pool.memset(krT[0:NOPE], 0.0).then_inc(S["kr_zeroed"][0], 1)
                wait(pool, "u_copied", l, 11)
                for j in range(NCK - 1):
                    z = pool.memset(Kt[:, j, :, (j + 1) * CK:], 0.0)
                z.then_inc(S["keys_zeroed"][0], 1)
                kv = u2(U_SKV)[:, 0, :]
                for dst, src in ((out["k"], kv[:, 0:128]), (out["v"], kv[:, 128:256])):
                    pool.dma_start(dst[0].rearrange("l t k d -> l t (k d)")[l], src).then_inc(out_sem, 16)
                wait(pool, "kvout_copied", l, 1)
                pool.dma_start(out["ckv"][0][l], o_ckv[:]).then_inc(out_sem, 16)
                pool.dma_start(out["kr"][0][l], o_kr[:]).then_inc(out_sem, 16)
                wait(pool, "recur_ready", l, 1)
                pool.memset(AT, 0.0).then_inc(S["attn_zeroed"][0], 1)
                wait(pool, "st_copied", l, 1)
                sto = out["st"][0].rearrange("l r (q s) d e -> l r q (s d) e", s=2)
                for r in range(2):
                    for q in range(HP):
                        at = (r * HP + q) * HD
                        pool.dma_start(sto[l, r, q], o_st[:, at:at + HD]).then_inc(out_sem, 16)
            for g, name in enumerate(("y_p", "y_s")):
                pool.wait_ge(fin_copied, 4 * (g + 1))
                pool.dma_start(out[name][0], xrow[:, g * D:(g + 1) * D]).then_inc(y_out, 16)
            pool.wait_ge(y_out, 32)
            pool.wait_ge(out_sem, 16 * STORES * DEPTH)

        @block.tensor
        def _(pe):
            mm = nc.tensor.matmul

            def tr(o, i, n=P):
                return nc.tensor.transpose(o, i, ident[0:n, 0:n])

            def used(ins):
                ins.then_inc(unit_used, 1)

            pe.wait_ge(glob_in, 16 * 7)
            tr(ps[:, 0, 0:GROWS], gvec_rows[:], GROWS).then_inc(g_turned, 1)
            for b in range(KB):
                for g in range(NG):
                    t = tr(ps[:, 1 + b // 2, (b % 2) * TT + g * T:(b % 2) * TT + (g + 1) * T],
                           xrow[:, g * D + b * P:g * D + (b + 1) * P])
                if b % 2:
                    t.then_inc(x_turned, 1)
            pe.wait_ge(cond_ready, 1)

            for l in range(DEPTH):
                pe.wait_ge(layer_in, (l + 1) * 16 * LOADS)
                pe.wait_ge(x_stored, 4)
                pe.wait_ge(g_stored, 1)
                wait(pe, "moe_added", l, 0)
                tr(ps[:, 0, 0:VROWS], lvec_rows[:], VROWS).then_inc(S["vec_turned"][0], 1)
                for j in range(3):
                    c = tr(ps[0:(P if j < 2 else NOPE + ROPE), 1, j * P:(j + 1) * P],
                           kcache[:, j, 0:(P if j < 2 else NOPE + ROPE)])
                c.then_inc(S["cache_turned"][0], 1)

                def ada_rows(n0, bank, k):
                    for q in range(2):
                        ws = []
                        for c in range(SECT):
                            unit_full(pe, l, n0 + q * SECT + c)
                            ws.append(slot(l, n0 + q * SECT + c).rearrange("p (b n) -> p b n", b=KB))
                        for b in range(KB):
                            for c in range(SECT):
                                m = mm(ps[32 * c:32 * c + 32, bank, q * 256:(q + 1) * 256], scond[:, b, :], ws[c][:, b, :],
                                       start=(b == 0), stop=(b == KB - 1))
                                if b == KB - 1:
                                    used(m)
                    wait(pe, "rows_copied", l, k + 1)

                def ada_turn(bank, k):
                    for i in range(4):
                        m = tr(ps[:, bank, i * P:(i + 1) * P], modrows[:, k, i * P:(i + 1) * P])
                    m.then_inc(S["rows_turned"][0], 1)

                ada_rows(U_ADA1, 6, 0)
                ada_turn(7, 0)

                def mean_square(k):
                    wait(pe, "squares", l, k + 1)
                    bank = 0 if k == 0 else 4
                    if k == 0:
                        wait(pe, "vec_stored", l, 1)
                    for b in range(KB):
                        m = mm(ps[:, bank, 0:TT], C["mean_d"], xn[:, b, :], start=(b == 0), stop=(b == KB - 1))
                    m.then_inc(S["mean_done"][0], 1)

                mean_square(0)

                def in_unit(j):
                    unit_full(pe, l, U_IN + j)
                    w_ = IN_UNITS[j][1]
                    return slot(l, U_IN + j)[:, 0:KB * w_].rearrange("p (b n) -> p b n", b=KB)

                def into(i):
                    if i == 0:
                        wait(pe, "cache_copied", l, 1)
                    if i == 6:
                        wait(pe, "mod_done", l, 1)
                    if i == 7:
                        wait(pe, "rstd_done", l, 1)
                    if i >= 8:
                        wait(pe, "u_copied", l, i - 7)
                    return (i + 1) % 8

                def feature_major(i, lhs):
                    bank = into(i)
                    for h in range(2):
                        for b in range(KB):
                            if i == 0 and h == 0:
                                wait(pe, "h_ready", l, b + 1)
                            m = mm(ps[:, bank, h * TT:(h + 1) * TT], lhs(h, b), hT[:, b, :], start=(b == 0), stop=(b == KB - 1))
                    return m

                def token_major(i, w):
                    bank = into(i)
                    for g in range(NG):
                        for b in range(KB):
                            m = mm(ps[:, bank, g * 256:(g + 1) * 256], hT[:, b, g * T:(g + 1) * T], w[:, b, :],
                                   start=(b == 0), stop=(b == KB - 1))
                    return m

                for j in range(N_IN):
                    w = in_unit(j)
                    if j == 1:
                        bank = into(1)
                        for b in range(KB):
                            mm(ps[:, bank, 0:TT], w[:, b, 0:KVL], hT[:, b, :], start=(b == 0), stop=(b == KB - 1))
                        for b in range(KB):
                            m = mm(ps[NOPE:NOPE + ROPE, bank, TT:2 * TT], w[:, b, KVL:KVL + ROPE], hT[:, b, :],
                                   start=(b == 0), stop=(b == KB - 1))
                    elif j in (5, 7):
                        m = token_major(j, w)
                    elif j == 8:
                        bank = into(8)
                        for h in range(SH):
                            r, c = h // 2, h % 2
                            for b in range(KB):
                                m = mm(ps[64 * r:64 * r + 64, bank, c * TT:(c + 1) * TT], w[:, b, h * SD:(h + 1) * SD],
                                       hT[:, b, :], start=(b == 0), stop=(b == KB - 1))
                    elif j == 9:
                        bank = into(9)
                        for b in range(KB):
                            mm(ps[:, bank, 0:TT], w[:, b, 0:128], hT[:, b, :], start=(b == 0), stop=(b == KB - 1))
                        m = token_major(10, w)
                    else:
                        m = feature_major(j, lambda h, b, w=w: w[:, b, h * P:(h + 1) * P])
                    used(m)

                wait(pe, "lat_sq", l, 1)
                wait(pe, "u_copied", l, 11)
                for b in range(2):
                    mm(ps[:, 3, 0:TT], C["mean_q"], cqn[:, b, :], start=(b == 0), stop=(b == 1))
                mm(ps[:, 3, TT:2 * TT], C["mean_kv"], rsq[:, 0:TT], start=True, stop=True).then_inc(S["lat_mean"][0], 1)
                for k in (1, 2):
                    ada_rows(U_ADA2 + (k - 1) * 2 * SECT, 3 + k, k)
                    ada_turn(5 + k, k)
                wait(pe, "mod_rest", l, 1)
                mm(B(4), C["flip"], U[:, U_I, :], start=True, stop=True).then_inc(S["flip_done"][0], 1)
                srt = U[:, U_SQ:U_SK + 1, :].rearrange("p i t -> p (i t)").rearrange("p (b t) -> p b t", t=TT)[:, 0:3, T:TT]
                mm(ps[:, 5, 0:3 * T], C["swap_s"], srt, start=True, stop=True).then_inc(S["srot_done"][0], 1)
                for g in range(NG):
                    for cb in range(2):
                        m = mm(ps[:, 6 + g, cb * 256:(cb + 1) * 256], u2(U_FN)[:, g, cb * P:(cb + 1) * P], C["dft"],
                               start=True, stop=True)
                m.then_inc(S["fn1_done"][0], 1)
                wait(pe, "cqn_ready", l, 1)
                HQ = NOPE + ROPE
                for h in range(MH):
                    for b in range(2):
                        m = mm(ps[0:HQ, h // 2, (h % 2) * TT:(h % 2 + 1) * TT], wq[:, b, h * HQ:(h + 1) * HQ], cqn[:, b, :],
                               start=(b == 0), stop=(b == 1))
                m.then_inc(S["mq_done"][0], 1)
                wait(pe, "kvn_ready", l, 1)
                for n in range(3):
                    m = mm(ps[:, 2 + n // 2, (n % 2) * 256:(n % 2 + 1) * 256], ckvT[:, n, :], wkv[:, :, NOPE:],
                           start=True, stop=True)
                m.then_inc(S["mv_done"][0], 1)
                wait(pe, "kr_zeroed", l, 1)
                mm(ps[0:HQ, 3, 256:384], C["swap_m"][0:HQ, 0:HQ], krT[:, 1, :], start=True, stop=True)\
                    .then_inc(S["krot_done"][0], 1)
                wait(pe, "fn1_copied", l, 1)
                for cb in range(2):
                    for h, m_ in enumerate(("fcos", "fsin")):
                        m = mm(ps[:, 6, cb * TT:(cb + 1) * TT], C[m_], F1[:, cb, h].rearrange("p g t -> p (g t)"),
                               start=(h == 0), stop=(h == 1))
                m.then_inc(S["fn2_done"][0], 1)
                wait(pe, "flip_copied", l, 1)
                wait(pe, "srot_used", l, 1)
                wait(pe, "mq_copied", l, 1)
                for h, bank in enumerate((4, 5, 0, 1)):
                    m = mm(ps[0:NOPE, bank, 0:3 * T], wkv[:, h, 0:NOPE], ckvT[:].rearrange("p n t -> p (n t)"),
                           start=True, stop=True)
                m.then_inc(S["mk_done"][0], 1)
                wait(pe, "fn2_copied", l, 1)
                for ob in range(2):
                    for cb in range(2):
                        m = mm(ps[:, 7, ob * TT:(ob + 1) * TT], fnw[:, cb, ob * P:(ob + 1) * P], F2[:, cb, :],
                               start=(cb == 0), stop=(cb == 1))
                m.then_inc(S["fn3_done"][0], 1)
                mm(ps[0:HQ, 6, :].rearrange("p (h t) -> p h t", h=MH), C["swap_m"][0:HQ, 0:HQ], qT[:, :, T:TT], start=True, stop=True)\
                    .then_inc(S["qrot_done"][0], 1)
                wait(pe, "mk_copied", l, 1)
                tr(ps[:, 0, 0:P], ckvT[:, 0, :])
                tr(ps[:, 0, P:P + HQ], krT[:, 0, :], HQ).then_inc(S["kv_turned"][0], 1)

                def score(o, q, k):
                    return mm(o, q, k, start=True, stop=True)

                def transpose_probs(n):
                    wait(pe, "probs", l, n + 1)
                    if n == 0:
                        wait(pe, "qrot_used", l, 1)
                        wait(pe, "fn3_copied", l, 1)
                        wait(pe, "kvout_copied", l, 1)
                    wait(pe, "p_copied", l, n)
                    for h in range(4):
                        for c in range(3):
                            i = 3 * h + c
                            src = prS[:, h, c * T:(c + 1) * T] if c < 2 else prP[:, h, :]
                            m = tr(ps[:, (6 + i // 4) % 8, (i % 4) * T:(i % 4 + 1) * T], src)
                    m.then_inc(S["p_turned"][0], 1)

                def values(n, v):
                    wait(pe, "p_copied", l, n + 1)
                    if n == 0:
                        wait(pe, "mk_copied", l, 1)
                    wait(pe, "pv_copied", l, n)
                    for h in range(4):
                        r = (h % 2) * 64
                        o = ps[r:r + 64, 1, (h // 2) * TT:(h // 2 + 1) * TT]
                        mm(o[:, 0:T], v(h, 2), pT[:, 3 * h + 2, :], start=True, stop=True)
                        mm(o[:, T:TT], v(h, 0), pT[:, 3 * h, :], start=True, stop=False)
                        m = mm(o[:, T:TT], v(h, 1), pT[:, 3 * h + 1, :], start=False, stop=True)
                    m.then_inc(S["pv_done"][0], 1)

                wait(pe, "srot_used", l, 1)
                wait(pe, "mv_copied", l, 1)
                wait(pe, "krot_used", l, 1)
                for h in range(SH):
                    r, c = h // 2, h % 2
                    q = u2(U_SQ)[64 * r:64 * r + 64, c, :]
                    k = u2(U_SK)[64 * r:64 * r + 64, 0, :]
                    score(ps[:, 4 + r, c * T:(c + 1) * T], q[:, 0:T], k[:, 0:T])
                    score(ps[:, 2 + r, c * TT:c * TT + T], q[:, T:TT], k[:, T:TT])
                    m = score(ps[:, 2 + r, c * TT + T:(c + 1) * TT], q[:, T:TT], kcT[64 * r:64 * r + 64, :])
                m.then_inc(S["scores"][0], 1)
                transpose_probs(0)

                def swa_v(h, c):
                    k = h // 2
                    if c == 1:
                        return vcache[:, k * SD:(k + 1) * SD]
                    return u2(U_SKV)[:, 0 if c == 2 else 1, 128 + k * SD:128 + (k + 1) * SD]

                values(0, swa_v)
                wait(pe, "exps", l, 1)
                wait(pe, "kr_ready", l, 1)
                wait(pe, "qrot_used", l, 1)
                for h in range(MH):
                    r, c = h // 2, h % 2
                    score(ps[:, 4 + r, c * T:(c + 1) * T], qT[:, h, 0:T], kT[:, h, 0, :])
                    m = score(ps[:, 2 + r, c * TT:(c + 1) * TT], qT[:, h, T:TT], kT[:, h, 1:3, :].rearrange("p n t -> p (n t)"))
                m.then_inc(S["scores"][0], 1)
                transpose_probs(1)
                values(1, lambda h, c: vM[:, (1, 2, 0)[c], h * MV:(h + 1) * MV])

                wait(pe, "recur_ready", l, 1)
                wait(pe, "exps", l, 2)
                for n in range(4):
                    m = tr(ps[:, 2, n * P:(n + 1) * P], KD[:, n, :])
                m.then_inc(S["kd_turned"][0], 1)
                wait(pe, "p_copied", l, 2)
                wait(pe, "keys_zeroed", l, 1)
                for r in range(2):
                    for n in range(8):
                        for j in range(NCK):
                            m = mm(ps[:, 4 + 2 * r + n // 4, (n % 4) * T + j * CK:(n % 4) * T + (j + 1) * CK],
                                   Kt[64 * r:64 * r + 64, j, n, :], Qt[64 * r:64 * r + 64, n, j * CK:(j + 1) * CK],
                                   start=True, stop=True)
                m.then_inc(S["at_done"][0], 1)
                wait(pe, "kd_copied", l, 1)
                for n in range(4):
                    for r in range(2):
                        h = 2 * (n % 2) + r
                        m = mm(ps[64 * r:64 * r + 64, 3, n * HD:(n + 1) * HD], KDt[:, n, 64 * r:64 * r + 64],
                               Vh[:, n // 2, 0, h * HD:(h + 1) * HD], start=True, stop=True)
                m.then_inc(S["st_done"][0], 1)
                wait(pe, "at_masked", l, 1)
                wait(pe, "pv_copied", l, 2)
                wait(pe, "st_copied", l, 1)
                for d in range(2):
                    for q in range(HP):
                        for g in range(NG):
                            n = (d * HP + q) * NG + g
                            for r in range(2):
                                h = 2 * q + r
                                o = ps[64 * r:64 * r + 64, 2 * d + r, (q * NG + g) * T:(q * NG + g + 1) * T]
                                if g == 1:
                                    mm(o, s0[64 * r:64 * r + 64, d, q, :], QD[64 * r:64 * r + 64, d * HP + q, :],
                                       start=True, stop=False)
                                m = mm(o, Vh[:, d, g, h * HD:(h + 1) * HD], AT[:, r * 8 + n, :],
                                       start=(g == 0), stop=True)
                    m.then_inc(S["of_done"][0], 1)
                wait(pe, "o_sq", l, 1)
                mm(B(4), C["mean_h"], Qt[:, 0:4, :].rearrange("p n t -> p (n t)"), start=True, stop=True)\
                    .then_inc(S["o_mean"][0], 1)

                wait(pe, "o_ready", l, 1)
                for j in range(N_OUT):
                    unit_full(pe, l, U_OUT + j)
                    w = slot(l, U_OUT + j).rearrange("p (b n) -> p b n", b=KB)
                    for h in range(2):
                        for b in range(KB):
                            m = mm(ps[:, j, h * TT:(h + 1) * TT], w[:, b, h * P:(h + 1) * P], OT[:, b, :],
                                   start=(b == 0), stop=(b == KB - 1))
                    used(m)

                mean_square(1)
                wait(pe, "h_ready", l, 2 * KB)
                for g in range(NG):
                    for b in range(KB):
                        m = mm(ps[:, 6, g * NE:(g + 1) * NE], hT[:, b, g * T:(g + 1) * T], wr[:, b, :],
                               start=(b == 0), stop=(b == KB - 1))
                m.then_inc(S["route_done"][0], 1)
                wait(pe, "mix_added", l, N_OUT)
                for g in range(NG):
                    for b in range(KB):
                        m = tr(ps[:, 2 * g + b // 4, (b % 4) * P:(b % 4 + 1) * P], hT[:, b, g * T:(g + 1) * T])
                m.then_inc(S["h_turned"][0], 1)
                for i in range(2):
                    unit_full(pe, l, U_SH + i)
                    w = slot(l, U_SH + i).rearrange("p (b n) -> p b n", b=KB)
                    if i == 0:
                        wait(pe, "rstd_done", l, 2)
                    for h in range(2):
                        for b in range(KB):
                            m = mm(ps[:, 4 + i, h * TT:(h + 1) * TT], w[:, b, h * P:(h + 1) * P], hT[:, b, :],
                                   start=(b == 0), stop=(b == KB - 1))
                    used(m)
                wait(pe, "mask_ready", l, 1)
                for g in range(NG):
                    m = mm(ps[:, 7, NG * NE:(NG + 1) * NE], C["ones"], sel[:, g, :], start=(g == 0), stop=(g == 1))
                m.then_inc(S["over_counted"][0], 1)
                for g in range(NG):
                    o = ps[:, 7, g * NE:(g + 1) * NE]
                    m = mm(o, C["before"], sel[:, g, :], start=True, stop=(g == 0))
                    if g == 1:
                        m = mm(o, C["ones"], sel[:, 0, :], start=False, stop=True)
                m.then_inc(S["ranks_done"][0], 1)
                wait(pe, "shid", l, 1)
                wait(pe, "h_split", l, 1)
                unit_full(pe, l, U_SH + 2)
                w = slot(l, U_SH + 2).rearrange("p (b n) -> p b n", b=2)
                for b in range(KB):
                    for f in range(2):
                        m = mm(ps[:, b // 2, (b % 2) * TT:(b % 2 + 1) * TT], w[:, f, b * P:(b + 1) * P],
                               hid[:, f * TT:(f + 1) * TT], start=(f == 0 and b % 2 == 0), stop=False,
                               skip_group_check=True)
                used(m)

                def gather(buf, i, at):
                    if not (isinstance(at, int) and at == 0):
                        pe.wait_ge(S["gather_copied"][0], at)
                    for b in (2 * i, 2 * i + 1):
                        o = ps[:, 4, (b % 2) * 256:(b % 2 + 1) * 256]
                        for n, (part, g) in enumerate(((h_hi, 0), (h_lo, 0), (h_hi, 1), (h_lo, 1))):
                            m = mm(o, part[:, g, b * P:(b + 1) * P], sel01[:, buf, g, :], start=(n == 0), stop=(n == 3))
                    m.then_inc(S["gathered"][0], 1)

                def scatter():
                    for b in range(KB):
                        for part in (y_hi, y_lo):
                            m = mm(ps[:, b // 2, (b % 2) * TT:(b % 2 + 1) * TT], part[:, b * P:(b + 1) * P], slotT[:],
                                   start=False, stop=False, skip_group_check=True)
                    m.then_inc(S["scattered"][0], 1)

                FILLS = S["gathered"][1]
                wait(pe, "sel_ready", l, 1)
                unit_done(pe, l, U_SH + 1)
                wait(pe, "ssilu", l, 1)
                for i in range(4):
                    gather(0, i, l * FILLS + i)
                wait(pe, "over_marked", l, 1)
                mm(ps[:, 7, 256:384], C["ones"], over_diag[:], start=True, stop=True).then_inc(S["over_counted"][0], 1)
                wait(pe, "over_listed", l, 1)
                with pe.Fori(0, NPAIR // PB, 1) as it:
                    for p in range(PB):
                        buf, fill = (p // 2) % 2, l * FILLS + 4 + 2 * p + it * 2 * PB
                        pe.wait_ge(S["gather_copied"][0], l * FILLS + 4 + 4 * (p // 2) + it * 2 * PB)
                        pe.wait_ge(S["slotT_ready"][0], l * (NPAIR + 1) + p + 1 + it * PB)
                        for h in range(2):
                            for e in range(2):
                                unit_full(pe, l, U_EX + 6 * p + 2 * h + e, it * 32 * (6 * PB // RING))
                            for b in range(4):
                                for e in range(2):
                                    w = slot(l, U_EX + 6 * p + 2 * h + e).rearrange("p (m b n) -> p m b n", m=2, b=4)
                                    at = ((2 * p + e) % GE) * SLOTS
                                    m = mm(ps[64 * e:64 * e + 64, 5, :], hslots[:, buf, 4 * h + b, at:at + SLOTS], w[:, :, b, :],
                                           start=(h == 0 and b == 0), stop=(h == 1 and b == 3))
                                    if b == 3:
                                        used(m)
                        pe.wait_ge(S["sel_ready"][0], l * (NGRP + 2) + 2 + p // 2 + it * (PB // 2))
                        gather(1 - buf, 2 * (p % 2), fill)
                        pe.wait_ge(S["y_ready"][0], l * (NPAIR + 1) + p + 1 + it * PB)
                        scatter()
                        pe.wait_ge(S["hid_ready"][0], l * NPAIR + p + 1 + it * PB)
                        for f in range(2):
                            tr(ps[:, 5, f * P:(f + 1) * P], hid[:, f * P:(f + 1) * P])
                        for g in range(NG):
                            at = (p % 2) * P
                            m = tr(ps[:, 5, 256 + g * T:256 + (g + 1) * T], selw[:, buf, g, at:at + P])
                        m.then_inc(S["turned"][0], 1)
                        gather(1 - buf, 2 * (p % 2) + 1, fill + 1)
                        pe.wait_ge(S["hidT_copied"][0], l * NPAIR + p + 1 + it * PB)
                        for e in range(2):
                            unit_full(pe, l, U_EX + 6 * p + 4 + e, it * 32 * (6 * PB // RING))
                        for f in range(2):
                            for c in range(2):
                                for e in range(2):
                                    w = slot(l, U_EX + 6 * p + 4 + e).rearrange("p (f n) -> p f n", f=2)
                                    m = mm(ps[64 * e:64 * e + 64, 6 + c, :], hidT[:, f, 64 * e:64 * e + 64],
                                           w[:, f, c * 512:(c + 1) * 512], start=(f == 0), stop=(f == 1))
                                    if f == 1 and c == 1:
                                        used(m)
                wait(pe, "y_ready", l, NPAIR + 1)
                scatter()
                tr(ps[:, 5, 0:P], hT[:, 0, 0:P]).then_inc(V[l]["over_down"], 1)

                def visit(k):
                    pe.wait_ge(V[l]["over_full"], 48 * k + 48)
                    for g in range(NG):
                        for b in range(KB):
                            w = over_w[:, 0:4].rearrange("p (m i) (c n) -> p m (i c) n", m=2, n=DE)[:, :, b, :]
                            m = mm(B(4 + g), hT[:, b, g * T:(g + 1) * T], w, start=(b == 0), stop=(b == KB - 1))
                    m.then_inc(V[l]["over_up"], 1)
                    pe.wait_ge(V[l]["over_hid"], k + 1)
                    for f in range(2):
                        for g in range(NG):
                            m = tr(ps[:, 6, f * TT + g * T:f * TT + (g + 1) * T], hid[:, g * DE + f * P:g * DE + (f + 1) * P])
                    m.then_inc(V[l]["over_turned"], 1)
                    pe.wait_ge(V[l]["over_copied"], k + 1)
                    for b in range(KB):
                        for f in range(2):
                            m = mm(ps[:, b // 2, (b % 2) * TT:(b % 2 + 1) * TT], over_w[:, 4 + f, b * P:(b + 1) * P],
                                   over_hT[:, f, :], start=False, stop=False, skip_group_check=True)
                    m.then_inc(V[l]["over_down"], 1)

                over_visits(pe, l, visit)
                tr(ps[:, 5, 0:P], hT[:, 0, 0:P]).then_inc(S["sums_done"][0], 1)

            pe.wait_ge(fin_sq, 1)
            for b in range(KB):
                m = mm(ps[:, 4, 0:TT], C["mean_d"], xn[:, b, :], start=(b == 0), stop=(b == KB - 1))
            m.then_inc(fin_mean, 1)
            pe.wait_ge(fin_y, 1)
            for g in range(NG):
                for b in range(KB):
                    m = tr(ps[:, g * 2 + b // 4, (b % 4) * P:(b % 4 + 1) * P], hT[:, b, g * T:(g + 1) * T])
                    if b % 4 == 3:
                        m.then_inc(fin_turned, 1)

        @block.scalar
        def _(act):
            fn = nc.scalar.activation
            chain = Chain("act_order", ACT_LINKS)

            def rsqrt(out_ap, tmp, src, name, l, s=None):
                chain.link(act, fn(tmp, src, ACT.Ln, bias=epsc[:, 0:1]))
                r = fn(out_ap, tmp, ACT.Exp, scale=-0.5)
                r.then_inc(s if s is not None else S[name][0], 1)

            act.wait_ge(consts_set, 5)
            act.wait_ge(g_stored, 1)
            fn(stmp[:, 0:16], gvec[:, R_COND:R_COND + 16], ACT.Exp, scale=-1.0).then_inc(setup_act, 1)
            act.wait_ge(setup_dve, 1)
            fn(stmp[:, 16:24], stmp[:, 24:32], ACT.Exp).then_inc(setup_act, 1)
            for j in range(4):
                act.wait_ge(x_turned, j + 1)
                fn(xT[:, 2 * j:2 * j + 2, :].rearrange("p b t -> p (b t)"), B(1 + j), ACT.Copy).then_inc(x_stored, 1)

            for l in range(DEPTH):
                chain.layer(l)

                def copy(dst, src, name=None):
                    c = fn(dst, src, ACT.Copy)
                    if name:
                        c.then_inc(S[name][0], 1)
                    return c

                wait(act, "vec_turned", l, 1)
                copy(lvec[:], ps[:, 0, 0:VROWS], "vec_stored")
                wait(act, "cache_turned", l, 1)
                copy(kcT[:], ps[:, 1, 0:P])
                copy(ckvT[:, 2, :], ps[:, 1, P:2 * P])
                copy(krT[NOPE:, 2, :], ps[NOPE:NOPE + ROPE, 1, 2 * P:3 * P], "cache_copied")
                unit_done(act, l, U_ADA1 + 2 * SECT - 1)
                copy(modrows[:, 0, :], B(6), "rows_copied")
                wait(act, "mean_done", l, 1)
                rsqrt(rstd[:], lnv[:], ps[:, 0, 0:TT], "rstd_done", l)
                for i in range(11):
                    unit_done(act, l, U_IN + min(i, N_IN - 1))
                    if i == 0:
                        if l > 0:
                            act.wait_ge(out_sem, l * 16 * STORES)
                    bank = (i + 1) % 8
                    if i == 1:
                        copy(U[:, i, 0:TT], ps[:, bank, 0:TT])
                        copy(krT[NOPE:, 0:2, :].rearrange("p n t -> p (n t)"), ps[NOPE:NOPE + ROPE, bank, TT:2 * TT], "u_copied")
                    elif i == 9:
                        copy(U[:, i, 0:TT], ps[:, bank, 0:TT], "u_copied")
                    else:
                        copy(U[:, i, :], ps[:, bank, :], "u_copied")
                wait(act, "u_copied", l, 11)
                flat = lambda x: x.rearrange("p n t -> p (n t)")
                parts = ((flat(lf), flat(U[:, U_ZF:U_ZB + 1, :])), (flat(Gc[:, 0:4, :]), U[:, U_HQ, :]),
                         (flat(Gc[:, 4:8, :]), U[:, U_HG, :]))
                for dst, src in parts:
                    e = fn(dst, src, ACT.Exp, scale=-1.0)
                chain.link(act, e)
                for dst, _ in parts:
                    e = fn(dst, dst, ACT.Ln, bias=1.0)
                chain.link(act, e)
                for dst, _ in parts:
                    e = fn(dst, dst, ACT.Exp, scale=-1.0)
                e.then_inc(S["hg_exp"][0], 1)
                wait(act, "lat_mean", l, 1)
                wait(act, "lat_sq", l, 1)
                rsqrt(rsq[:], gs[:], B(3), "lat_rstd", l)
                for k in (1, 2):
                    unit_done(act, l, U_ADA2 + 2 * k * SECT - 1)
                    copy(modrows[:, k, :], B(3 + k), "rows_copied")
                wait(act, "flip_done", l, 1)
                copy(Vh[:, 1, :, :].rearrange("p g n -> p (g n)"), B(4))
                copy(Vh[:, 0, :, :].rearrange("p g n -> p (g n)"), U[:, U_I, :], "flip_copied")
                wait(act, "fn1_done", l, 1)
                for g in range(NG):
                    c = copy(F1[:, :, :, g, :], ps[:, 6 + g, :].rearrange("p (c h t) -> p c h t", c=2, h=2))
                c.then_inc(S["fn1_copied"][0], 1)
                wait(act, "hg_f", l, 1)
                fn(lf[:, 0:4, :], Qt[:, 0:4, :], ACT.Ln)
                fn(lf[:, 4:8, ::-1], Qt[:, 4:8, :], ACT.Ln).then_inc(S["hg_ln"][0], 1)
                wait(act, "mq_done", l, 1)
                copy(qT[:].rearrange("p h t -> p (h t)"), ps[0:NOPE + ROPE, 0:2, :].rearrange("p b t -> p (b t)"), "mq_copied")
                wait(act, "mv_done", l, 1)
                wait(act, "krot_done", l, 1)
                copy(vM[:].rearrange("p n t -> p (n t)"), ps[:, 2:4, :].rearrange("p b t -> p (b t)")[:, 0:768], "mv_copied")
                wait(act, "fn2_done", l, 1)
                copy(F2.rearrange("p b t -> p (b t)"), B(6), "fn2_copied")
                wait(act, "mk_done", l, 1)
                for h, bank in enumerate((4, 5, 0, 1)):
                    c = copy(kT[0:NOPE, h].rearrange("p n t -> p (n t)"), ps[0:NOPE, bank, 0:3 * T])
                c.then_inc(S["mk_copied"][0], 1)
                wait(act, "fn3_done", l, 1)
                copy(OT[:, 4:6, :].rearrange("p b t -> p (b t)"), B(7), "fn3_copied")
                wait(act, "kv_turned", l, 1)
                copy(o_ckv[:], ps[:, 0, 0:P])
                copy(o_kr[:], ps[:, 0, P + NOPE:P + NOPE + ROPE], "kvout_copied")

                def softmax_exp(n, scale):
                    wait(act, "negmax", l, n + 1)
                    for h in range(4):
                        r, c = h // 2, h % 2
                        fn(prS[:, h, :], ps[:, 2 + r, c * TT:(c + 1) * TT], ACT.Exp, bias=negm[:, h:h + 1], scale=scale,
                           accum_out=den[:, h:h + 1])
                        e = fn(prP[:, h, :], ps[:, 4 + r, c * T:(c + 1) * T], ACT.Exp, bias=negm[:, 4 + h:5 + h], scale=scale,
                               accum_out=den[:, 4 + h:5 + h])
                        if h == 3 and n == 1:
                            e.then_inc(S["exps"][0], 1)
                    if n == 0:
                        fn(esk[:], mx[:], ACT.Exp).then_inc(S["exps"][0], 1)

                def softmax_out(n, blk):
                    wait(act, "p_turned", l, n + 1)
                    for i, bank in enumerate((6, 7, 0)):
                        c = copy(pT[:, 4 * i:4 * i + 4, :].rearrange("p n t -> p (n t)"), B(bank))
                    c.then_inc(S["p_copied"][0], 1)
                    wait(act, "pv_done", l, n + 1)
                    copy(OT[:, blk:blk + 2, :].rearrange("p b t -> p (b t)"), B(1), "pv_copied")

                softmax_exp(0, SWA_SCALE)
                softmax_out(0, 6)
                softmax_exp(1, MLA_SCALE)
                wait(act, "diffs", l, 1)
                fn(Qt[:], Qt[:], ACT.Exp)
                for j in range(NCK):
                    kj = Kt[:, j, :, 0:(j + 1) * CK]
                    fn(kj, kj, ACT.Exp)
                fn(KD[:], KD[:], ACT.Exp)
                fn(QD[:], QD[:], ACT.Exp).then_inc(S["decays"][0], 1)
                softmax_out(1, 0)
                wait(act, "kd_turned", l, 1)
                copy(KDt[:].rearrange("p n t -> p (n t)"), B(2), "kd_copied")
                wait(act, "st_done", l, 1)
                copy(o_st[:], ps[:, 3, 0:256], "st_copied")
                wait(act, "of_done", l, 1)
                ofw = prS[:, 0:2, :].rearrange("p n t -> p (n t)")
                for r in range(2):
                    c = copy(ofw[64 * r:64 * r + 64], ps[64 * r:64 * r + 64, r, :])
                c.then_inc(S["of_copied"][0], 1)
                wait(act, "o_mean", l, 1)
                rsqrt(rsq[:], prP[:].rearrange("p n t -> p (n t)"), B(4), "o_rstd", l)
                wait(act, "mean_done", l, 2)
                rsqrt(rstd[:], lnv[:], ps[:, 4, 0:TT], "rstd_done", l)
                wait(act, "route_done", l, 1)
                fn(sg[:].rearrange("p g e -> p (g e)"), ps[:, 6, 0:NG * NE], ACT.Exp, scale=-1.0).then_inc(S["route_exp"][0], 1)
                wait(act, "h_turned", l, 1)
                act.wait_ge(out_sem, (l + 1) * 16 * STORES)
                copy(h_hi[:].rearrange("p g n -> p (g n)"), ps[:, 0:4, :].rearrange("p b n -> p (b n)"), "hhi_done")
                unit_done(act, l, U_SH)
                fn(silu_g[:], B(4), ACT.Silu).then_inc(S["ssilu"][0], 1)
                with act.Fori(0, NPAIR // PB, 1) as it:
                    for p in range(PB):
                        unit_done(act, l, U_EX + 6 * p + 3, it * 6 * PB)
                        fn(silu_g[:, 0:256], ps[:, 5, 0:256], ACT.Silu).then_inc(S["silu_done"][0], 1)
                        act.wait_ge(S["turned"][0], l * NPAIR + p + 1 + it * PB)
                        fn(hidT[:].rearrange("p f t -> p (f t)"), ps[:, 5, 0:256], ACT.Copy).then_inc(S["hidT_copied"][0], 1)
                        act.wait_ge(S["gathered"][0], l * S["gathered"][1] + 4 + 2 * p + 2 + it * 2 * PB)
                        i = 2 * (p % 2) + 1
                        fn(hslots[:, 1 - (p // 2) % 2, 2 * i:2 * i + 2, :].rearrange("p b n -> p (b n)"), B(4), ACT.Copy)\
                            .then_inc(S["gather_copied"][0], 1)
                        unit_done(act, l, U_EX + 6 * p + 5, it * 6 * PB)
                        act.wait_ge(S["slotT_ready"][0], l * (NPAIR + 1) + p + 2 + it * PB)
                        fn(y_hi[:], ps[:, 6:8, :].rearrange("p b n -> p (b n)"), ACT.Copy, scale=gslot[:, 0:1])\
                            .then_inc(S["yhi_done"][0], 1)

                def visit(k):
                    act.wait_ge(V[l]["over_up"], k + 1)
                    fn(silu_g[:].rearrange("p (g n) -> p g n", g=NG), ps[:, 4:6, 0:DE], ACT.Silu)\
                        .then_inc(V[l]["over_silu"], 1)
                    act.wait_ge(V[l]["over_turned"], k + 1)
                    fn(over_hT[:].rearrange("p f t -> p (f t)"), B(6), ACT.Copy).then_inc(V[l]["over_copied"], 1)

                over_visits(act, l, visit)

            act.wait_ge(fin_mean, 1)
            chain2 = sem("fin_act")
            fn(lnv[:], ps[:, 4, 0:TT], ACT.Ln, bias=epsc[:, 0:1]).then_inc(chain2, 1)
            act.wait_ge(chain2, 1)
            fn(rstd[:], lnv[:], ACT.Exp, scale=-0.5).then_inc(fin_rstd, 1)
            for i in range(4):
                act.wait_ge(fin_turned, i + 1)
                for q in range(2):
                    fn(xrow[:, i * 512 + q * 256:i * 512 + (q + 1) * 256], ps[:, i, q * 256:(q + 1) * 256], ACT.Copy)\
                        .then_inc(fin_copied, 1)

        @block.vector
        def _(dve):
            v = nc.vector
            chain = Chain("dve_order", DVE_LINKS)
            sc_ = sem("dve_setup")
            cnt_ = [0]

            def link0(ins):
                cnt_[0] += 1
                ins.then_inc(sc_, 1)
                dve.wait_ge(sc_, cnt_[0])

            dve.wait_ge(consts_set, 5)
            dve.wait_ge(g_turned, 1)
            v.tensor_copy(gvec[:], ps[:, 0, 0:GROWS]).then_inc(g_stored, 1)
            dve.wait_ge(g_stored, 1)
            lg = gvec[:, R_LB:R_LB + 8].rearrange("p (r l q) -> p l r q", r=2, l=DEPTH)
            m_ = stmp[:, 32:36].rearrange("p (r q) -> p r q", r=2)
            d_ = stmp[:, 24:32].rearrange("p (l r q) -> p l r q", l=DEPTH, r=2)
            e_ = stmp[:, 16:24].rearrange("p (l r q) -> p l r q", l=DEPTH, r=2)
            link0(v.tensor_tensor(m_, lg[:, 0], lg[:, 1], ALU.max))
            link0(v.tensor_tensor(d_[:, 0], lg[:, 0], m_, ALU.subtract))
            v.tensor_tensor(d_[:, 1], lg[:, 1], m_, ALU.subtract).then_inc(setup_dve, 1)
            dve.wait_ge(setup_act, 1)
            link0(v.tensor_scalar(stmp[:, 40:56], stmp[:, 0:16], 1.0, None, ALU.add))
            link0(v.reciprocal(stmp[:, 40:56], stmp[:, 40:56]))
            link0(v.tensor_tensor(scond[:, :, 0:2].rearrange("p b g -> p g b"), gvec[:, 0:16].rearrange("p (g b) -> p g b", g=2),
                                  stmp[:, 40:56].rearrange("p (g b) -> p g b", g=2), ALU.mult))
            dve.wait_ge(setup_act, 2)
            link0(v.tensor_tensor(m_, e_[:, 0], e_[:, 1], ALU.add))
            link0(v.reciprocal(stmp[:, 36:40], stmp[:, 32:36]))
            r_ = stmp[:, 36:40].rearrange("p (r q) -> p r q", r=2)
            for i in range(DEPTH):
                link0(v.tensor_tensor(e_[:, i], e_[:, i], r_, ALU.mult))
            link0(v.tensor_tensor(d_[:, 1], e_[:, 0], e_[:, 1], ALU.add))
            link0(v.tensor_tensor(lb[:, 0], e_[:, 0], e_[:, 0], ALU.subtract))
            link0(v.tensor_tensor(lb[:, 1], d_[:, 1], e_[:, 0], ALU.subtract))
            link0(v.tensor_scalar(oml[:], lb[:], -1.0, 1.0, ALU.mult, ALU.add))
            dve.wait_ge(x_stored, 4)
            v.memset(stmp[:, 56:57], 0.0).then_inc(cond_ready, 1)

            for l in range(DEPTH):
                chain.layer(l)
                link = lambda ins: chain.link(dve, ins)
                sig = lambda ins, name: ins.then_inc(S[name][0], 1)

                def add_sections(k):
                    wait(dve, "rows_turned", l, k + 1)
                    for q in range(2):
                        i = 2 * k + q
                        rows = ps[:, 7 if k == 0 else 5 + k, q * 256:(q + 1) * 256].rearrange("p (h c r) -> p h c r", h=2, c=4)
                        bias = lvec[:, 8 * i:8 * i + 8].rearrange("p (c h) -> p h c", h=2)
                        ins = v.tensor_tensor(mod[:, i].rearrange("p (c h) g -> p h c g", h=2), rows[:, :, :, 0:2],
                                              bias.unsqueeze(3).broadcast_to([P, 2, 4, 2]), ALU.add)
                    if k == 0:
                        ins.then_inc(S["mod_done"][0], 1)
                        wait(dve, "mod_done", l, 1)
                    else:
                        link(ins)

                def norm_mod(k):
                    sig(v.tensor_tensor(xn, xT[:], xT[:], ALU.mult), "squares")
                    if k == 0:
                        wait(dve, "vec_stored", l, 1)
                        add_sections(0)
                        link(v.scalar_tensor_tensor(gain[:, 0], mod[:, 1], 1.0,
                                                    lvec[:, R_N1:R_N1 + 8].unsqueeze(2).broadcast_to([P, KB, NG]),
                                                    ALU.add, ALU.mult))
                    wait(dve, "rstd_done", l, k + 1)
                    link(v.tensor_tensor(xn, xT[:], rstd[:].unsqueeze(1).broadcast_to([P, KB, TT]), ALU.mult))
                    for b in range(KB):
                        for g in range(NG):
                            t = slice(g * T, (g + 1) * T)
                            ins = v.tensor_scalar(hT[:, b, t], xn[:, b, t], gain[:, k, b, g:g + 1],
                                                  mod[:, 3 * k, b, g:g + 1], ALU.mult, ALU.add)
                        sig(ins, "h_ready")

                norm_mod(0)

                wait(dve, "u_copied", l, 2)
                v.tensor_tensor(cqn, u2(U_Q), u2(U_Q), ALU.mult)
                sig(v.tensor_tensor(rsq[:, 0:TT], U[:, U_KV, 0:TT], U[:, U_KV, 0:TT], ALU.mult), "lat_sq")
                wait(dve, "hg_exp", l, 1)
                flat = lambda x: x.rearrange("p n t -> p (n t)")
                for d in range(2):
                    for q in range(HP):
                        n = 2 * (d * HP + q)
                        link(v.tensor_scalar(Qt[:, n:n + 2, :], lf[:, n:n + 2, :], oml[:, l, d, q:q + 1], lb[:, l, d, q:q + 1],
                                             ALU.mult, ALU.add))
                v.tensor_scalar(kk[:, 0:4, :], Qt[:, 0:4, :], -1.0, 1.0, ALU.mult, ALU.add)
                sig(v.tensor_scalar(kk[:, 4:8, ::-1], Qt[:, 4:8, :], -1.0, 1.0, ALU.mult, ALU.add), "hg_f")
                wait(dve, "lat_rstd", l, 1)
                q4 = U[:, U_HQ, :].rearrange("p (n t) -> p n t", t=T)
                v.tensor_tensor(qs[:, 0:4, :], q4, Gc[:, 0:4, :], ALU.mult)
                v.tensor_tensor(qs[:, 4:8, ::-1], q4, Gc[:, 0:4, :], ALU.mult)
                v.tensor_tensor(gs[:], U[:, U_HG, :], flat(Gc[:, 4:8, :]), ALU.mult)
                rq = rsq[:, 0:TT]
                link(v.tensor_tensor(cqn, u2(U_Q), rq.unsqueeze(1).broadcast_to([P, 2, TT]), ALU.mult))
                for b in range(2):
                    ins = v.tensor_scalar(cqn[:, b, :], cqn[:, b, :], lvec[:, R_QN + b:R_QN + b + 1], None, ALU.mult)
                sig(ins, "cqn_ready")
                sig(v.scalar_tensor_tensor(ckvT[:, 0:2, :].rearrange("p n t -> p (n t)"), U[:, U_KV, 0:TT],
                                           lvec[:, R_KVN:R_KVN + 1], rsq[:, TT:2 * TT], ALU.mult, ALU.mult), "kvn_ready")
                for k in (1, 2):
                    add_sections(k)
                v.scalar_tensor_tensor(gain[:, 1], mod[:, 4], 1.0, lvec[:, R_N2:R_N2 + 8].unsqueeze(2).broadcast_to([P, KB, NG]),
                                       ALU.add, ALU.mult).then_inc(S["mod_rest"][0], 1)
                wait(dve, "srot_done", l, 1)
                raw = U[:, U_SQ:U_SK + 1, :].rearrange("p i t -> p (i t)").rearrange("p (b t) -> p b t", t=TT)[:, 0:3, T:TT]
                rot = prP[:, 0:3, :]
                bc3 = lambda x: x.unsqueeze(1).broadcast_to([x.shape[0], 3, T])
                v.tensor_tensor(rot, ps[:, 5, 0:3 * T].rearrange("p (b t) -> p b t", b=3), bc3(C["sin_s"]), ALU.mult)
                link(v.tensor_tensor(raw, raw, bc3(C["cos_s"]), ALU.mult))
                sig(v.tensor_tensor(raw, raw, rot, ALU.add), "srot_used")
                wait(dve, "hg_ln", l, 1)
                for n in range(8):
                    ins = v.tensor_tensor_scan(Gc[:, n, :], C["ones"], lf[:, n, :], 0.0, ALU.mult, ALU.add)
                link(ins)
                wait(dve, "kr_zeroed", l, 1)
                NR = NOPE + ROPE
                wait(dve, "krot_done", l, 1)
                wait(dve, "mv_copied", l, 1)
                link(v.tensor_tensor(prS[0:NR, 0, 0:T], ps[0:NR, 3, 256:384], C["sin_m"][0:NR], ALU.mult))
                link(v.tensor_tensor(krT[:, 1, :], krT[:, 1, :], C["cos_m"][0:NR], ALU.mult))
                sig(v.tensor_tensor(krT[:, 1, :], krT[:, 1, :], prS[0:NR, 0, 0:T], ALU.add), "krot_used")
                wait(dve, "krot_used", l, 1)
                sig(v.tensor_copy(kT[NOPE:].rearrange("p h n t -> p h (n t)"),
                                  krT[NOPE:].rearrange("p n t -> p (n t)").unsqueeze(1).broadcast_to([ROPE, MH, 3 * T])), "kr_ready")
                wait(dve, "qrot_done", l, 1)
                qv = qT[:, :, T:TT]
                bc4 = lambda x: x.unsqueeze(1).broadcast_to([NR, MH, T])
                rt = prS[0:NR, :, 0:T]
                v.tensor_tensor(rt, ps[0:NR, 6, :].rearrange("p (h t) -> p h t", h=MH), bc4(C["sin_m"][0:NR]), ALU.mult)
                link(v.tensor_tensor(qv, qv, bc4(C["cos_m"][0:NR]), ALU.mult))
                sig(v.tensor_tensor(qv, qv, rt, ALU.add), "qrot_used")

                def softmax_max(n, scale):
                    wait(dve, "scores", l, n + 1)
                    if n == 1:
                        wait(dve, "exps", l, 1)
                    v.tensor_reduce(mx[:, 0:4], ps[:, 2:4, :].rearrange("p b (c t) -> p (b c) t", c=2), AX_X, ALU.max)
                    link(v.tensor_reduce(mx[:, 4:8].rearrange("p (b c) -> p b c", b=2),
                                         ps[:, 4:6, 0:TT].rearrange("p b (c t) -> p b c t", c=2), AX_X, ALU.max))
                    if n == 0:
                        link(v.tensor_scalar(mx[:], mx[:], scale, None, ALU.mult))
                        m2 = mx[:].rearrange("p (g h) -> p g h", g=2)
                        sk = sink[:].unsqueeze(1).broadcast_to([P, 2, SH])
                        link(v.tensor_tensor(m2, m2, sk, ALU.max))
                        link(v.tensor_scalar(negm[:], mx[:], -1.0, None, ALU.mult))
                        sig(v.tensor_tensor(m2, sk, m2, ALU.subtract), "negmax")
                    else:
                        sig(v.tensor_scalar(negm[:], mx[:], -scale, None, ALU.mult), "negmax")

                def softmax_div(n):
                    wait(dve, "exps", l, n + 1)
                    if n == 0:
                        link(v.tensor_tensor(den[:], den[:], esk[:], ALU.add))
                    link(v.reciprocal(den[:], den[:]))
                    v.tensor_tensor(prS[:], prS[:], den[:, 0:4].unsqueeze(2).broadcast_to([P, 4, 2 * T]), ALU.mult)
                    sig(v.tensor_tensor(prP[:], prP[:], den[:, 4:8].unsqueeze(2).broadcast_to([P, 4, T]), ALU.mult), "probs")

                softmax_max(0, SWA_SCALE)
                Gb = Gc[:].rearrange("p n (j t) -> p n j t", t=CK)
                mid = CK // 2 - 1
                Qf = Qt[:].rearrange("p n (j t) -> p (n j) t", t=CK)
                ref = Gc[:].rearrange("p n (j t) -> p (n j) t", t=CK)[:, :, mid:mid + 1]
                v.tensor_tensor(Qf, Gc[:].rearrange("p n (j t) -> p (n j) t", t=CK), ref.broadcast_to([P, 8 * NCK, CK]), ALU.subtract)
                for j in range(NCK):
                    w = (j + 1) * CK
                    v.tensor_tensor(Kt[:, j, :, 0:w], Gb[:, :, j, mid:mid + 1].broadcast_to([P, 8, w]), Gc[:, :, 0:w], ALU.subtract)
                gP = Gc[:].rearrange("p (n g) t -> p n g t", g=NG)
                v.tensor_tensor(KD[:], gP[:, :, 0, T - 1:T].broadcast_to([P, 4, T]), gP[:, :, 0, :], ALU.subtract)
                sig(v.tensor_copy(QD[:], gP[:, :, 1, :]), "diffs")
                softmax_div(0)
                softmax_max(1, MLA_SCALE)
                softmax_div(1)
                wait(dve, "decays", l, 1)
                for j in range(NCK):
                    w = (j + 1) * CK
                    v.tensor_tensor(Kt[:, j, :, 0:w], Kt[:, j, :, 0:w], kk[:, :, 0:w], ALU.mult)
                v.tensor_tensor(Qt[:], Qt[:], qs[:], ALU.mult)
                kP = kk[:].rearrange("p (n g) t -> p n g t", g=NG)
                qP = qs[:].rearrange("p (n g) t -> p n g t", g=NG)
                v.tensor_tensor(KD[:], KD[:], kP[:, :, 0, :], ALU.mult)
                sig(v.tensor_tensor(QD[:], QD[:], qP[:, :, 1, :], ALU.mult), "recur_ready")
                wait(dve, "at_done", l, 1)
                wait(dve, "attn_zeroed", l, 1)
                msk = C["causal"].bitcast(I32).unsqueeze(1).broadcast_to([P, 4, T])
                for i in range(4):
                    ins = v.copy_predicated(AT[:, 4 * i:4 * i + 4, :], msk, B(4 + i).rearrange("p (n t) -> p n t", n=4))
                sig(ins, "at_masked")
                wait(dve, "of_done", l, 2)
                wait(dve, "of_copied", l, 1)
                for r in range(2):
                    h = slice(64 * r, 64 * r + 64)
                    link(v.tensor_tensor(KD[h], ps[h, 2 + r, :].rearrange("p (n t) -> p n t", t=T)[:, :, ::-1],
                                         prS[h, 0:2, :].rearrange("p b (c t) -> p (b c) t", c=2), ALU.add))
                sig(v.tensor_tensor(Qt[:, 0:4, :], KD[:], KD[:], ALU.mult), "o_sq")
                link(v.tensor_tensor(gs[:], gs[:], flat(KD[:]), ALU.mult))
                wait(dve, "o_rstd", l, 1)
                sig(v.scalar_tensor_tensor(OT[:, 2:4, :].rearrange("p b t -> p (b t)"), gs[:], lvec[:, R_HGN:R_HGN + 1], rsq[:],
                                           ALU.mult, ALU.mult), "o_ready")

                for j in range(N_OUT):
                    unit_done(dve, l, U_OUT + j)
                    for h in range(2):
                        b = 2 * j + h
                        for g in range(NG):
                            t = slice(g * T, (g + 1) * T)
                            ins = v.scalar_tensor_tensor(xT[:, b, t], ps[:, j, h * TT + g * T:h * TT + (g + 1) * T],
                                                         mod[:, 2, b, g:g + 1], xT[:, b, t], ALU.mult, ALU.add)
                    sig(ins, "mix_added")
                wait(dve, "mix_added", l, N_OUT)
                norm_mod(1)

                wait(dve, "route_exp", l, 1)
                link(v.tensor_scalar(sg[:], sg[:], 1.0, None, ALU.add))
                link(v.reciprocal(sg[:], sg[:]))
                link(v.tensor_tensor(sbs[:], sg[:], brt[:].unsqueeze(1).broadcast_to([P, NG, NE]), ALU.add))
                for g in range(NG):
                    link(v.max(top8[:, g, :], sbs[:, g, :]))
                for g in range(NG):
                    th = top8[:, g, TOPK - 1:TOPK]
                    link(v.tensor_scalar(sel[:, g, :], sbs[:, g, :], th, None, ALU.is_gt))
                    link(v.tensor_reduce(cnt[:, g, 0:1], sel[:, g, :], AX_X, ALU.add))
                    link(v.tensor_scalar(cnt[:, g, 1:2], cnt[:, g, 0:1], -1.0, float(TOPK), ALU.mult, ALU.add))
                    link(v.tensor_scalar(eqm[:, g, :], sbs[:, g, :], th, None, ALU.is_equal))
                    link(v.tensor_tensor_scan(cum[:, g, :], C["ones"][:, 0:NE], eqm[:, g, :], 0.0, ALU.mult, ALU.add))
                    link(v.scalar_tensor_tensor(eqm[:, g, :], cum[:, g, :], cnt[:, g, 1:2], eqm[:, g, :], ALU.is_le, ALU.mult))
                sig(v.tensor_tensor(sel[:], sel[:], eqm[:], ALU.add), "mask_ready")
                wait(dve, "mask_ready", l, 1)
                link(v.tensor_tensor(sg[:], sel[:], sg[:], ALU.mult))
                link(v.tensor_reduce(cnt[:, :, 0], sg[:], AX_X, ALU.add))
                link(v.reciprocal(cnt[:, :, 1], cnt[:, :, 0]))
                for g in range(NG):
                    v.tensor_scalar(gatew[:, g, 0:NE], sg[:, g, :], ROUTE_SCALE, cnt[:, g, 1:2], ALU.mult, ALU.mult)
                wait(dve, "ranks_done", l, 1)
                link(v.scalar_tensor_tensor(rank[:, :, 0:NE], ps[:, 7, 0:NG * NE].rearrange("p (g e) -> p g e", g=NG), 1.0, sel[:],
                                            ALU.add, ALU.mult))
                sig(v.tensor_scalar(rank[:, :, 0:NE], rank[:, :, 0:NE], -1.0, None, ALU.add), "gates_ready")
                wait(dve, "gates_ready", l, 1)
                v.scalar_tensor_tensor(over_gate[:], rank[:, :, 0:NE], float(SLOTS), gatew[:, :, 0:NE], ALU.is_ge, ALU.mult)
                wait(dve, "over_counted", l, 1)
                link(v.tensor_scalar(over_s[:, 0], ps[:, 7, NG * NE:(NG + 1) * NE], float(SLOTS), None, ALU.is_gt))
                link(v.tensor_tensor_scan(over_s[:, 1], C["ones"][:, 0:NE], over_s[:, 0], 0.0, ALU.mult, ALU.add))
                link(v.scalar_tensor_tensor(over_s[:, 2], over_s[:, 1], C["place"], over_s[:, 0], ALU.is_equal, ALU.mult))
                link(v.tensor_tensor(over_s[:, 2], over_s[:, 2], C["experts"], ALU.mult))
                link(v.tensor_reduce(over_at[:], over_s[:, 2], AX_X, ALU.add))
                sig(v.tensor_scalar(over_diag[:], ident, over_at[:, 0:1], None, ALU.mult), "over_marked")
                wait(dve, "hhi_done", l, 1)
                sig(v.tensor_tensor(h_lo[:].rearrange("p g n -> p (g n)"), ps[:, 0:4, :].rearrange("p b n -> p (b n)"),
                                    h_hi[:].bitcast(F32).rearrange("p g n -> p (g n)"), ALU.subtract), "h_split")
                wait(dve, "ssilu", l, 1)
                unit_done(dve, l, U_SH + 1)
                sig(v.tensor_tensor(hid[:], B(5), silu_g[:], ALU.mult), "shid")

                def places(buf, e0, n):
                    cols = lambda x: x.rearrange("p g (e s) -> p g e s", e=GE)
                    bc = lambda x: x.unsqueeze(3).broadcast_to([P, NG, GE, SLOTS])
                    w = v.tensor_tensor(cols(sel01[:, buf]), bc(rank[:, :, e0]),
                                        C["slots"].unsqueeze(1).unsqueeze(1).broadcast_to([P, NG, GE, SLOTS]), ALU.is_equal)
                    w.then_inc(sel_built, 1)
                    dve.wait_ge(sel_built, n)
                    v.tensor_tensor(cols(selw[:, buf]), cols(sel01[:, buf].bitcast(F32)), bc(gatew[:, :, e0]), ALU.mult)\
                        .then_inc(S["sel_ready"][0], 1)

                for q in range(2):
                    places(q, slice(q * GE, (q + 1) * GE), l * (NGRP + 2) + q + 1)
                v.memset(y_hi[:].bitcast(F32), 0.0)
                sig(v.memset(y_lo[:].bitcast(F32), 0.0), "y_ready")
                sig(v.memset(slotT[:].bitcast(F32), 0.0), "slotT_ready")
                FILLS = S["gathered"][1]

                def copy_fill(buf, i, at):
                    dve.wait_ge(S["gathered"][0], at)
                    v.tensor_copy(hslots[:, buf, 2 * i:2 * i + 2, :].rearrange("p b n -> p (b n)"), B(4))\
                        .then_inc(S["gather_copied"][0], 1)

                for i in range(4):
                    copy_fill(0, i, l * FILLS + i + 1)
                wait(dve, "over_counted", l, 2)
                v.tensor_copy(over_list[:, 0:OVER], ps[:, 7, 256:256 + OVER])
                sig(v.tensor_copy(over_list[:, OVER:], over_s[:, 1, NE - 1:NE]), "over_listed")
                with dve.Fori(0, NPAIR // PB, 1) as it:
                    for p in range(PB):
                        buf = (p // 2) % 2
                        dve.wait_ge(S["silu_done"][0], l * NPAIR + p + 1 + it * PB)
                        v.tensor_tensor(hid[:, 0:256], ps[:, 5, 256:512], silu_g[:, 0:256], ALU.mult)\
                            .then_inc(S["hid_ready"][0], 1)
                        copy_fill(1 - buf, 2 * (p % 2), l * FILLS + 4 + 2 * p + 1 + it * 2 * PB)
                        dve.wait_ge(S["turned"][0], l * NPAIR + p + 1 + it * PB)
                        dve.wait_ge(S["gather_copied"][0], l * FILLS + 4 + 2 * p + 2 + it * 2 * PB)
                        v.tensor_scalar(slotT[:], ps[:, 5, 256:512], 0.0, None, ALU.is_gt)
                        v.tensor_reduce(gslot[:], ps[:, 5, 256:512], AX_X, ALU.max).then_inc(S["slotT_ready"][0], 1)
                        if p % 2 == 1:
                            e0 = bass.ds(it * (2 * PB) + 2 * (p - 1) + 2 * GE, GE)
                            places(buf, e0, l * (NGRP + 2) + 3 + p // 2 + it * (PB // 2))
                        dve.wait_ge(S["yhi_done"][0], l * NPAIR + p + 1 + it * PB)
                        v.scalar_tensor_tensor(y_lo[:], ps[:, 6:8, :].rearrange("p b n -> p (b n)"), gslot[:, 0:1],
                                               y_hi[:].bitcast(F32), ALU.mult, ALU.subtract).then_inc(S["y_ready"][0], 1)

                def visit(k):
                    x = dve.value_load(over_list[0:1, bass.ds(k, 1)], min_val=0, max_val=NE - 1)
                    dve.wait_ge(V[l]["over_silu"], k + 1)
                    for g in range(NG):
                        h = v.scalar_tensor_tensor(hid[:, g * DE:(g + 1) * DE], ps[:, 4 + g, DE:2 * DE],
                                                   over_gate[:, g, bass.ds(x, 1)], silu_g[:, g * DE:(g + 1) * DE],
                                                   ALU.mult, ALU.mult)
                    h.then_inc(V[l]["over_hid"], 1)

                over_visits(dve, l, visit)
                wait(dve, "sums_done", l, 1)
                for b in range(KB):
                    for g in range(NG):
                        t = slice(g * T, (g + 1) * T)
                        ins = v.scalar_tensor_tensor(xT[:, b, t], ps[:, b // 2, (b % 2) * TT + g * T:(b % 2) * TT + (g + 1) * T],
                                                     mod[:, 5, b, g:g + 1], xT[:, b, t], ALU.mult, ALU.add)
                sig(ins, "moe_added")
                wait(dve, "moe_added", l, 1)
            assert chain.k == chain.n, ("DVE_LINKS", chain.k)

            v.tensor_tensor(xn, xT[:], xT[:], ALU.mult).then_inc(fin_sq, 1)
            dve.wait_ge(fin_rstd, 1)
            link0(v.tensor_tensor(xn, xT[:], rstd[:].unsqueeze(1).broadcast_to([P, KB, TT]), ALU.mult))
            for b in range(KB):
                ins = v.tensor_scalar(hT[:, b, :], xn[:, b, :], gvec[:, R_FG + b:R_FG + b + 1], None, ALU.mult)
            ins.then_inc(fin_y, 1)


_INS = ["x_prompt", "x_sample", "c", "cache_mla_ckv", "cache_mla_krope", "cache_swa_k", "cache_swa_v", "state_hgrn",
        "c_ctx", "w_ada", "b_ada", "norm1_g", "norm2_g", "w_in", "mla_q_norm_g", "mla_w_q_up", "mla_kv_norm_g",
        "mla_w_kv_up", "hg_lb_logits", "hg_norm_g", "fn_w", "swa_sink", "w_out", "moe_w_router", "moe_b_router",
        "moe_w_gate", "moe_w_up", "moe_w_down", "sh_w_gate", "sh_w_up", "sh_w_down", "final_norm_g"]
_OUTS = [("y_p", (1, T, D)), ("y_s", (1, T, D)), ("ckv", (1, DEPTH, T, KVL)), ("kr", (1, DEPTH, T, ROPE)),
         ("k", (1, DEPTH, T, SKV, SD)), ("v", (1, DEPTH, T, SKV, SD)), ("st", (1, DEPTH, 2, HH, HD, HD))]


def kernel(**inputs):
    import concourse.bacc as _bacc
    from concourse.bass_utils import run_bass_kernel_spmd as _run

    nc = _bacc.Bacc("TRN2", target_bir_lowering=False, num_devices=1)
    arrays, a, out = {}, {}, {}
    for name in _INS:
        x = np.ascontiguousarray(inputs[name])
        arrays[f"in_{name}"] = x
        a[name] = nc.dram_tensor(f"in_{name}", x.shape, F32, kind="ExternalInput").ap()
    arrays["in_consts"] = constant_array()
    a["consts"] = nc.dram_tensor("in_consts", arrays["in_consts"].shape, F32, kind="ExternalInput").ap()
    for name, shape in _OUTS:
        out[name] = nc.dram_tensor(f"out_{name}", shape, F32, kind="ExternalOutput").ap()
    build(nc, a, out)
    r = _run(nc, [arrays], core_ids=[0])
    return tuple(r.results[0][f"out_{name}"] for name, _ in _OUTS)
```

```python
from contextlib import ExitStack

import numpy as np
import concourse.bass as bass
from concourse import mybir

F32 = mybir.dt.float32
I32 = mybir.dt.int32
ALU = mybir.AluOpType
ACT = mybir.ActivationFunctionType
AX_X = mybir.AxisListType.X

P = 128
D = 1024
KB = D // P
DEPTH = 2
T = 128
NG = 2
TT = NG * T
EPS = 1e-6
GRID_W = 64
ROPE_BASE = 10000.0

MH, NOPE, ROPE, MV, QL, KVL = 4, 64, 32, 64, 256, 128
HH, HD = 4, 64
HP = HH // 2
SH, SKV, SD = 4, 2, 64
FNW, FNG = 256, 4
NE, TOPK, DE = 64, 6, 256
ROUTE_SCALE = 2.5
CK = 32
NCK = T // CK
MLA_SCALE = float(NOPE + ROPE) ** -0.5
SWA_SCALE = float(SD) ** -0.5

C_Q, C_KV = 0, QL
C_HQ = QL + KVL + ROPE
C_ZF, C_ZB, C_I, C_G = (C_HQ + n * 256 for n in range(1, 5))
C_FN = C_G + 256
C_SQ = C_FN + FNW
C_SK = C_SQ + SH * SD
IN_COLS = C_SK + 2 * SKV * SD
IN_UNITS = [(C_Q, 256), (C_KV, KVL + ROPE), (C_HQ, 256), (C_ZF, 256), (C_ZB, 256), (C_I, 256),
            (C_G, 256), (C_FN, 256), (C_SQ, 256), (C_SK, 256)]

UNIT = 2048
RING = 8
SECT = 4
SLOTS = 64
NPAIR = NE // 2
PB = 4
GE = 4
OVER_AFTER = NPAIR // PB // 2
OVER_CHUNK = 4
OVER = -(-(TT * TOPK // (SLOTS + 1)) // OVER_CHUNK) * OVER_CHUNK
NGRP = NE // GE
N_IN = len(IN_UNITS)
PAIR = 2 * SECT
NSP = 3 * DEPTH
U_ADA1 = 0
U_IN = U_ADA1 + PAIR
U_ADA2 = U_IN + N_IN
N_OUT = D // 256
U_OUT = U_ADA2 + (NSP - 1) * PAIR
U_SH = U_OUT + N_OUT
U_EX = U_SH + 3
OUT_BANK = (5, 0, 1, 2)
HG_BLOCKS = (2, 3)
N_LAYER = U_EX + 6 * NPAIR


def unit_at(l, n):
    if l == 0:
        return n
    return N_LAYER + (l - 1) * (N_LAYER - NSP * PAIR) + n - (PAIR if n < U_ADA2 else NSP * PAIR)


R_N1, R_N2, R_QN, R_KVN, R_HGN = 0, 8, 16, 18, 19
VROWS = 20
R_COND, R_LB, R_FG, R_BADA = 0, 16, 24, 32
GROWS = R_BADA + DEPTH * 6 * KB

VEC_LOADS = 6
LOADS = 14
STORES = 8
ACT_LINKS = 6
DVE_LINKS = 55

CONSTS = {}


def constant_array():
    parts = []
    at = 0

    def add(name, a):
        nonlocal at
        full = np.zeros((P, a.shape[1]), np.float32)
        full[:a.shape[0]] = a
        CONSTS[name] = (at, a.shape[1])
        at += a.shape[1]
        parts.append(full)

    n = np.arange(P)
    add("ident", np.eye(P))
    add("flip", np.eye(P)[::-1])
    ang = 2 * np.pi * np.outer(n, n) / T
    add("dft", np.concatenate([np.cos(ang), np.sin(ang)], axis=1))
    w = FNW // FNG
    ang = 2 * np.pi * np.outer(np.arange(w), np.arange(w)) / w
    s = 1.0 / np.sqrt(T * w)
    add("fcos", np.kron(np.eye(2), np.cos(ang)) * s)
    add("fsin", np.kron(np.eye(2), np.sin(ang)) * -s)

    def pair_swap(size, lo):
        m = np.zeros((size, size))
        for i in range(lo, size, 2):
            m[i + 1, i] = -1.0
            m[i, i + 1] = 1.0
        return m

    def tables(dim):
        nf = dim // 4
        inv = ROPE_BASE ** (-np.arange(nf, dtype=np.float32) / np.float32(nf))
        pos = np.stack([n // GRID_W, n % GRID_W]).astype(np.float32)
        a = pos[:, None, :] * inv[None, :, None]
        a = np.repeat(a.reshape(2 * nf, T), 2, axis=0)
        return np.cos(a), np.sin(a)

    add("swap_s", pair_swap(P, 0))
    add("swap_m", pair_swap(NOPE + ROPE, NOPE))
    cs, sn = tables(SD)
    add("cos_s", np.tile(cs, (2, 1)))
    add("sin_s", np.tile(sn, (2, 1)))
    cs, sn = tables(ROPE)
    add("cos_m", np.concatenate([np.ones((NOPE, T)), cs]))
    add("sin_m", np.concatenate([np.zeros((NOPE, T)), sn]))
    add("causal", (n[:, None] <= n[None, :]).astype(np.float32))
    add("mean_q", np.full((P, P), 1.0 / QL))
    add("mean_kv", np.full((P, P), 1.0 / KVL))
    add("mean_h", np.kron(np.eye(2), np.full((HD, HD), 1.0 / HD)))
    add("ones", np.ones((P, P)))
    add("before", (n[:, None] < n[None, :]).astype(np.float32))
    assert NE <= SLOTS
    add("slots", np.tile(np.arange(SLOTS), (P, 1)))
    add("place", np.arange(1, P + 1)[:, None])
    return np.ascontiguousarray(np.concatenate(parts, axis=1))


constant_array()
CONST_W = sum(w for _, w in CONSTS.values())


def build(nc, a, out):
    ctx = ExitStack()
    with ctx:
        def sb(name, shape, dt=F32):
            return ctx.enter_context(nc.sbuf_tensor(name, shape, dt))

        def sem(name):
            return ctx.enter_context(nc.semaphore(name))

        ring = sb("ring", [P, RING, UNIT])
        F32R = mybir.dt.float32r
        cst = sb("cst", [P, CONST_W])
        C = {k: cst[:, at:at + w] for k, (at, w) in CONSTS.items()}
        ident = C["ident"]
        xT = sb("xT", [P, KB, TT])
        HX = sb("HX", [P, 2 * KB * TT])
        hx = HX[:].rearrange("p (i b t) -> p i b t", i=2, b=KB)
        hT = hx[:, 0]
        xn = hx[:, 1]
        xrow = HX[:, KB * TT:]
        Kt = HX[:].rearrange("p (j n t) -> p j n t", j=NCK, n=8)
        rstd = sb("rstd", [P, TT])
        lnv = sb("lnv", [P, TT])
        gvec_rows = sb("gvec_rows", [GROWS, P])
        gvec = sb("gvec", [P, GROWS])
        lvec_rows = sb("lvec_rows", [VROWS, P])
        lvec = sb("lvec", [P, VROWS])
        scond = sb("scond", [P, KB, 32])
        stmp = sb("stmp", [P, 64])
        lb = sb("lb", [P, DEPTH, 2, HP])
        oml = sb("oml", [P, DEPTH, 2, HP])
        mod = sb("mod", [P, 6, KB, NG])
        modT = sb("modT", [P, NSP, 2, 2, 4, NG])
        gain = sb("gain", [P, 2, KB, NG])
        epsc = sb("epsc", [P, 1])
        wq = sb("wq", [P, 2, MH * (NOPE + ROPE)])
        wkv = sb("wkv", [P, MH, NOPE + MV])
        fnw = sb("fnw", [P, 2, FNW])
        wr = sb("wr", [P, KB, NE])
        brt = sb("brt", [P, NE])
        sink = sb("sink", [P, SH])
        kcache = sb("kcache", [P, 3, P])
        vcache = sb("vcache", [P, P])
        s0 = sb("s0", [P, 2, HP, HD])
        sg = sb("sg", [P, NG, NE])
        sbs = sb("sbs", [P, NG, NE])
        top8 = sb("top8", [P, NG, 8])
        sel = sb("sel", [P, NG, NE])
        eqm = sb("eqm", [P, NG, NE])
        cum = sb("cum", [P, NG, NE])
        cnt = sb("cnt", [P, NG, 2])
        rank = sb("rank", [P, NG, NE + 2 * GE])
        gatew = sb("gatew", [P, NG, NE + 2 * GE])
        gslot = sb("gslot", [P, 1])
        o_ckv = sb("o_ckv", [P, KVL])
        o_kr = sb("o_kr", [P, ROPE])
        o_st = sb("o_st", [P, 2 * HP * HD])

        mixers = ctx.enter_context(ExitStack())

        def sb(name, shape, dt=F32):
            return mixers.enter_context(nc.sbuf_tensor(name, shape, dt))

        U = sb("U", [P, 11, 512])
        u2 = lambda i: U[:, i, :].rearrange("p (b t) -> p b t", b=2)
        U_Q, U_KV, U_HQ, U_ZF, U_ZB, U_I, U_HG, U_FN, U_SQ, U_SK, U_SKV = range(11)
        OT = sb("OT", [P, 8, TT])
        cqn = OT[:, 0:2, :]
        ckvT = sb("ckvT", [P, 3, T])
        krT = sb("krT", [NOPE + ROPE, 3, T])
        qT = sb("qT", [NOPE + ROPE, MH, TT])
        kT = sb("kT", [NOPE + ROPE, MH, 3, T])
        vM = sb("vM", [P, 3, MH * MV])
        rsq = sb("rsq", [P, 512])
        kcT = sb("kcT", [P, T])
        prS = sb("prS", [P, 4, 2 * T])
        prP = sb("prP", [P, 4, T])
        pT = sb("pT", [P, 12, T])
        mx = sb("mx", [P, 8])
        negm = sb("negm", [P, 8])
        den = sb("den", [P, 8])
        esk = sb("esk", [P, 8])
        qs = sb("qs", [P, 8, T])
        kk = sb("kk", [P, 8, T])
        lf = U[:, U_ZF:U_ZB + 1, :].rearrange("p i (n t) -> p (i n) t", t=T)
        Gc = sb("Gc", [P, 8, T])
        Qt = sb("Qt", [P, 8, T])
        QD = sb("QD", [P, 4, T])
        KD = sb("KD", [P, 4, T])
        KDt = prP
        Vh = sb("Vh", [P, 2, NG, 256])
        AT = U[:, U_HQ:U_I + 1, :].rearrange("p i (n t) -> p (i n) t", t=T)
        gs = sb("gs", [P, 512])
        F1 = pT[:, 0:8, :].rearrange("p (c h g) t -> p c h g t", c=2, h=2)
        F2 = pT[:, 8:12, :].rearrange("p (b g) t -> p b (g t)", b=2)
        modrows = [pT[:, 8:12, :].rearrange("p c t -> p (c t)")] * 2 + [U[:, U_Q + k % 2, :] for k in range(NSP - 2)]
        mixers.close()
        moe = ctx.enter_context(ExitStack())

        def sb(name, shape, dt=F32):
            return moe.enter_context(nc.sbuf_tensor(name, shape, dt))

        h_hi = sb("h_hi", [P, NG, D], F32R)
        h_lo = sb("h_lo", [P, NG, D], F32R)
        sel01 = sb("sel01", [P, 2, NG, GE * SLOTS], F32R)
        selw = sb("selw", [P, 2, NG, GE * SLOTS])
        hslots = sb("hslots", [P, 2, KB, GE * SLOTS])
        slotT = sb("slotT", [P, TT], F32R)
        silu_g = sb("silu_g", [P, 512])
        hid = sb("hid", [P, 512])
        hidT = sb("hidT", [P, 2, P])
        y_hi = sb("y_hi", [P, D], F32R)
        y_lo = sb("y_lo", [P, D], F32R)
        over_w = sb("over_w", [P, 6, 1024])
        over_hT = sb("over_hT", [P, 2, TT])
        over_gate = sb("over_gate", [P, NG, NE])
        over_s = sb("over_s", [P, 3, NE])
        over_diag = sb("over_diag", [P, P])
        over_at = sb("over_at", [P, 1])
        over_list = sb("over_list", [P, OVER + 2], I32)
        over_any = sb("over_any", [P, 1])

        ps = ctx.enter_context(nc.psum_tensor("ps", [P, 8, 512], F32))
        B = lambda i: ps[:, i, :]

        slot_full = [sem(f"slot_full{i}") for i in range(RING)]
        unit_used = sem("unit_used")
        sel_built = sem("sel_built")
        S = {}

        def declare(**per_layer):
            for name, n in per_layer.items():
                S[name] = (sem(name), n)

        def wait(eng, name, l, k):
            s, n = S[name]
            assert 0 <= k <= n, name
            if l * n + k > 0:
                eng.wait_ge(s, l * n + k)

        class Chain:

            def __init__(self, name, per_layer):
                self.s, self.n, self.k, self.l = sem(name), per_layer, 0, 0

            def layer(self, l):
                assert self.k in (0, self.n), (self.k, self.n)
                self.l, self.k = l, 0

            def link(self, eng, ins):
                self.k += 1
                ins.then_inc(self.s, 1)
                eng.wait_ge(self.s, self.l * self.n + self.k)

        glob_in, vec_in, layer_in = sem("glob_in"), sem("vec_in"), sem("layer_in")
        out_sem, y_out = sem("out_sem"), sem("y_out")
        x_turned, x_stored, cond_turned, cond_ready, g_turned, g_stored = (
            sem(n) for n in ("x_turned", "x_stored", "cond_turned", "cond_ready", "g_turned", "g_stored"))
        setup_dve, setup_act, consts_set = sem("setup_dve"), sem("setup_act"), sem("consts_set")
        fin_mean, fin_rstd, fin_y, fin_turned, fin_copied = (
            sem(n) for n in ("fin_mean", "fin_rstd", "fin_y", "fin_turned", "fin_copied"))
        rows_copied, rows_turned, mod_taken = (sem(n) for n in ("rows_copied", "rows_turned", "mod_taken"))
        declare(vec_turned=1, vec_stored=1,
                squares=4, squares2=N_OUT, mean_done=2, rstd_done=2, xn_ready=2, h_ready=2 * KB, h_ready_lat=2 * KB,
                u_copied=11, cache_turned=1, cache_copied=1,
                lat_sq=1, lat_mean=1, lat_rstd=1, cqn_ready=1, kvn_ready=1,
                hg_exp=1, hg_f=1, hg_ln=1,
                flip_done=1, flip_copied=1, srot_done=1, srot_used=1,
                fn1_done=1, fn1_copied=1, fn2_done=1, fn2_copied=1, fn3_done=1, fn3_copied=1,
                mq_done=1, mq_copied=1, mv_done=1, mv_copied=1, krot_done=1, krot_used=1,
                kv_turned=1, kvout_copied=1,
                mk_done=1, mk_copied=1, qrot_done=1, qrot_used=1, kr_ready=1,
                scores=2, negmax=2, exps=2, probs=2, p_turned=2, p_copied=2, pv_done=2, pv_copied=2,
                kr_zeroed=1, keys_zeroed=1, attn_zeroed=1, diffs=1, decays=1, recur_ready=1, kd_turned=1, kd_copied=1, st_done=1, st_copied=1,
                at_done=2, at_masked=1, of_done=2, of_copied=1, o_sq=1, o_mean=1, o_rstd=1, o_ready=1,
                mix_added=N_OUT,
                route_done=1, route_exp=1, mask_ready=1, ranks_done=1, gates_ready=1,
                h_turned=1, hhi_done=1, h_split=1, ssilu=1, shid=1,
                sel_ready=NGRP + 2, gathered=4 + 2 * NPAIR, gather_copied=4 + 2 * NPAIR,
                silu_done=NPAIR, hid_ready=NPAIR, turned=NPAIR, hidT_copied=NPAIR, slotT_ready=NPAIR + 1,
                yhi_done=NPAIR, y_ready=NPAIR + 1, scattered=NPAIR + 1, moe_added=1,
                over_marked=1, sums_done=1, over_counted=2, over_listed=1)
        V = [{name: sem(f"{name}{l}") for name in ("over_full", "over_up", "over_silu", "over_hid", "over_turned",
                                                   "over_copied", "over_down")} for l in range(DEPTH)]

        def over_visits(eng, l, visit):
            n = eng.value_load(over_list[0:1, OVER:OVER + 1], min_val=0, max_val=OVER)
            with eng.If(n > 0):
                with eng.Fori(0, OVER // OVER_CHUNK, 1) as c:
                    with eng.If(n > c * OVER_CHUNK):
                        with eng.Fori(0, OVER_CHUNK, 1) as i:
                            with eng.If(n > c * OVER_CHUNK + i):
                                visit(c * OVER_CHUNK + i)

        HALVES = ((0, OVER_AFTER), (OVER_AFTER, NPAIR // PB))

        def unit_full(eng, l, n, more=0):
            n = unit_at(l, n)
            eng.wait_ge(slot_full[n % RING], (n // RING + 1) * 32 + more)

        def slot(l, n):
            return ring[:, unit_at(l, n) % RING, :]

        def unit_done(eng, l, n, more=0):
            eng.wait_ge(unit_used, unit_at(l, n) + 1 + more)

        block = ctx.enter_context(nc.Block())

        @block.sync
        def _(sp):
            w_in_v = a["w_in"].rearrange("l (b p) n -> l p b n", p=P)
            w_ada_v = a["w_ada"].rearrange("l (b p) n -> l p b n", p=P)
            w_out_v = a["w_out"].rearrange("l (b p) n -> l p b n", p=P)

            def load(l, n, parts, it=0):
                at_ = unit_at(l, n)
                if at_ >= RING:
                    sp.wait_ge(unit_used, at_ - RING + 1 + it * 6 * PB)
                s = slot_full[at_ % RING]
                for at, src in parts:
                    b, w = src.shape[1:]
                    dst = slot(l, n)[:, at:at + b * w].rearrange("p (b n) -> p b n", b=b)
                    sp.dma_start(dst, src).then_inc(s, 16)

            def halves(v, w):
                h = v.shape[1] // 2
                return [(0, v[:, 0:h]), (h * w, v[:, h:])]

            sp.dma_start(gvec_rows[R_COND:R_COND + 8], a["c_ctx"].rearrange("(b p) -> b p", p=P)).then_inc(glob_in, 16)
            sp.dma_start(gvec_rows[R_COND + 8:R_COND + 16], a["c"].rearrange("o (b p) -> (o b) p", p=P)).then_inc(glob_in, 16)
            sp.dma_start(gvec_rows[R_LB:R_LB + 8], a["hg_lb_logits"].rearrange("r l (b p) -> (r l b) p", p=P)).then_inc(glob_in, 16)
            sp.dma_start(gvec_rows[R_FG:R_FG + 8], a["final_norm_g"].rearrange("(b p) -> b p", p=P)).then_inc(glob_in, 16)
            sp.dma_start(gvec_rows[R_BADA:GROWS], a["b_ada"].rearrange("l (b p) -> (l b) p", p=P)).then_inc(glob_in, 16)
            sp.dma_start(cst[:], a["consts"]).then_inc(glob_in, 16)
            for g, name in enumerate(("x_prompt", "x_sample")):
                sp.dma_start(xrow[:, g * D:(g + 1) * D], a[name][0]).then_inc(glob_in, 16)
            gate_v, up_v, down_v = (a[n].rearrange("l e (b p) n -> l e p b n", p=P)
                                    for n in ("moe_w_gate", "moe_w_up", "moe_w_down"))
            for l in range(DEPTH):
                def ada(n, k):
                    for j in range(PAIR):
                        c0 = ((k % 3) * PAIR + j) * 256
                        load(0, n + j, halves(w_ada_v[k // 3, :, :, c0:c0 + 256], 256))

                if l == 0:
                    ada(U_ADA1, 0)
                for j, (c0, w) in enumerate(IN_UNITS):
                    load(l, U_IN + j, halves(w_in_v[l, :, :, c0:c0 + w], w))
                if l == 0:
                    for k in range(1, NSP):
                        ada(U_ADA2 + (k - 1) * PAIR, k)
                for j in range(N_OUT):
                    load(l, U_OUT + j, halves(w_out_v[l, :, :, j * 256:(j + 1) * 256], 256))
                for j, name in enumerate(("sh_w_gate", "sh_w_up", "sh_w_down")):
                    v = a[name].rearrange("l (b p) n -> l p b n", p=P)[l]
                    load(l, U_SH + j, halves(v, v.shape[2]))
                def visit(k):
                    x = sp.value_load(over_list[0:1, bass.ds(k, 1)], min_val=0, max_val=NE - 1)
                    sp.wait_ge(V[l]["over_down"], k + 1)
                    for i, v_ in enumerate((gate_v, up_v)):
                        sp.dma_start(over_w[:, 2 * i:2 * i + 2].rearrange("p i (b n) -> p (i b) n", n=DE), v_[l, x])\
                            .then_inc(V[l]["over_full"], 16)
                    sp.dma_start(over_w[:, 4:6], down_v[l, x]).then_inc(V[l]["over_full"], 16)

                for half, (lo, hi) in enumerate(HALVES):
                    with sp.Fori(lo, hi, 1) as it:
                        for p in range(PB):
                            for h in range(2):
                                for e in range(2):
                                    x = it * (2 * PB) + 2 * p + e
                                    b = slice(4 * h, 4 * h + 4)
                                    load(l, U_EX + 6 * p + 2 * h + e,
                                         [(0, gate_v[l, x, :, b]), (1024, up_v[l, x, :, b])], it)
                            for e in range(2):
                                load(l, U_EX + 6 * p + 4 + e, halves(down_v[l, it * (2 * PB) + 2 * p + e], D), it)
                    if half == 0:
                        wait(sp, "over_listed", l, 1)
                        over_visits(sp, l, visit)

        @block.gpsimd
        def _(pool):
            pool.memset(epsc[:], EPS).then_inc(consts_set, 1)
            pool.memset(scond[:], 0.0).then_inc(consts_set, 1)
            pool.memset(rank[:], -1.0).then_inc(consts_set, 1)
            pool.memset(gatew[:], 0.0).then_inc(consts_set, 1)
            pool.memset(kcache[:], 0.0).then_inc(consts_set, 1)
            pool.wait_ge(consts_set, 5)
            for l in range(DEPTH):
                wait(pool, "gates_ready", l, 0)
                rows = (("norm1_g", R_N1, 8), ("norm2_g", R_N2, 8),
                        ("mla_q_norm_g", R_QN, 2), ("mla_kv_norm_g", R_KVN, 1))
                loads = [(lvec_rows[r:r + n], a[name].rearrange("l (b p) -> l b p", p=P)[l]) for name, r, n in rows]
                hgn = a["hg_norm_g"].rearrange("l (o p) -> l o p", o=1)
                loads += [(lvec_rows[R_HGN:R_HGN + 1, r * HD:(r + 1) * HD], hgn[l]) for r in range(2)]
                assert len(loads) == VEC_LOADS
                for dst, src in loads:
                    pool.dma_start(dst, src).then_inc(vec_in, 16)
                loads = [
                    (wq[:], a["mla_w_q_up"].rearrange("l (b p) n -> l p b n", p=P)[l]),
                    (wkv[:].rearrange("p h n -> p (h n)"), a["mla_w_kv_up"][l]),
                    (fnw[:], a["fn_w"].rearrange("l (b p) n -> l p b n", p=P)[l]),
                    (wr[:], a["moe_w_router"].rearrange("l (b p) n -> l p b n", p=P)[l]),
                    (brt[:], a["moe_b_router"].rearrange("l (o n) -> l o n", o=1)[l].broadcast_to([P, NE])),
                    (sink[:], a["swa_sink"].rearrange("l (o n) -> l o n", o=1)[l].broadcast_to([P, SH])),
                    (kcache[:, 0, :], a["cache_swa_k"][0].rearrange("l t k d -> l t (k d)")[l]),
                    (kcache[:, 1, :], a["cache_mla_ckv"][0][l]),
                    (kcache[:, 2, NOPE:NOPE + ROPE], a["cache_mla_krope"][0][l]),
                    (vcache[:], a["cache_swa_v"][0].rearrange("l t k d -> l t (k d)")[l]),
                ]
                st = a["state_hgrn"][0].rearrange("l r (q s) d e -> l r q (s d) e", s=2)
                loads += [(s0[:, r, q, :], st[l, r, q]) for r in range(2) for q in range(HP)]
                assert len(loads) == LOADS
                for dst, src in loads:
                    pool.dma_start(dst, src).then_inc(layer_in, 16)
                wait(pool, "moe_added", l, 0)
                pool.memset(krT[0:NOPE], 0.0).then_inc(S["kr_zeroed"][0], 1)
                wait(pool, "u_copied", l, 11)
                pool.memset(Kt[:, 2, :, 3 * CK:], 0.0).then_inc(S["keys_zeroed"][0], 1)
                kv = u2(U_SKV)[:, 0, :]
                for dst, src in ((out["k"], kv[:, 0:128]), (out["v"], kv[:, 128:256])):
                    pool.dma_start(dst[0].rearrange("l t k d -> l t (k d)")[l], src).then_inc(out_sem, 16)
                wait(pool, "kvout_copied", l, 1)
                pool.dma_start(out["ckv"][0][l], o_ckv[:]).then_inc(out_sem, 16)
                pool.dma_start(out["kr"][0][l], o_kr[:]).then_inc(out_sem, 16)
                wait(pool, "recur_ready", l, 1)
                pool.memset(AT, 0.0).then_inc(S["attn_zeroed"][0], 1)
                wait(pool, "st_copied", l, 1)
                sto = out["st"][0].rearrange("l r (q s) d e -> l r q (s d) e", s=2)
                for r in range(2):
                    for q in range(HP):
                        at = (r * HP + q) * HD
                        pool.dma_start(sto[l, r, q], o_st[:, at:at + HD]).then_inc(out_sem, 16)
                wait(pool, "hhi_done", l, 1)
                pool.memset(y_hi[:].bitcast(F32), 0.0)
                pool.memset(y_lo[:].bitcast(F32), 0.0).then_inc(S["y_ready"][0], 1)
                pool.memset(slotT[:].bitcast(F32), 0.0).then_inc(S["slotT_ready"][0], 1)
            for g, name in enumerate(("y_p", "y_s")):
                pool.wait_ge(fin_copied, 3 + g)
                pool.dma_start(out[name][0], xrow[:, g * D:(g + 1) * D]).then_inc(y_out, 16)
            pool.wait_ge(y_out, 32)
            pool.wait_ge(out_sem, 16 * STORES * DEPTH)

        @block.tensor
        def _(pe):
            mm = nc.tensor.matmul

            def tr(o, i, n=P):
                return nc.tensor.transpose(o, i, ident[0:n, 0:n])

            def used(ins):
                ins.then_inc(unit_used, 1)

            pe.wait_ge(glob_in, 16 * 8)
            tr(ps[:, 0, 0:GROWS], gvec_rows[:], GROWS).then_inc(g_turned, 1)
            for b in range(KB):
                for g in range(NG):
                    t = tr(ps[:, 1 + b // 2, (b % 2) * TT + g * T:(b % 2) * TT + (g + 1) * T],
                           xrow[:, g * D + b * P:g * D + (b + 1) * P])
                if b % 2:
                    t.then_inc(x_turned, 1)
            pe.wait_ge(cond_ready, 1)

            for l in range(DEPTH):
                pe.wait_ge(vec_in, (l + 1) * 16 * VEC_LOADS)
                pe.wait_ge(x_stored, 4)
                pe.wait_ge(g_stored, 1)
                wait(pe, "moe_added", l, 0)
                tr(ps[:, 0, 0:VROWS], lvec_rows[:], VROWS).then_inc(S["vec_turned"][0], 1)

                def sum_squares(bank, j):
                    for b in (2 * j, 2 * j + 1):
                        m = mm(ps[:, bank, 0:TT], C["ones"], xn[:, b, :], start=(b == 0), stop=(b == KB - 1))
                    if b == KB - 1:
                        m.then_inc(S["mean_done"][0], 1)

                for j in range(KB // 2):
                    wait(pe, "squares", l, j + 1)
                    sum_squares(5, j)

                def ada_section(k, q, bank):
                    n0 = (U_ADA1 if k == 0 else U_ADA2 + (k - 1) * PAIR) + q * SECT
                    ws = []
                    for c in range(SECT):
                        unit_full(pe, 0, n0 + c)
                        ws.append(slot(0, n0 + c).rearrange("p (b n) -> p b n", b=KB))
                    for b in range(KB):
                        for c in range(SECT):
                            m = mm(ps[32 * c:32 * c + 32, bank, q * 256:(q + 1) * 256], scond[:, b, :], ws[c][:, b, :],
                                   start=(b == 0), stop=(b == KB - 1))
                            if b == KB - 1:
                                used(m)

                def ada_turn(k, bank):
                    pe.wait_ge(rows_copied, k + 1)
                    for i in range(4):
                        m = tr(ps[:, bank, i * P:(i + 1) * P], modrows[k][:, i * P:(i + 1) * P])
                    m.then_inc(rows_turned, 1)

                if l == 0:
                    for q in range(2):
                        ada_section(0, q, 6)
                    ada_turn(0, 7)
                pe.wait_ge(layer_in, (l + 1) * 16 * LOADS)
                for j in range(3):
                    c = tr(ps[0:(P if j < 2 else NOPE + ROPE), 1, j * P:(j + 1) * P],
                           kcache[:, j, 0:(P if j < 2 else NOPE + ROPE)])
                c.then_inc(S["cache_turned"][0], 1)

                def in_unit(j):
                    unit_full(pe, l, U_IN + j)
                    w_ = IN_UNITS[j][1]
                    return slot(l, U_IN + j)[:, 0:KB * w_].rearrange("p (b n) -> p b n", b=KB)

                def into(i):
                    if i == 0:
                        wait(pe, "cache_copied", l, 1)
                    if i == 6:
                        pe.wait_ge(mod_taken, 1)
                    if i == 4:
                        wait(pe, "rstd_done", l, 1)
                    if i == 7:
                        wait(pe, "vec_stored", l, 1)
                    if i >= 8:
                        wait(pe, "u_copied", l, i - 7)
                    return (i + 1) % 8

                def feature_major(i, lhs):
                    bank = into(i)
                    for h in range(2):
                        for b in range(KB):
                            if i == 0 and h == 0:
                                wait(pe, "h_ready", l, b + 1)
                                wait(pe, "h_ready_lat", l, b + 1)
                            m = mm(ps[:, bank, h * TT:(h + 1) * TT], lhs(h, b), hT[:, b, :], start=(b == 0), stop=(b == KB - 1))
                    return m

                def token_major(i, w):
                    bank = into(i)
                    for g in range(NG):
                        for b in range(KB):
                            m = mm(ps[:, bank, g * 256:(g + 1) * 256], hT[:, b, g * T:(g + 1) * T], w[:, b, :],
                                   start=(b == 0), stop=(b == KB - 1))
                    return m

                for j in range(N_IN):
                    w = in_unit(j)
                    if j == 1:
                        bank = into(1)
                        for b in range(KB):
                            mm(ps[:, bank, 0:TT], w[:, b, 0:KVL], hT[:, b, :], start=(b == 0), stop=(b == KB - 1))
                        for b in range(KB):
                            m = mm(ps[NOPE:NOPE + ROPE, bank, TT:2 * TT], w[:, b, KVL:KVL + ROPE], hT[:, b, :],
                                   start=(b == 0), stop=(b == KB - 1))
                    elif j in (5, 7):
                        m = token_major(j, w)
                    elif j == 8:
                        bank = into(8)
                        for h in range(SH):
                            r, c = h // 2, h % 2
                            for b in range(KB):
                                m = mm(ps[64 * r:64 * r + 64, bank, c * TT:(c + 1) * TT], w[:, b, h * SD:(h + 1) * SD],
                                       hT[:, b, :], start=(b == 0), stop=(b == KB - 1))
                    elif j == 9:
                        bank = into(9)
                        for b in range(KB):
                            mm(ps[:, bank, 0:TT], w[:, b, 0:128], hT[:, b, :], start=(b == 0), stop=(b == KB - 1))
                        m = token_major(10, w)
                    else:
                        m = feature_major(j, lambda h, b, w=w: w[:, b, h * P:(h + 1) * P])
                    used(m)

                wait(pe, "lat_sq", l, 1)
                wait(pe, "u_copied", l, 11)
                for b in range(2):
                    mm(ps[:, 3, 0:TT], C["mean_q"], cqn[:, b, :], start=(b == 0), stop=(b == 1))
                mm(ps[:, 3, TT:2 * TT], C["mean_kv"], rsq[:, 0:TT], start=True, stop=True).then_inc(S["lat_mean"][0], 1)
                mm(B(4), C["flip"], U[:, U_I, :], start=True, stop=True).then_inc(S["flip_done"][0], 1)
                srt = U[:, U_SQ:U_SK + 1, :].rearrange("p i t -> p (i t)").rearrange("p (b t) -> p b t", t=TT)[:, 0:3, T:TT]
                mm(ps[:, 5, 0:3 * T], C["swap_s"], srt, start=True, stop=True).then_inc(S["srot_done"][0], 1)
                for g in range(NG):
                    for cb in range(2):
                        m = mm(ps[:, 6 + g, cb * 256:(cb + 1) * 256], u2(U_FN)[:, g, cb * P:(cb + 1) * P], C["dft"],
                               start=True, stop=True)
                m.then_inc(S["fn1_done"][0], 1)
                if l == 0:
                    for q in range(2):
                        ada_section(1, q, 2)
                wait(pe, "cqn_ready", l, 1)
                HQ = NOPE + ROPE
                for h in range(MH):
                    for b in range(2):
                        m = mm(ps[0:HQ, h // 2, (h % 2) * TT:(h % 2 + 1) * TT], wq[:, b, h * HQ:(h + 1) * HQ], cqn[:, b, :],
                               start=(b == 0), stop=(b == 1))
                m.then_inc(S["mq_done"][0], 1)
                if l == 0:
                    ada_turn(1, 2)
                    pe.wait_ge(mod_taken, 2)
                wait(pe, "kvn_ready", l, 1)
                for n in range(3):
                    m = mm(ps[:, 2 + n // 2, (n % 2) * 256:(n % 2 + 1) * 256], ckvT[:, n, :], wkv[:, :, NOPE:],
                           start=True, stop=True)
                m.then_inc(S["mv_done"][0], 1)
                wait(pe, "kr_zeroed", l, 1)
                mm(ps[0:HQ, 3, 256:384], C["swap_m"][0:HQ, 0:HQ], krT[:, 1, :], start=True, stop=True)\
                    .then_inc(S["krot_done"][0], 1)
                wait(pe, "fn1_copied", l, 1)
                for cb in range(2):
                    for h, m_ in enumerate(("fcos", "fsin")):
                        m = mm(ps[:, 6, cb * TT:(cb + 1) * TT], C[m_], F1[:, cb, h].rearrange("p g t -> p (g t)"),
                               start=(h == 0), stop=(h == 1))
                m.then_inc(S["fn2_done"][0], 1)
                wait(pe, "flip_copied", l, 1)
                wait(pe, "srot_used", l, 1)
                wait(pe, "mq_copied", l, 1)
                for h, bank in enumerate((4, 5, 0, 1)):
                    m = mm(ps[0:NOPE, bank, 0:3 * T], wkv[:, h, 0:NOPE], ckvT[:].rearrange("p n t -> p (n t)"),
                           start=True, stop=True)
                m.then_inc(S["mk_done"][0], 1)
                wait(pe, "fn2_copied", l, 1)
                for ob in range(2):
                    for cb in range(2):
                        m = mm(ps[:, 7, ob * TT:(ob + 1) * TT], fnw[:, cb, ob * P:(ob + 1) * P], F2[:, cb, :],
                               start=(cb == 0), stop=(cb == 1))
                m.then_inc(S["fn3_done"][0], 1)
                mm(ps[0:HQ, 6, :].rearrange("p (h t) -> p h t", h=MH), C["swap_m"][0:HQ, 0:HQ], qT[:, :, T:TT], start=True, stop=True)\
                    .then_inc(S["qrot_done"][0], 1)
                wait(pe, "mk_copied", l, 1)
                tr(ps[:, 0, 0:P], ckvT[:, 0, :])
                tr(ps[:, 0, P:P + HQ], krT[:, 0, :], HQ).then_inc(S["kv_turned"][0], 1)

                def score(o, q, k):
                    return mm(o, q, k, start=True, stop=True)

                def transpose_probs(n):
                    wait(pe, "probs", l, n + 1)
                    if n == 0:
                        wait(pe, "qrot_used", l, 1)
                        wait(pe, "fn3_copied", l, 1)
                        wait(pe, "kvout_copied", l, 1)
                    wait(pe, "p_copied", l, n)
                    for h in range(4):
                        for c in range(3):
                            i = 3 * h + c
                            src = prS[:, h, c * T:(c + 1) * T] if c < 2 else prP[:, h, :]
                            m = tr(ps[:, (6, 7, 0, 2, 3, 4)[3 * n + i // 4], (i % 4) * T:(i % 4 + 1) * T], src)
                    m.then_inc(S["p_turned"][0], 1)

                def values(n, v):
                    wait(pe, "p_copied", l, n + 1)
                    if n == 0:
                        wait(pe, "mk_copied", l, 1)
                    wait(pe, "pv_copied", l, n)
                    for h in range(4):
                        r = (h % 2) * 64
                        o = ps[r:r + 64, 1, (h // 2) * TT:(h // 2 + 1) * TT]
                        mm(o[:, 0:T], v(h, 2), pT[:, 3 * h + 2, :], start=True, stop=True)
                        mm(o[:, T:TT], v(h, 0), pT[:, 3 * h, :], start=True, stop=False)
                        m = mm(o[:, T:TT], v(h, 1), pT[:, 3 * h + 1, :], start=False, stop=True)
                    m.then_inc(S["pv_done"][0], 1)

                wait(pe, "srot_used", l, 1)
                wait(pe, "mv_copied", l, 1)
                wait(pe, "krot_used", l, 1)
                for h in range(SH):
                    r, c = h // 2, h % 2
                    q = u2(U_SQ)[64 * r:64 * r + 64, c, :]
                    k = u2(U_SK)[64 * r:64 * r + 64, 0, :]
                    score(ps[:, 4 + r, c * T:(c + 1) * T], q[:, 0:T], k[:, 0:T])
                    score(ps[:, 2 + r, c * TT:c * TT + T], q[:, T:TT], k[:, T:TT])
                    m = score(ps[:, 2 + r, c * TT + T:(c + 1) * TT], q[:, T:TT], kcT[64 * r:64 * r + 64, :])
                m.then_inc(S["scores"][0], 1)
                if l == 0:
                    wait(pe, "qrot_used", l, 1)
                    for q in range(2):
                        ada_section(2, q, 6)
                    pe.wait_ge(rows_copied, 3)
                transpose_probs(0)

                def swa_v(h, c):
                    k = h // 2
                    if c == 1:
                        return vcache[:, k * SD:(k + 1) * SD]
                    return u2(U_SKV)[:, 0 if c == 2 else 1, 128 + k * SD:128 + (k + 1) * SD]

                values(0, swa_v)
                wait(pe, "exps", l, 1)
                wait(pe, "kr_ready", l, 1)
                wait(pe, "qrot_used", l, 1)
                for h in range(MH):
                    r, c = h // 2, h % 2
                    score(ps[:, 4 + r, c * T:(c + 1) * T], qT[:, h, 0:T], kT[:, h, 0, :])
                    m = score(ps[:, 2 + r, c * TT:(c + 1) * TT], qT[:, h, T:TT], kT[:, h, 1:3, :].rearrange("p n t -> p (n t)"))
                m.then_inc(S["scores"][0], 1)
                def within(r):
                    for n in range(8):
                        for j in range(NCK):
                            w = (j + 1) * CK if j < 2 else P
                            m = mm(ps[0:w, 6 - 2 * r + n // 4, (n % 4) * T + j * CK:(n % 4) * T + (j + 1) * CK],
                                   Kt[64 * r:64 * r + 64, j, n, 0:w], Qt[64 * r:64 * r + 64, n, j * CK:(j + 1) * CK],
                                   start=True, stop=True)
                    m.then_inc(S["at_done"][0], 1)

                if l == 0:
                    ada_turn(2, 0)
                wait(pe, "recur_ready", l, 1)
                wait(pe, "keys_zeroed", l, 1)
                within(0)
                if l == 0:
                    pe.wait_ge(mod_taken, 3)
                    for q in range(2):
                        ada_section(3, q, 0)
                transpose_probs(1)
                values(1, lambda h, c: vM[:, (1, 2, 0)[c], h * MV:(h + 1) * MV])

                if l == 0:
                    ada_turn(3, 0)
                for n in range(4):
                    m = tr(ps[:, 2, n * P:(n + 1) * P], KD[:, n, :])
                m.then_inc(S["kd_turned"][0], 1)
                within(1)
                wait(pe, "kd_copied", l, 1)
                for n in range(4):
                    for r in range(2):
                        h = 2 * (n % 2) + r
                        m = mm(ps[64 * r:64 * r + 64, 3, n * HD:(n + 1) * HD], KDt[:, n, 64 * r:64 * r + 64],
                               Vh[:, n // 2, 0, h * HD:(h + 1) * HD], start=True, stop=True)
                m.then_inc(S["st_done"][0], 1)
                if l == 0:
                    wait(pe, "pv_copied", l, 2)
                    for q in range(2):
                        ada_section(4, q, 1)
                    pe.wait_ge(mod_taken, 4)
                    pe.wait_ge(rows_copied, 5)
                wait(pe, "at_masked", l, 1)
                wait(pe, "pv_copied", l, 2)
                wait(pe, "st_copied", l, 1)
                for d in range(2):
                    for q in range(HP):
                        for g in range(NG):
                            n = (d * HP + q) * NG + g
                            for r in range(2):
                                h = 2 * q + r
                                o = ps[64 * r:64 * r + 64, 2 * d + r, (q * NG + g) * T:(q * NG + g + 1) * T]
                                if g == 1:
                                    mm(o, s0[64 * r:64 * r + 64, d, q, :], QD[64 * r:64 * r + 64, d * HP + q, :],
                                       start=True, stop=False)
                                m = mm(o, Vh[:, d, g, h * HD:(h + 1) * HD], AT[:, r * 8 + n, :],
                                       start=(g == 0), stop=True)
                    m.then_inc(S["of_done"][0], 1)
                def project(j, h, blocks):
                    for b in blocks:
                        w = slot(l, U_OUT + j).rearrange("p (b n) -> p b n", b=KB)
                        m = mm(ps[:, OUT_BANK[j], h * TT:(h + 1) * TT], w[:, b, h * P:(h + 1) * P], OT[:, b, :],
                               start=(h == 0 and b == 0), stop=(h == 1 and b == HG_BLOCKS[1]),
                               skip_group_check=True)
                    return m

                others = tuple(b for b in range(KB) if b not in HG_BLOCKS)
                if l == 0:
                    ada_turn(4, 6)
                    ada_section(5, 0, 7)
                else:
                    unit_full(pe, l, U_OUT)
                    project(0, 0, others)
                wait(pe, "o_sq", l, 1)
                mm(B(4), C["mean_h"], Qt[:, 0:4, :].rearrange("p n t -> p (n t)"), start=True, stop=True)\
                    .then_inc(S["o_mean"][0], 1)
                if l == 0:
                    ada_section(5, 1, 7)
                    unit_full(pe, l, U_OUT)
                    project(0, 0, others)
                project(0, 1, others)

                wait(pe, "o_ready", l, 1)
                for j in range(N_OUT):
                    unit_full(pe, l, U_OUT + j)
                    for h in range(2):
                        if j > 0:
                            project(j, h, others)
                        m = project(j, h, HG_BLOCKS)
                    used(m)
                    if j > 0:
                        wait(pe, "squares2", l, j)
                        sum_squares(4, j - 1)

                if l == 0:
                    ada_turn(5, 6)
                wait(pe, "squares2", l, N_OUT)
                sum_squares(4, N_OUT - 1)
                pe.wait_ge(mod_taken, NSP)
                for g in range(NG):
                    for b in range(KB):
                        wait(pe, "h_ready" if g == 0 else "h_ready_lat", l, KB + b + 1)
                        m = mm(ps[:, 6, g * NE:(g + 1) * NE], hT[:, b, g * T:(g + 1) * T], wr[:, b, :],
                               start=(b == 0), stop=(b == KB - 1))
                m.then_inc(S["route_done"][0], 1)
                wait(pe, "mix_added", l, N_OUT)
                for g in range(NG):
                    for b in range(KB):
                        m = tr(ps[:, 2 * g + b // 4, (b % 4) * P:(b % 4 + 1) * P], hT[:, b, g * T:(g + 1) * T])
                m.then_inc(S["h_turned"][0], 1)
                for i in range(2):
                    unit_full(pe, l, U_SH + i)
                    w = slot(l, U_SH + i).rearrange("p (b n) -> p b n", b=KB)
                    if i == 0:
                        wait(pe, "rstd_done", l, 2)
                    for h in range(2):
                        for b in range(KB):
                            m = mm(ps[:, 4 + i, h * TT:(h + 1) * TT], w[:, b, h * P:(h + 1) * P], hT[:, b, :],
                                   start=(b == 0), stop=(b == KB - 1))
                    used(m)
                    if i == 0:
                        wait(pe, "mask_ready", l, 1)
                        for g in range(NG):
                            mm(ps[:, 7, NG * NE:(NG + 1) * NE], C["ones"], sel[:, g, :], start=(g == 0), stop=(g == 1))
                        mm(ps[:, 7, (NG + 1) * NE:(NG + 2) * NE], C["ones"], sel[:, 0, :], start=True, stop=True)\
                            .then_inc(S["over_counted"][0], 1)
                        for g in range(NG):
                            o = ps[:, 7, g * NE:(g + 1) * NE]
                            m = mm(o, C["before"], sel[:, g, :], start=True, stop=(g == 0))
                            if g == 1:
                                m = mm(o, C["ones"], sel[:, 0, :], start=False, stop=True)
                        m.then_inc(S["ranks_done"][0], 1)
                def gather(buf, i, at):
                    if not (isinstance(at, int) and at == 0):
                        pe.wait_ge(S["gather_copied"][0], at)
                    for b in (2 * i, 2 * i + 1):
                        o = ps[:, 4, (b % 2) * 256:(b % 2 + 1) * 256]
                        for n, (part, g) in enumerate(((h_hi, 0), (h_lo, 0), (h_hi, 1), (h_lo, 1))):
                            m = mm(o, part[:, g, b * P:(b + 1) * P], sel01[:, buf, g, :], start=(n == 0), stop=(n == 3))
                    m.then_inc(S["gathered"][0], 1)

                def scatter():
                    for b in range(KB):
                        for part in (y_hi, y_lo):
                            m = mm(ps[:, b // 2, (b % 2) * TT:(b % 2 + 1) * TT], part[:, b * P:(b + 1) * P], slotT[:],
                                   start=False, stop=False, skip_group_check=True)
                    m.then_inc(S["scattered"][0], 1)

                FILLS = S["gathered"][1]
                wait(pe, "sel_ready", l, 1)
                wait(pe, "h_split", l, 1)
                wait(pe, "ssilu", l, 1)
                w = slot(l, U_SH + 2).rearrange("p (b n) -> p b n", b=2)
                for i in range(4):
                    gather(0, i, l * FILLS + i)
                    if i == 0:
                        wait(pe, "shid", l, 1)
                        unit_full(pe, l, U_SH + 2)
                    for b in (2 * i, 2 * i + 1):
                        for f in range(2):
                            m = mm(ps[:, b // 2, (b % 2) * TT:(b % 2 + 1) * TT], w[:, f, b * P:(b + 1) * P],
                                   hid[:, f * TT:(f + 1) * TT], start=(f == 0 and b % 2 == 0), stop=False,
                                   skip_group_check=True)
                used(m)
                wait(pe, "over_marked", l, 1)
                tr(ps[:, 7, 384:512], hT[:, 0, 0:P]).then_inc(V[l]["over_down"], 1)
                mm(ps[:, 7, 256:384], C["ones"], over_diag[:], start=True, stop=True).then_inc(S["over_counted"][0], 1)
                wait(pe, "over_listed", l, 1)
                def visit(k):
                    pe.wait_ge(V[l]["over_full"], 48 * k + 48)
                    def gate_up(g):
                        for b in range(KB):
                            w = over_w[:, 0:4].rearrange("p (m i) (c n) -> p m (i c) n", m=2, n=DE)[:, :, b, :]
                            m = mm(B(4 + g), hT[:, b, g * T:(g + 1) * T], w, start=(b == 0), stop=(b == KB - 1))
                        return m

                    with pe.If(any_context > 0):
                        gate_up(0)
                    gate_up(1).then_inc(V[l]["over_up"], 1)
                    pe.wait_ge(V[l]["over_hid"], k + 1)
                    for f in range(2):
                        for g in range(NG):
                            m = tr(ps[:, 6, f * TT + g * T:f * TT + (g + 1) * T], hid[:, g * DE + f * P:g * DE + (f + 1) * P])
                    m.then_inc(V[l]["over_turned"], 1)
                    pe.wait_ge(V[l]["over_copied"], k + 1)
                    for b in range(KB):
                        for f in range(2):
                            m = mm(ps[:, b // 2, (b % 2) * TT:(b % 2 + 1) * TT], over_w[:, 4 + f, b * P:(b + 1) * P],
                                   over_hT[:, f, :], start=False, stop=False, skip_group_check=True)
                    m.then_inc(V[l]["over_down"], 1)

                for half, (lo, hi) in enumerate(HALVES):
                    with pe.Fori(lo, hi, 1) as it:
                        for p in range(PB):
                            buf, fill = (p // 2) % 2, l * FILLS + 4 + 2 * p + it * 2 * PB
                            pe.wait_ge(S["gather_copied"][0], l * FILLS + 4 + 4 * (p // 2) + it * 2 * PB)
                            pe.wait_ge(S["slotT_ready"][0], l * (NPAIR + 1) + p + 1 + it * PB)
                            for h in range(2):
                                for e in range(2):
                                    unit_full(pe, l, U_EX + 6 * p + 2 * h + e, it * 32 * (6 * PB // RING))
                                for b in range(4):
                                    for e in range(2):
                                        w = slot(l, U_EX + 6 * p + 2 * h + e).rearrange("p (m b n) -> p m b n", m=2, b=4)
                                        at = ((2 * p + e) % GE) * SLOTS
                                        m = mm(ps[64 * e:64 * e + 64, 5, :], hslots[:, buf, 4 * h + b, at:at + SLOTS], w[:, :, b, :],
                                               start=(h == 0 and b == 0), stop=(h == 1 and b == 3))
                                        if b == 3:
                                            used(m)
                            pe.wait_ge(S["sel_ready"][0], l * (NGRP + 2) + 2 + p // 2 + it * (PB // 2))
                            gather(1 - buf, 2 * (p % 2), fill)
                            pe.wait_ge(S["y_ready"][0], l * (NPAIR + 1) + p + 1 + it * PB)
                            scatter()
                            pe.wait_ge(S["hid_ready"][0], l * NPAIR + p + 1 + it * PB)
                            for f in range(2):
                                tr(ps[:, 5, f * P:(f + 1) * P], hid[:, f * P:(f + 1) * P])
                            for g in range(NG):
                                at = (p % 2) * P
                                m = tr(ps[:, 5, 256 + g * T:256 + (g + 1) * T], selw[:, buf, g, at:at + P])
                            m.then_inc(S["turned"][0], 1)
                            gather(1 - buf, 2 * (p % 2) + 1, fill + 1)
                            pe.wait_ge(S["hidT_copied"][0], l * NPAIR + p + 1 + it * PB)
                            for e in range(2):
                                unit_full(pe, l, U_EX + 6 * p + 4 + e, it * 32 * (6 * PB // RING))
                            for f in range(2):
                                for c in range(2):
                                    for e in range(2):
                                        w = slot(l, U_EX + 6 * p + 4 + e).rearrange("p (f n) -> p f n", f=2)
                                        m = mm(ps[64 * e:64 * e + 64, 6 + c, :], hidT[:, f, 64 * e:64 * e + 64],
                                               w[:, f, c * 512:(c + 1) * 512], start=(f == 0), stop=(f == 1))
                                        if f == 1 and c == 1:
                                            used(m)
                    if half == 0:
                        done = hi * PB
                        pe.wait_ge(S["gather_copied"][0], l * FILLS + 4 + 2 * done)
                        pe.wait_ge(S["slotT_ready"][0], l * (NPAIR + 1) + done + 1)
                        pe.wait_ge(S["y_ready"][0], l * (NPAIR + 1) + done + 1)
                        any_context = pe.value_load(over_list[0:1, OVER + 1:OVER + 2], min_val=0, max_val=1)
                        over_visits(pe, l, visit)
                wait(pe, "y_ready", l, NPAIR + 1)
                scatter()
                tr(ps[:, 5, 0:P], hT[:, 0, 0:P]).then_inc(S["sums_done"][0], 1)

            for b in range(KB):
                wait(pe, "squares", DEPTH, b // 2 + 1)
                m = mm(ps[:, 4, 0:TT], C["ones"], xn[:, b, :], start=(b == 0), stop=(b == KB - 1))
            m.then_inc(fin_mean, 1)
            for b in range(KB):
                pe.wait_ge(fin_y, b + 1)
                for g in range(NG):
                    m = tr(ps[:, 2 * (b // 4) + g, (b % 4) * P:(b % 4 + 1) * P], hT[:, b, g * T:(g + 1) * T])
                    if b % 4 == 3:
                        m.then_inc(fin_turned, 1)

        @block.scalar
        def _(act):
            fn = nc.scalar.activation
            chain = Chain("act_order", ACT_LINKS)

            def rsqrt(out_ap, tmp, src, name, l, scale=1.0):
                chain.link(act, fn(tmp, src, ACT.Ln, bias=epsc[:, 0:1], scale=scale))
                fn(out_ap, tmp, ACT.Exp, scale=-0.5).then_inc(S[name][0], 1)

            act.wait_ge(consts_set, 5)
            act.wait_ge(g_stored, 1)
            fn(stmp[:, 0:16], gvec[:, R_COND:R_COND + 16], ACT.Exp, scale=-1.0).then_inc(setup_act, 1)
            act.wait_ge(setup_dve, 1)
            fn(stmp[:, 16:24], stmp[:, 24:32], ACT.Exp).then_inc(setup_act, 1)
            for j in range(4):
                act.wait_ge(x_turned, j + 1)
                fn(xT[:, 2 * j:2 * j + 2, :].rearrange("p b t -> p (b t)"), B(1 + j), ACT.Copy).then_inc(x_stored, 1)

            for l in range(DEPTH):
                chain.layer(l)

                def copy(dst, src, name=None):
                    c = fn(dst, src, ACT.Copy)
                    if name:
                        c.then_inc(S[name][0], 1)
                    return c

                wait(act, "vec_turned", l, 1)
                copy(lvec[:], ps[:, 0, 0:VROWS], "vec_stored")
                wait(act, "mean_done", l, 1)
                rsqrt(rstd[:], lnv[:], ps[:, 5, 0:TT], "rstd_done", l, scale=1.0 / D)

                def modulate(k):
                    wait(act, "xn_ready", l, k + 1)
                    for b in range(KB):
                        fn(hT[:, b, T:TT], xn[:, b, T:TT], ACT.Identity, scale=gain[:, k, b, 1:2], bias=mod[:, 3 * k, b, 1:2])\
                            .then_inc(S["h_ready_lat"][0], 1)

                def ada_copy(k, bank):
                    unit_done(act, 0, (U_ADA1 if k == 0 else U_ADA2 + (k - 1) * PAIR) + PAIR - 1)
                    fn(modrows[k], B(bank), ACT.Copy).then_inc(rows_copied, 1)

                def ada_take(k, bank):
                    act.wait_ge(rows_turned, k + 1)
                    rows = B(bank).rearrange("p (i c r) -> p i c r", i=4, c=SECT)
                    fn(modT[:, k].rearrange("p q h c g -> p (q h) c g"), rows[:, :, :, 0:NG], ACT.Copy).then_inc(mod_taken, 1)

                if l == 0:
                    ada_copy(0, 6)
                    ada_take(0, 7)
                modulate(0)
                wait(act, "cache_turned", l, 1)
                copy(kcT[:], ps[:, 1, 0:P])
                copy(ckvT[:, 2, :], ps[:, 1, P:2 * P])
                copy(krT[NOPE:, 2, :], ps[NOPE:NOPE + ROPE, 1, 2 * P:3 * P], "cache_copied")
                for i in range(11):
                    unit_done(act, l, U_IN + min(i, N_IN - 1))
                    if i == 0:
                        if l > 0:
                            act.wait_ge(out_sem, l * 16 * STORES)
                    bank = (i + 1) % 8
                    if i == 1:
                        copy(U[:, i, 0:TT], ps[:, bank, 0:TT])
                        copy(krT[NOPE:, 0:2, :].rearrange("p n t -> p (n t)"), ps[NOPE:NOPE + ROPE, bank, TT:2 * TT], "u_copied")
                    elif i == 9:
                        copy(U[:, i, 0:TT], ps[:, bank, 0:TT], "u_copied")
                    else:
                        copy(U[:, i, :], ps[:, bank, :], "u_copied")
                    if i == 6:
                        wait(act, "u_copied", l, 7)
                        flat = lambda x: x.rearrange("p n t -> p (n t)")
                        parts = ((flat(lf), flat(U[:, U_ZF:U_ZB + 1, :])), (flat(Gc[:, 0:4, :]), U[:, U_HQ, :]),
                                 (flat(Gc[:, 4:8, :]), U[:, U_HG, :]))
                        for dst, src in parts:
                            e = fn(dst, src, ACT.Exp, scale=-1.0)
                        chain.link(act, e)
                        for dst, _ in parts:
                            e = fn(dst, dst, ACT.Ln, bias=1.0)
                        chain.link(act, e)
                        for dst, _ in parts:
                            e = fn(dst, dst, ACT.Exp, scale=-1.0)
                        e.then_inc(S["hg_exp"][0], 1)
                wait(act, "hg_f", l, 1)
                fn(lf[:, 0:4, :], Qt[:, 0:4, :], ACT.Ln)
                fn(lf[:, 4:8, ::-1], Qt[:, 4:8, :], ACT.Ln).then_inc(S["hg_ln"][0], 1)
                wait(act, "lat_mean", l, 1)
                wait(act, "lat_sq", l, 1)
                rsqrt(rsq[:], prP[:].rearrange("p n t -> p (n t)"), B(3), "lat_rstd", l)
                wait(act, "flip_done", l, 1)
                copy(Vh[:, 1, :, :].rearrange("p g n -> p (g n)"), B(4))
                copy(Vh[:, 0, :, :].rearrange("p g n -> p (g n)"), U[:, U_I, :], "flip_copied")
                wait(act, "fn1_done", l, 1)
                for g in range(NG):
                    c = copy(F1[:, :, :, g, :], ps[:, 6 + g, :].rearrange("p (c h t) -> p c h t", c=2, h=2))
                c.then_inc(S["fn1_copied"][0], 1)
                if l == 0:
                    ada_copy(1, 2)
                wait(act, "mq_done", l, 1)
                copy(qT[:].rearrange("p h t -> p (h t)"), ps[0:NOPE + ROPE, 0:2, :].rearrange("p b t -> p (b t)"), "mq_copied")
                if l == 0:
                    ada_take(1, 2)
                wait(act, "mv_done", l, 1)
                wait(act, "krot_done", l, 1)
                copy(vM[:].rearrange("p n t -> p (n t)"), ps[:, 2:4, :].rearrange("p b t -> p (b t)")[:, 0:768], "mv_copied")
                wait(act, "fn2_done", l, 1)
                copy(F2.rearrange("p b t -> p (b t)"), B(6), "fn2_copied")
                wait(act, "mk_done", l, 1)
                for h, bank in enumerate((4, 5, 0, 1)):
                    c = copy(kT[0:NOPE, h].rearrange("p n t -> p (n t)"), ps[0:NOPE, bank, 0:3 * T])
                c.then_inc(S["mk_copied"][0], 1)
                wait(act, "fn3_done", l, 1)
                copy(OT[:, 4:6, :].rearrange("p b t -> p (b t)"), B(7), "fn3_copied")
                wait(act, "kv_turned", l, 1)
                copy(o_ckv[:], ps[:, 0, 0:P])
                copy(o_kr[:], ps[:, 0, P + NOPE:P + NOPE + ROPE], "kvout_copied")

                def softmax_exp(n, scale):
                    wait(act, "negmax", l, n + 1)
                    for h in range(4):
                        r, c = h // 2, h % 2
                        fn(prS[:, h, :], ps[:, 2 + r, c * TT:(c + 1) * TT], ACT.Exp, bias=negm[:, h:h + 1], scale=scale,
                           accum_out=den[:, h:h + 1])
                        e = fn(prP[:, h, :], ps[:, 4 + r, c * T:(c + 1) * T], ACT.Exp, bias=negm[:, 4 + h:5 + h], scale=scale,
                               accum_out=den[:, 4 + h:5 + h])
                        if h == 3 and n == 1:
                            e.then_inc(S["exps"][0], 1)
                    if n == 0:
                        fn(esk[:], mx[:], ACT.Exp).then_inc(S["exps"][0], 1)

                def softmax_out(n, blk):
                    wait(act, "p_turned", l, n + 1)
                    for i, bank in enumerate(((6, 7, 0), (2, 3, 4))[n]):
                        c = copy(pT[:, 4 * i:4 * i + 4, :].rearrange("p n t -> p (n t)"), B(bank))
                    c.then_inc(S["p_copied"][0], 1)
                    wait(act, "pv_done", l, n + 1)
                    copy(OT[:, blk:blk + 2, :].rearrange("p b t -> p (b t)"), B(1), "pv_copied")

                softmax_exp(0, SWA_SCALE)
                wait(act, "diffs", l, 1)
                fn(Qt[:], Qt[:], ACT.Exp)
                for j in range(NCK):
                    kj = Kt[:, j, :, 0:(j + 1) * CK]
                    fn(kj, kj, ACT.Exp)
                fn(KD[:], KD[:], ACT.Exp)
                fn(QD[:], QD[:], ACT.Exp).then_inc(S["decays"][0], 1)
                if l == 0:
                    ada_copy(2, 6)
                softmax_out(0, 6)
                if l == 0:
                    ada_take(2, 0)
                softmax_exp(1, MLA_SCALE)
                if l == 0:
                    ada_copy(3, 0)
                softmax_out(1, 0)
                if l == 0:
                    ada_take(3, 0)
                wait(act, "kd_turned", l, 1)
                copy(KDt[:].rearrange("p n t -> p (n t)"), B(2), "kd_copied")
                wait(act, "st_done", l, 1)
                copy(o_st[:], ps[:, 3, 0:256], "st_copied")
                if l == 0:
                    ada_copy(4, 1)
                wait(act, "of_done", l, 1)
                ofw = prS[:, 0:2, :].rearrange("p n t -> p (n t)")
                for r in range(2):
                    c = copy(ofw[64 * r:64 * r + 64], ps[64 * r:64 * r + 64, r, :])
                c.then_inc(S["of_copied"][0], 1)
                if l == 0:
                    ada_take(4, 6)
                wait(act, "o_mean", l, 1)
                rsqrt(rsq[:], prP[:].rearrange("p n t -> p (n t)"), B(4), "o_rstd", l)
                if l == 0:
                    ada_copy(5, 7)
                    ada_take(5, 6)
                wait(act, "mean_done", l, 2)
                rsqrt(rstd[:], lnv[:], ps[:, 4, 0:TT], "rstd_done", l, scale=1.0 / D)
                modulate(1)
                wait(act, "route_done", l, 1)
                fn(sg[:].rearrange("p g e -> p (g e)"), ps[:, 6, 0:NG * NE], ACT.Exp, scale=-1.0).then_inc(S["route_exp"][0], 1)
                wait(act, "h_turned", l, 1)
                act.wait_ge(out_sem, (l + 1) * 16 * STORES)
                copy(h_hi[:].rearrange("p g n -> p (g n)"), ps[:, 0:4, :].rearrange("p b n -> p (b n)"), "hhi_done")
                unit_done(act, l, U_SH)
                fn(silu_g[:], B(4), ACT.Silu).then_inc(S["ssilu"][0], 1)
                def visit(k):
                    act.wait_ge(V[l]["over_up"], k + 1)
                    fn(silu_g[:].rearrange("p (g n) -> p g n", g=NG), ps[:, 4:6, 0:DE], ACT.Silu)\
                        .then_inc(V[l]["over_silu"], 1)
                    act.wait_ge(V[l]["over_turned"], k + 1)
                    fn(over_hT[:].rearrange("p f t -> p (f t)"), B(6), ACT.Copy).then_inc(V[l]["over_copied"], 1)

                for half, (lo, hi) in enumerate(HALVES):
                    with act.Fori(lo, hi, 1) as it:
                        for p in range(PB):
                            unit_done(act, l, U_EX + 6 * p + 3, it * 6 * PB)
                            fn(silu_g[:, 0:256], ps[:, 5, 0:256], ACT.Silu).then_inc(S["silu_done"][0], 1)
                            act.wait_ge(S["turned"][0], l * NPAIR + p + 1 + it * PB)
                            fn(hidT[:].rearrange("p f t -> p (f t)"), ps[:, 5, 0:256], ACT.Copy).then_inc(S["hidT_copied"][0], 1)
                            act.wait_ge(S["gathered"][0], l * S["gathered"][1] + 4 + 2 * p + 2 + it * 2 * PB)
                            i = 2 * (p % 2) + 1
                            fn(hslots[:, 1 - (p // 2) % 2, 2 * i:2 * i + 2, :].rearrange("p b n -> p (b n)"), B(4), ACT.Copy)\
                                .then_inc(S["gather_copied"][0], 1)
                            unit_done(act, l, U_EX + 6 * p + 5, it * 6 * PB)
                            act.wait_ge(S["slotT_ready"][0], l * (NPAIR + 1) + p + 2 + it * PB)
                            fn(y_hi[:], ps[:, 6:8, :].rearrange("p b n -> p (b n)"), ACT.Copy, scale=gslot[:, 0:1])\
                                .then_inc(S["yhi_done"][0], 1)
                    if half == 0:
                        wait(act, "over_listed", l, 1)
                        over_visits(act, l, visit)

            act.wait_ge(fin_mean, 1)
            chain2 = sem("fin_act")
            fn(lnv[:], ps[:, 4, 0:TT], ACT.Ln, bias=epsc[:, 0:1], scale=1.0 / D).then_inc(chain2, 1)
            act.wait_ge(chain2, 1)
            fn(rstd[:], lnv[:], ACT.Exp, scale=-0.5).then_inc(fin_rstd, 1)
            for i in range(4):
                half, g = i // 2, i % 2
                act.wait_ge(fin_turned, i + 1)
                fn(xrow[:, g * D + half * 512:g * D + (half + 1) * 512], B(i), ACT.Copy).then_inc(fin_copied, 1)

        @block.vector
        def _(dve):
            v = nc.vector
            chain = Chain("dve_order", DVE_LINKS)
            sc_ = sem("dve_setup")
            cnt_ = [0]

            def link0(ins):
                cnt_[0] += 1
                ins.then_inc(sc_, 1)
                dve.wait_ge(sc_, cnt_[0])

            dve.wait_ge(consts_set, 5)
            dve.wait_ge(g_turned, 1)
            v.tensor_copy(gvec[:], ps[:, 0, 0:GROWS]).then_inc(g_stored, 1)
            dve.wait_ge(g_stored, 1)
            lg = gvec[:, R_LB:R_LB + 8].rearrange("p (r l q) -> p l r q", r=2, l=DEPTH)
            m_ = stmp[:, 32:36].rearrange("p (r q) -> p r q", r=2)
            d_ = stmp[:, 24:32].rearrange("p (l r q) -> p l r q", l=DEPTH, r=2)
            e_ = stmp[:, 16:24].rearrange("p (l r q) -> p l r q", l=DEPTH, r=2)
            link0(v.tensor_tensor(m_, lg[:, 0], lg[:, 1], ALU.max))
            link0(v.tensor_tensor(d_[:, 0], lg[:, 0], m_, ALU.subtract))
            v.tensor_tensor(d_[:, 1], lg[:, 1], m_, ALU.subtract).then_inc(setup_dve, 1)
            dve.wait_ge(setup_act, 1)
            link0(v.tensor_scalar(stmp[:, 40:56], stmp[:, 0:16], 1.0, None, ALU.add))
            link0(v.reciprocal(stmp[:, 40:56], stmp[:, 40:56]))
            link0(v.tensor_tensor(scond[:, :, 0:2].rearrange("p b g -> p g b"), gvec[:, 0:16].rearrange("p (g b) -> p g b", g=2),
                                  stmp[:, 40:56].rearrange("p (g b) -> p g b", g=2), ALU.mult))
            dve.wait_ge(setup_act, 2)
            link0(v.tensor_tensor(m_, e_[:, 0], e_[:, 1], ALU.add))
            link0(v.reciprocal(stmp[:, 36:40], stmp[:, 32:36]))
            r_ = stmp[:, 36:40].rearrange("p (r q) -> p r q", r=2)
            for i in range(DEPTH):
                link0(v.tensor_tensor(e_[:, i], e_[:, i], r_, ALU.mult))
            link0(v.tensor_tensor(d_[:, 1], e_[:, 0], e_[:, 1], ALU.add))
            link0(v.tensor_tensor(lb[:, 0], e_[:, 0], e_[:, 0], ALU.subtract))
            link0(v.tensor_tensor(lb[:, 1], d_[:, 1], e_[:, 0], ALU.subtract))
            link0(v.tensor_scalar(oml[:], lb[:], -1.0, 1.0, ALU.mult, ALU.add))
            dve.wait_ge(x_stored, 4)
            v.memset(stmp[:, 56:57], 0.0).then_inc(cond_ready, 1)

            def square(j):
                nb = slice(2 * j, 2 * j + 2)
                v.tensor_tensor(xn[:, nb], xT[:, nb], xT[:, nb], ALU.mult).then_inc(S["squares"][0], 1)

            for j in range(KB // 2):
                square(j)

            for l in range(DEPTH):
                chain.layer(l)
                link = lambda ins: chain.link(dve, ins)
                sig = lambda ins, name: ins.then_inc(S[name][0], 1)

                def add_sections(k):
                    dve.wait_ge(mod_taken, 3 * l + k + 1)
                    for q in range(2):
                        r = R_BADA + (l * 6 + 2 * k + q) * KB
                        bias = gvec[:, r:r + KB].rearrange("p (c h) -> p h c", h=2)
                        ins = v.tensor_tensor(mod[:, 2 * k + q].rearrange("p (c h) g -> p h c g", h=2), modT[:, 3 * l + k, q],
                                              bias.unsqueeze(3).broadcast_to([P, 2, 4, 2]), ALU.add)
                    link(ins)

                def norm_mod(k):
                    if k == 0:
                        wait(dve, "vec_stored", l, 1)
                        add_sections(0)
                        link(v.scalar_tensor_tensor(gain[:, 0], mod[:, 1], 1.0,
                                                    lvec[:, R_N1:R_N1 + 8].unsqueeze(2).broadcast_to([P, KB, NG]),
                                                    ALU.add, ALU.mult))
                    wait(dve, "rstd_done", l, k + 1)
                    sig(v.tensor_tensor(xn, xT[:], rstd[:].unsqueeze(1).broadcast_to([P, KB, TT]), ALU.mult), "xn_ready")
                    wait(dve, "xn_ready", l, k + 1)
                    for b in range(KB):
                        sig(v.tensor_scalar(hT[:, b, 0:T], xn[:, b, 0:T], gain[:, k, b, 0:1], mod[:, 3 * k, b, 0:1],
                                            ALU.mult, ALU.add), "h_ready")

                norm_mod(0)

                wait(dve, "u_copied", l, 2)
                v.tensor_tensor(cqn, u2(U_Q), u2(U_Q), ALU.mult)
                sig(v.tensor_tensor(rsq[:, 0:TT], U[:, U_KV, 0:TT], U[:, U_KV, 0:TT], ALU.mult), "lat_sq")
                wait(dve, "hg_exp", l, 1)
                flat = lambda x: x.rearrange("p n t -> p (n t)")
                for d in range(2):
                    for q in range(HP):
                        n = 2 * (d * HP + q)
                        link(v.tensor_scalar(Qt[:, n:n + 2, :], lf[:, n:n + 2, :], oml[:, l, d, q:q + 1], lb[:, l, d, q:q + 1],
                                             ALU.mult, ALU.add))
                v.tensor_scalar(kk[:, 0:4, :], Qt[:, 0:4, :], -1.0, 1.0, ALU.mult, ALU.add)
                sig(v.tensor_scalar(kk[:, 4:8, ::-1], Qt[:, 4:8, :], -1.0, 1.0, ALU.mult, ALU.add), "hg_f")
                q4 = U[:, U_HQ, :].rearrange("p (n t) -> p n t", t=T)
                v.tensor_tensor(qs[:, 0:4, :], q4, Gc[:, 0:4, :], ALU.mult)
                v.tensor_tensor(qs[:, 4:8, ::-1], q4, Gc[:, 0:4, :], ALU.mult)
                link(v.tensor_tensor(gs[:], U[:, U_HG, :], flat(Gc[:, 4:8, :]), ALU.mult))
                wait(dve, "hg_ln", l, 1)
                for n in range(8):
                    ins = v.tensor_tensor_scan(Gc[:, n, :], C["ones"], lf[:, n, :], 0.0, ALU.mult, ALU.add)
                link(ins)
                wait(dve, "lat_rstd", l, 1)
                rq = rsq[:, 0:TT]
                link(v.tensor_tensor(cqn, u2(U_Q), rq.unsqueeze(1).broadcast_to([P, 2, TT]), ALU.mult))
                for b in range(2):
                    ins = v.tensor_scalar(cqn[:, b, :], cqn[:, b, :], lvec[:, R_QN + b:R_QN + b + 1], None, ALU.mult)
                sig(ins, "cqn_ready")
                sig(v.scalar_tensor_tensor(ckvT[:, 0:2, :].rearrange("p n t -> p (n t)"), U[:, U_KV, 0:TT],
                                           lvec[:, R_KVN:R_KVN + 1], rsq[:, TT:2 * TT], ALU.mult, ALU.mult), "kvn_ready")
                wait(dve, "srot_done", l, 1)
                raw = U[:, U_SQ:U_SK + 1, :].rearrange("p i t -> p (i t)").rearrange("p (b t) -> p b t", t=TT)[:, 0:3, T:TT]
                rot = prP[:, 0:3, :]
                bc3 = lambda x: x.unsqueeze(1).broadcast_to([x.shape[0], 3, T])
                v.tensor_tensor(rot, ps[:, 5, 0:3 * T].rearrange("p (b t) -> p b t", b=3), bc3(C["sin_s"]), ALU.mult)
                link(v.tensor_tensor(raw, raw, bc3(C["cos_s"]), ALU.mult))
                sig(v.tensor_tensor(raw, raw, rot, ALU.add), "srot_used")
                wait(dve, "u_copied", l, 11)
                Gb = Gc[:].rearrange("p n (j t) -> p n j t", t=CK)
                mid = CK // 2 - 1
                Qf = Qt[:].rearrange("p n (j t) -> p (n j) t", t=CK)
                ref = Gc[:].rearrange("p n (j t) -> p (n j) t", t=CK)[:, :, mid:mid + 1]
                v.tensor_tensor(Qf, Gc[:].rearrange("p n (j t) -> p (n j) t", t=CK), ref.broadcast_to([P, 8 * NCK, CK]), ALU.subtract)
                for j in range(NCK):
                    w = (j + 1) * CK
                    v.tensor_tensor(Kt[:, j, :, 0:w], Gb[:, :, j, mid:mid + 1].broadcast_to([P, 8, w]), Gc[:, :, 0:w], ALU.subtract)
                gP = Gc[:].rearrange("p (n g) t -> p n g t", g=NG)
                v.tensor_tensor(KD[:], gP[:, :, 0, T - 1:T].broadcast_to([P, 4, T]), gP[:, :, 0, :], ALU.subtract)
                sig(v.tensor_copy(QD[:], gP[:, :, 1, :]), "diffs")
                wait(dve, "kr_zeroed", l, 1)
                NR = NOPE + ROPE
                wait(dve, "krot_done", l, 1)
                wait(dve, "mv_copied", l, 1)
                link(v.tensor_tensor(prS[0:NR, 0, 0:T], ps[0:NR, 3, 256:384], C["sin_m"][0:NR], ALU.mult))
                link(v.tensor_tensor(krT[:, 1, :], krT[:, 1, :], C["cos_m"][0:NR], ALU.mult))
                sig(v.tensor_tensor(krT[:, 1, :], krT[:, 1, :], prS[0:NR, 0, 0:T], ALU.add), "krot_used")
                wait(dve, "krot_used", l, 1)
                sig(v.tensor_copy(kT[NOPE:].rearrange("p h n t -> p h (n t)"),
                                  krT[NOPE:].rearrange("p n t -> p (n t)").unsqueeze(1).broadcast_to([ROPE, MH, 3 * T])), "kr_ready")
                wait(dve, "qrot_done", l, 1)
                qv = qT[:, :, T:TT]
                bc4 = lambda x: x.unsqueeze(1).broadcast_to([NR, MH, T])
                rt = prS[0:NR, :, 0:T]
                v.tensor_tensor(rt, ps[0:NR, 6, :].rearrange("p (h t) -> p h t", h=MH), bc4(C["sin_m"][0:NR]), ALU.mult)
                link(v.tensor_tensor(qv, qv, bc4(C["cos_m"][0:NR]), ALU.mult))
                sig(v.tensor_tensor(qv, qv, rt, ALU.add), "qrot_used")

                def softmax_max(n, scale):
                    wait(dve, "scores", l, n + 1)
                    if n == 1:
                        wait(dve, "exps", l, 1)
                    v.tensor_reduce(mx[:, 0:4], ps[:, 2:4, :].rearrange("p b (c t) -> p (b c) t", c=2), AX_X, ALU.max)
                    link(v.tensor_reduce(mx[:, 4:8].rearrange("p (b c) -> p b c", b=2),
                                         ps[:, 4:6, 0:TT].rearrange("p b (c t) -> p b c t", c=2), AX_X, ALU.max))
                    if n == 0:
                        link(v.tensor_scalar(mx[:], mx[:], scale, None, ALU.mult))
                        m2 = mx[:].rearrange("p (g h) -> p g h", g=2)
                        sk = sink[:].unsqueeze(1).broadcast_to([P, 2, SH])
                        link(v.tensor_tensor(m2, m2, sk, ALU.max))
                        link(v.tensor_scalar(negm[:], mx[:], -1.0, None, ALU.mult))
                        sig(v.tensor_tensor(m2, sk, m2, ALU.subtract), "negmax")
                    else:
                        sig(v.tensor_scalar(negm[:], mx[:], -scale, None, ALU.mult), "negmax")

                def softmax_div(n):
                    wait(dve, "exps", l, n + 1)
                    if n == 0:
                        link(v.tensor_tensor(den[:], den[:], esk[:], ALU.add))
                    link(v.reciprocal(den[:], den[:]))
                    v.tensor_tensor(prS[:], prS[:], den[:, 0:4].unsqueeze(2).broadcast_to([P, 4, 2 * T]), ALU.mult)
                    sig(v.tensor_tensor(prP[:], prP[:], den[:, 4:8].unsqueeze(2).broadcast_to([P, 4, T]), ALU.mult), "probs")

                softmax_max(0, SWA_SCALE)
                softmax_div(0)
                wait(dve, "decays", l, 1)
                for j in range(NCK):
                    w = (j + 1) * CK
                    v.tensor_tensor(Kt[:, j, :, 0:w], Kt[:, j, :, 0:w], kk[:, :, 0:w], ALU.mult)
                v.tensor_tensor(Qt[:], Qt[:], qs[:], ALU.mult)
                kP = kk[:].rearrange("p (n g) t -> p n g t", g=NG)
                qP = qs[:].rearrange("p (n g) t -> p n g t", g=NG)
                v.tensor_tensor(KD[:], KD[:], kP[:, :, 0, :], ALU.mult)
                sig(v.tensor_tensor(QD[:], QD[:], qP[:, :, 1, :], ALU.mult), "recur_ready")
                softmax_max(1, MLA_SCALE)
                softmax_div(1)
                wait(dve, "attn_zeroed", l, 1)
                msk = C["causal"].bitcast(I32).unsqueeze(1).broadcast_to([P, 4, T])
                for r in range(2):
                    wait(dve, "at_done", l, r + 1)
                    for i in range(2):
                        ins = v.copy_predicated(AT[:, 8 * r + 4 * i:8 * r + 4 * i + 4, :], msk,
                                                B(6 - 2 * r + i).rearrange("p (n t) -> p n t", n=4))
                sig(ins, "at_masked")
                wait(dve, "of_done", l, 2)
                wait(dve, "of_copied", l, 1)
                for r in range(2):
                    h = slice(64 * r, 64 * r + 64)
                    link(v.tensor_tensor(KD[h], ps[h, 2 + r, :].rearrange("p (n t) -> p n t", t=T)[:, :, ::-1],
                                         prS[h, 0:2, :].rearrange("p b (c t) -> p (b c) t", c=2), ALU.add))
                sig(v.tensor_tensor(Qt[:, 0:4, :], KD[:], KD[:], ALU.mult), "o_sq")
                link(v.tensor_tensor(gs[:], gs[:], flat(KD[:]), ALU.mult))
                wait(dve, "o_rstd", l, 1)
                sig(v.scalar_tensor_tensor(OT[:, 2:4, :].rearrange("p b t -> p (b t)"), gs[:], lvec[:, R_HGN:R_HGN + 1], rsq[:],
                                           ALU.mult, ALU.mult), "o_ready")

                for k in (1, 2):
                    add_sections(k)
                v.scalar_tensor_tensor(gain[:, 1], mod[:, 4], 1.0, lvec[:, R_N2:R_N2 + 8].unsqueeze(2).broadcast_to([P, KB, NG]),
                                       ALU.add, ALU.mult)
                for j in range(N_OUT):
                    unit_done(dve, l, U_OUT + j)
                    for h in range(2):
                        b = 2 * j + h
                        for g in range(NG):
                            t = slice(g * T, (g + 1) * T)
                            ins = v.scalar_tensor_tensor(xT[:, b, t], ps[:, OUT_BANK[j], h * TT + g * T:h * TT + (g + 1) * T],
                                                         mod[:, 2, b, g:g + 1], xT[:, b, t], ALU.mult, ALU.add)
                    sig(ins, "mix_added")
                    wait(dve, "mix_added", l, j + 1)
                    nb = slice(2 * j, 2 * j + 2)
                    sig(v.tensor_tensor(xn[:, nb], xT[:, nb], xT[:, nb], ALU.mult), "squares2")
                norm_mod(1)

                wait(dve, "route_exp", l, 1)
                link(v.tensor_scalar(sg[:], sg[:], 1.0, None, ALU.add))
                link(v.reciprocal(sg[:], sg[:]))
                link(v.tensor_tensor(sbs[:], sg[:], brt[:].unsqueeze(1).broadcast_to([P, NG, NE]), ALU.add))
                for g in range(NG):
                    link(v.max(top8[:, g, :], sbs[:, g, :]))
                for g in range(NG):
                    th = top8[:, g, TOPK - 1:TOPK]
                    link(v.tensor_scalar(sel[:, g, :], sbs[:, g, :], th, None, ALU.is_gt))
                    link(v.tensor_reduce(cnt[:, g, 0:1], sel[:, g, :], AX_X, ALU.add))
                    link(v.tensor_scalar(cnt[:, g, 1:2], cnt[:, g, 0:1], -1.0, float(TOPK), ALU.mult, ALU.add))
                    link(v.tensor_scalar(eqm[:, g, :], sbs[:, g, :], th, None, ALU.is_equal))
                    link(v.tensor_tensor_scan(cum[:, g, :], C["ones"][:, 0:NE], eqm[:, g, :], 0.0, ALU.mult, ALU.add))
                    link(v.scalar_tensor_tensor(eqm[:, g, :], cum[:, g, :], cnt[:, g, 1:2], eqm[:, g, :], ALU.is_le, ALU.mult))
                sig(v.tensor_tensor(sel[:], sel[:], eqm[:], ALU.add), "mask_ready")
                wait(dve, "mask_ready", l, 1)
                link(v.tensor_tensor(sg[:], sel[:], sg[:], ALU.mult))
                link(v.tensor_reduce(cnt[:, :, 0], sg[:], AX_X, ALU.add))
                link(v.reciprocal(cnt[:, :, 1], cnt[:, :, 0]))
                for g in range(NG):
                    v.tensor_scalar(gatew[:, g, 0:NE], sg[:, g, :], ROUTE_SCALE, cnt[:, g, 1:2], ALU.mult, ALU.mult)
                wait(dve, "ranks_done", l, 1)
                link(v.scalar_tensor_tensor(rank[:, :, 0:NE], ps[:, 7, 0:NG * NE].rearrange("p (g e) -> p g e", g=NG), 1.0, sel[:],
                                            ALU.add, ALU.mult))
                sig(v.tensor_scalar(rank[:, :, 0:NE], rank[:, :, 0:NE], -1.0, None, ALU.add), "gates_ready")
                wait(dve, "gates_ready", l, 1)
                wait(dve, "hhi_done", l, 1)
                sig(v.tensor_tensor(h_lo[:].rearrange("p g n -> p (g n)"), ps[:, 0:4, :].rearrange("p b n -> p (b n)"),
                                    h_hi[:].bitcast(F32).rearrange("p g n -> p (g n)"), ALU.subtract), "h_split")
                def places(buf, e0, n):
                    cols = lambda x: x.rearrange("p g (e s) -> p g e s", e=GE)
                    bc = lambda x: x.unsqueeze(3).broadcast_to([P, NG, GE, SLOTS])
                    w = v.tensor_tensor(cols(sel01[:, buf]), bc(rank[:, :, e0]),
                                        C["slots"].unsqueeze(1).unsqueeze(1).broadcast_to([P, NG, GE, SLOTS]), ALU.is_equal)
                    w.then_inc(sel_built, 1)
                    dve.wait_ge(sel_built, n)
                    v.tensor_tensor(cols(selw[:, buf]), cols(sel01[:, buf].bitcast(F32)), bc(gatew[:, :, e0]), ALU.mult)\
                        .then_inc(S["sel_ready"][0], 1)

                for q in range(2):
                    places(q, slice(q * GE, (q + 1) * GE), l * (NGRP + 2) + q + 1)
                    if q == 0:
                        wait(dve, "ssilu", l, 1)
                        unit_done(dve, l, U_SH + 1)
                        sig(v.tensor_tensor(hid[:], B(5), silu_g[:], ALU.mult), "shid")
                v.scalar_tensor_tensor(over_gate[:], rank[:, :, 0:NE], float(SLOTS), gatew[:, :, 0:NE], ALU.is_ge, ALU.mult)
                wait(dve, "over_counted", l, 1)
                v.tensor_reduce(over_any[:], ps[:, 7, (NG + 1) * NE:(NG + 2) * NE], AX_X, ALU.max)
                link(v.tensor_scalar(over_s[:, 0], ps[:, 7, NG * NE:(NG + 1) * NE], float(SLOTS), None, ALU.is_gt))
                link(v.tensor_tensor_scan(over_s[:, 1], C["ones"][:, 0:NE], over_s[:, 0], 0.0, ALU.mult, ALU.add))
                link(v.scalar_tensor_tensor(over_s[:, 2], over_s[:, 1], C["place"], over_s[:, 0], ALU.is_equal, ALU.mult))
                link(v.tensor_tensor(over_s[:, 2], over_s[:, 2], C["slots"][:, 0:NE], ALU.mult))
                link(v.tensor_reduce(over_at[:], over_s[:, 2], AX_X, ALU.add))
                sig(v.tensor_scalar(over_diag[:], ident, over_at[:, 0:1], None, ALU.mult), "over_marked")
                FILLS = S["gathered"][1]

                def copy_fill(buf, i, at):
                    dve.wait_ge(S["gathered"][0], at)
                    v.tensor_copy(hslots[:, buf, 2 * i:2 * i + 2, :].rearrange("p b n -> p (b n)"), B(4))\
                        .then_inc(S["gather_copied"][0], 1)

                for i in range(4):
                    copy_fill(0, i, l * FILLS + i + 1)
                wait(dve, "over_counted", l, 2)
                v.tensor_copy(over_list[:, 0:OVER], ps[:, 7, 256:256 + OVER])
                v.tensor_scalar(over_list[:, OVER + 1:], over_any[:], float(SLOTS), None, ALU.is_gt)
                sig(v.tensor_copy(over_list[:, OVER:OVER + 1], over_s[:, 1, NE - 1:NE]), "over_listed")
                def visit(k):
                    x = dve.value_load(over_list[0:1, bass.ds(k, 1)], min_val=0, max_val=NE - 1)
                    dve.wait_ge(V[l]["over_silu"], k + 1)
                    for g in range(NG):
                        h = v.scalar_tensor_tensor(hid[:, g * DE:(g + 1) * DE], ps[:, 4 + g, DE:2 * DE],
                                                   over_gate[:, g, bass.ds(x, 1)], silu_g[:, g * DE:(g + 1) * DE],
                                                   ALU.mult, ALU.mult)
                    h.then_inc(V[l]["over_hid"], 1)

                for half, (lo, hi) in enumerate(HALVES):
                    with dve.Fori(lo, hi, 1) as it:
                        for p in range(PB):
                            buf = (p // 2) % 2
                            dve.wait_ge(S["silu_done"][0], l * NPAIR + p + 1 + it * PB)
                            v.tensor_tensor(hid[:, 0:256], ps[:, 5, 256:512], silu_g[:, 0:256], ALU.mult)\
                                .then_inc(S["hid_ready"][0], 1)
                            copy_fill(1 - buf, 2 * (p % 2), l * FILLS + 4 + 2 * p + 1 + it * 2 * PB)
                            dve.wait_ge(S["turned"][0], l * NPAIR + p + 1 + it * PB)
                            dve.wait_ge(S["gather_copied"][0], l * FILLS + 4 + 2 * p + 2 + it * 2 * PB)
                            v.tensor_scalar(slotT[:], ps[:, 5, 256:512], 0.0, None, ALU.is_gt)
                            v.tensor_reduce(gslot[:], ps[:, 5, 256:512], AX_X, ALU.max).then_inc(S["slotT_ready"][0], 1)
                            if p % 2 == 1:
                                e0 = bass.ds(it * (2 * PB) + 2 * (p - 1) + 2 * GE, GE)
                                places(buf, e0, l * (NGRP + 2) + 3 + p // 2 + it * (PB // 2))
                            dve.wait_ge(S["yhi_done"][0], l * NPAIR + p + 1 + it * PB)
                            v.scalar_tensor_tensor(y_lo[:], ps[:, 6:8, :].rearrange("p b n -> p (b n)"), gslot[:, 0:1],
                                                   y_hi[:].bitcast(F32), ALU.mult, ALU.subtract).then_inc(S["y_ready"][0], 1)
                    if half == 0:
                        over_visits(dve, l, visit)
                wait(dve, "sums_done", l, 1)
                for j in range(KB // 2):
                    for b in (2 * j, 2 * j + 1):
                        for g in range(NG):
                            t = slice(g * T, (g + 1) * T)
                            ins = v.scalar_tensor_tensor(xT[:, b, t], ps[:, j, (b % 2) * TT + g * T:(b % 2) * TT + (g + 1) * T],
                                                         mod[:, 5, b, g:g + 1], xT[:, b, t], ALU.mult, ALU.add)
                    if j < KB // 2 - 1:
                        link(ins)
                    else:
                        sig(ins, "moe_added")
                        wait(dve, "moe_added", l, 1)
                    square(j)
            assert chain.k == chain.n, ("DVE_LINKS", chain.k)

            dve.wait_ge(fin_rstd, 1)
            for b in range(KB):
                v.scalar_tensor_tensor(hT[:, b, :], xT[:, b, :], gvec[:, R_FG + b:R_FG + b + 1], rstd[:], ALU.mult, ALU.mult)\
                    .then_inc(fin_y, 1)


_INS = ["x_prompt", "x_sample", "c", "cache_mla_ckv", "cache_mla_krope", "cache_swa_k", "cache_swa_v", "state_hgrn",
        "c_ctx", "w_ada", "b_ada", "norm1_g", "norm2_g", "w_in", "mla_q_norm_g", "mla_w_q_up", "mla_kv_norm_g",
        "mla_w_kv_up", "hg_lb_logits", "hg_norm_g", "fn_w", "swa_sink", "w_out", "moe_w_router", "moe_b_router",
        "moe_w_gate", "moe_w_up", "moe_w_down", "sh_w_gate", "sh_w_up", "sh_w_down", "final_norm_g"]
_OUTS = [("y_p", (1, T, D)), ("y_s", (1, T, D)), ("ckv", (1, DEPTH, T, KVL)), ("kr", (1, DEPTH, T, ROPE)),
         ("k", (1, DEPTH, T, SKV, SD)), ("v", (1, DEPTH, T, SKV, SD)), ("st", (1, DEPTH, 2, HH, HD, HD))]


def kernel(**inputs):
    import concourse.bacc as _bacc
    from concourse.bass_utils import run_bass_kernel_spmd as _run

    nc = _bacc.Bacc("TRN2", target_bir_lowering=False, num_devices=1)
    arrays, a, out = {}, {}, {}
    for name in _INS:
        x = np.ascontiguousarray(inputs[name])
        arrays[f"in_{name}"] = x
        a[name] = nc.dram_tensor(f"in_{name}", x.shape, F32, kind="ExternalInput").ap()
    arrays["in_consts"] = constant_array()
    a["consts"] = nc.dram_tensor("in_consts", arrays["in_consts"].shape, F32, kind="ExternalInput").ap()
    for name, shape in _OUTS:
        out[name] = nc.dram_tensor(f"out_{name}", shape, F32, kind="ExternalOutput").ap()
    build(nc, a, out)
    r = _run(nc, [arrays], core_ids=[0])
    return tuple(r.results[0][f"out_{name}"] for name, _ in _OUTS)
```
